# Optimizing a Trainium2 kernel written in Bass

```python
import math
import jax, jax.numpy as jnp
from jax import lax
import numpy as np

D_MODEL = 1024
BATCH = 1
SEQ = 256
DEPTH = 1
DEC_BATCH = 8
DEC_SEQ = 1
PAST_LEN = 2048
PAGE_SIZE = 128

N_MIXERS = 2
SSD_EXPAND = 2
SSD_INNER = SSD_EXPAND * D_MODEL
SSD_HEAD_DIM = 64
SSD_HEADS = SSD_INNER // SSD_HEAD_DIM
SSD_GROUPS = 8
SSD_HPG = SSD_HEADS // SSD_GROUPS
SSD_STATE = 128
SSD_CONV = 4
SSD_CHUNK = 128
SSD_GN = SSD_GROUPS * SSD_STATE
SSD_CONV_DIM = SSD_INNER + 2 * SSD_GN
SSD_IN_DIM = SSD_INNER + SSD_CONV_DIM + SSD_HEADS
SC_WIDTH = 3
N_EXPERTS = 32
TOP_K = 4
D_EXPERT = D_MODEL
SWIGLU_LIMIT = 7.0
SWIGLU_ALPHA = 1.702
EPS = 1e-5

kernel_name = 'hybrid_ssd_shortconv_moe_adaln_step'

def rmsnorm(x, g):
    xf = x.astype(jnp.float32)
    y = xf * lax.rsqrt(jnp.mean(xf * xf, axis=-1, keepdims=True) + EPS)
    return y.astype(x.dtype) * g

def causal_dwconv(u, buf, w):
    full = jnp.concatenate([buf.astype(u.dtype), u], axis=1)
    l = u.shape[1]
    k_w = w.shape[0]
    out = full[:, 0:l] * w[0]
    for k in range(1, k_w):
        out = out + full[:, k:k + l] * w[k]
    return out, full[:, l:]

def ssd_scan(x, dt, A, Bm, Cm, h0):
    out_dtype = x.dtype
    b, l = x.shape[0], x.shape[1]
    q = min(SSD_CHUNK, l)
    nc = -(-l // q)
    pad = nc * q - l
    x = x.astype(jnp.float32)
    Bm = Bm.astype(jnp.float32)
    Cm = Cm.astype(jnp.float32)
    dt = dt.astype(jnp.float32)
    if pad:
        pw = ((0, 0), (0, pad), (0, 0), (0, 0))
        x = jnp.pad(x, pw)
        Bm = jnp.pad(Bm, pw)
        Cm = jnp.pad(Cm, pw)
        dt = jnp.pad(dt, ((0, 0), (0, pad), (0, 0)))
    xg = x.reshape(b, nc, q, SSD_GROUPS, SSD_HPG, SSD_HEAD_DIM)
    dtc = dt.reshape(b, nc, q, SSD_GROUPS, SSD_HPG)
    Bc = Bm.reshape(b, nc, q, SSD_GROUPS, SSD_STATE)
    Cc = Cm.reshape(b, nc, q, SSD_GROUPS, SSD_STATE)
    dA = dtc * A.reshape(SSD_GROUPS, SSD_HPG)
    Acs = jnp.cumsum(dA, axis=2)
    xdt = xg * dtc[..., None]
    diff = Acs[:, :, :, None] - Acs[:, :, None, :]
    mask = jnp.tril(jnp.ones((q, q), dtype=bool))[:, :, None, None]
    Lmat = jnp.exp(jnp.where(mask, diff, -jnp.inf))
    CB = jnp.einsum('bclgn,bcsgn->bclsg', Cc, Bc)
    y_diag = jnp.einsum('bclsg,bclsgr,bcsgrp->bclgrp', CB, Lmat, xdt)
    decay = jnp.exp(Acs[:, :, -1:] - Acs)
    st = jnp.einsum('bcsgn,bcsgr,bcsgrp->bcgrpn', Bc, decay, xdt)
    chunk_decay = jnp.exp(Acs[:, :, -1])

    def step(h, inp):
        dec, s = inp
        return dec[..., None, None] * h + s, h

    h_init = h0.astype(jnp.float32).reshape(b, SSD_GROUPS, SSD_HPG, SSD_HEAD_DIM, SSD_STATE)
    h_final, prev = lax.scan(step, h_init, (jnp.moveaxis(chunk_decay, 1, 0), jnp.moveaxis(st, 1, 0)))
    prev = jnp.moveaxis(prev, 0, 1)
    y_off = jnp.einsum('bclgn,bcgrpn,bclgr->bclgrp', Cc, prev, jnp.exp(Acs))
    y = (y_diag + y_off).reshape(b, nc * q, SSD_HEADS, SSD_HEAD_DIM)[:, :l]
    return y.astype(out_dtype), h_final.reshape(b, SSD_HEADS, SSD_HEAD_DIM, SSD_STATE)

def ssd_mixer(h, conv_buf, ssm_state, p):
    b, l, _ = h.shape
    zxbcdt = h @ p['ssd_w_in']
    z = zxbcdt[..., :SSD_INNER]
    xbc = zxbcdt[..., SSD_INNER:SSD_INNER + SSD_CONV_DIM]
    dt_raw = zxbcdt[..., SSD_INNER + SSD_CONV_DIM:]
    xbc_c, new_buf = causal_dwconv(xbc, conv_buf, p['ssd_conv_w'])
    xbc_c = jax.nn.silu(xbc_c + p['ssd_conv_b'])
    xs = xbc_c[..., :SSD_INNER].reshape(b, l, SSD_HEADS, SSD_HEAD_DIM)
    Bm = xbc_c[..., SSD_INNER:SSD_INNER + SSD_GN].reshape(b, l, SSD_GROUPS, SSD_STATE)
    Cm = xbc_c[..., SSD_INNER + SSD_GN:].reshape(b, l, SSD_GROUPS, SSD_STATE)
    dt = jax.nn.softplus(dt_raw.astype(jnp.float32) + p['ssd_dt_bias'].astype(jnp.float32))
    A = -jnp.exp(p['ssd_A_log'].astype(jnp.float32))
    y, new_state = ssd_scan(xs, dt, A, Bm, Cm, ssm_state)
    y = y + xs * p['ssd_D'][:, None]
    g = (y * jax.nn.silu(z.reshape(b, l, SSD_HEADS, SSD_HEAD_DIM))).reshape(b, l, SSD_GROUPS, SSD_INNER // SSD_GROUPS)
    gf = g.astype(jnp.float32)
    gn = gf * lax.rsqrt(jnp.mean(gf * gf, axis=-1, keepdims=True) + EPS)
    gn = gn.reshape(b, l, SSD_INNER).astype(h.dtype) * p['ssd_norm_w']
    return gn @ p['ssd_w_out'], new_buf, new_state.astype(ssm_state.dtype)

def short_conv_mixer(h, buf, p):
    bcx = h @ p['sc_w_in']
    bg = bcx[..., :D_MODEL]
    cg = bcx[..., D_MODEL:2 * D_MODEL]
    xh = bcx[..., 2 * D_MODEL:]
    conv, new_buf = causal_dwconv(cg * xh, buf, p['sc_conv_w'])
    return (bg * conv) @ p['sc_w_out'], new_buf

def moe(h, i, p):
    shp = h.shape
    t = h.reshape(-1, D_MODEL)
    logits = (t @ p['router_w'][i]).astype(jnp.float32) + p['router_b'][i].astype(jnp.float32)
    vals, idx = lax.top_k(logits, TOP_K)
    probs = jax.nn.softmax(vals, axis=-1)
    comb = jnp.einsum('tk,tke->te', probs, jax.nn.one_hot(idx, N_EXPERTS, dtype=jnp.float32)).astype(t.dtype)
    out = jnp.zeros_like(t)
    for e in range(N_EXPERTS):
        gu = t @ p['moe_w_gate_up'][i, e] + p['moe_b_gate_up'][i, e]
        gate = jnp.minimum(gu[:, 0::2], SWIGLU_LIMIT)
        up = jnp.clip(gu[:, 1::2], -SWIGLU_LIMIT, SWIGLU_LIMIT)
        act = (up + 1.0) * (gate * jax.nn.sigmoid(SWIGLU_ALPHA * gate))
        o = act @ p['moe_w_down'][i, e] + p['moe_b_down'][i, e]
        out = out + comb[:, e:e + 1] * o
    return out.reshape(shp)

def trunk(x, c, ssm_conv_buf, ssm_state, sconv_buf, p):
    for i in range(DEPTH):
        mod = jax.nn.silu(c) @ p['ada_w'][i] + p['ada_b'][i]
        sh1, sc1, g1, sh2, sc2, g2 = jnp.split(mod[:, None, :], 6, axis=-1)
        h = rmsnorm(x, p['norm1_w'][i]) * (1.0 + sc1) + sh1
        if i % N_MIXERS == 0:
            m, ssm_conv_buf, ssm_state = ssd_mixer(h, ssm_conv_buf, ssm_state, p)
        else:
            m, sconv_buf = short_conv_mixer(h, sconv_buf, p)
        x = x + g1 * m
        h = rmsnorm(x, p['norm2_w'][i]) * (1.0 + sc2) + sh2
        x = x + g2 * moe(h, i, p)
    return rmsnorm(x, p['final_norm_w']), ssm_state, ssm_conv_buf, sconv_buf

def setup_inputs(seed: int = 0) -> dict:
    key = jax.random.key(seed)
    ks = jax.random.split(key, 32)
    f32 = jnp.float32

    def nrm(k, shape, scale):
        return jax.random.normal(k, shape, f32) * scale

    dt0 = jnp.exp(jax.random.uniform(ks[13], (SSD_HEADS,), f32, math.log(1e-3), math.log(1e-1)))
    return {
        'x_prompt': nrm(ks[0], (BATCH, SEQ, D_MODEL), 1.0),
        'x_sample': nrm(ks[1], (DEC_BATCH, DEC_SEQ, D_MODEL), 1.0),
        'c_prompt': nrm(ks[2], (BATCH, D_MODEL), 1.0),
        'c_sample': nrm(ks[3], (DEC_BATCH, D_MODEL), 1.0),
        'state_ssm': nrm(ks[4], (DEC_BATCH, SSD_HEADS, SSD_HEAD_DIM, SSD_STATE), 0.5),
        'state_ssm_conv': nrm(ks[5], (DEC_BATCH, SSD_CONV - 1, SSD_CONV_DIM), 1.0),
        'state_sconv': nrm(ks[6], (DEC_BATCH, SC_WIDTH - 1, D_MODEL), 1.0),
        'ada_w': nrm(ks[7], (DEPTH, D_MODEL, 6 * D_MODEL), 0.5 * D_MODEL ** -0.5),
        'ada_b': nrm(ks[8], (DEPTH, 6 * D_MODEL), 0.02),
        'norm1_w': 1.0 + nrm(ks[9], (DEPTH, D_MODEL), 0.02),
        'norm2_w': 1.0 + nrm(ks[10], (DEPTH, D_MODEL), 0.02),
        'ssd_w_in': nrm(ks[11], (D_MODEL, SSD_IN_DIM), D_MODEL ** -0.5),
        'ssd_conv_w': nrm(ks[12], (SSD_CONV, SSD_CONV_DIM), SSD_CONV ** -0.5),
        'ssd_conv_b': nrm(ks[14], (SSD_CONV_DIM,), 0.02),
        'ssd_dt_bias': dt0 + jnp.log(-jnp.expm1(-dt0)),
        'ssd_A_log': jnp.log(jax.random.uniform(ks[15], (SSD_HEADS,), f32, 1.0, 16.0)),
        'ssd_D': 1.0 + nrm(ks[16], (SSD_HEADS,), 0.02),
        'ssd_norm_w': 1.0 + nrm(ks[17], (SSD_INNER,), 0.02),
        'ssd_w_out': nrm(ks[18], (SSD_INNER, D_MODEL), SSD_INNER ** -0.5),
        'sc_w_in': nrm(ks[19], (D_MODEL, 3 * D_MODEL), D_MODEL ** -0.5),
        'sc_conv_w': nrm(ks[20], (SC_WIDTH, D_MODEL), SC_WIDTH ** -0.5),
        'sc_w_out': nrm(ks[21], (D_MODEL, D_MODEL), D_MODEL ** -0.5),
        'router_w': nrm(ks[22], (DEPTH, D_MODEL, N_EXPERTS), D_MODEL ** -0.5),
        'router_b': nrm(ks[23], (DEPTH, N_EXPERTS), 0.01),
        'moe_w_gate_up': nrm(ks[24], (DEPTH, N_EXPERTS, D_MODEL, 2 * D_EXPERT), D_MODEL ** -0.5),
        'moe_b_gate_up': nrm(ks[25], (DEPTH, N_EXPERTS, 2 * D_EXPERT), 0.01),
        'moe_w_down': nrm(ks[26], (DEPTH, N_EXPERTS, D_EXPERT, D_MODEL), D_EXPERT ** -0.5),
        'moe_b_down': nrm(ks[27], (DEPTH, N_EXPERTS, D_MODEL), 0.01),
        'final_norm_w': 1.0 + nrm(ks[28], (D_MODEL,), 0.02),
    }

def reference(x_prompt, x_sample, c_prompt, c_sample, state_ssm, state_ssm_conv, state_sconv,
              ada_w, ada_b, norm1_w, norm2_w, ssd_w_in, ssd_conv_w, ssd_conv_b, ssd_dt_bias, ssd_A_log,
              ssd_D, ssd_norm_w, ssd_w_out, sc_w_in, sc_conv_w, sc_w_out, router_w, router_b,
              moe_w_gate_up, moe_b_gate_up, moe_w_down, moe_b_down, final_norm_w):
    p = dict(ada_w=ada_w, ada_b=ada_b, norm1_w=norm1_w, norm2_w=norm2_w, ssd_w_in=ssd_w_in,
             ssd_conv_w=ssd_conv_w, ssd_conv_b=ssd_conv_b, ssd_dt_bias=ssd_dt_bias, ssd_A_log=ssd_A_log,
             ssd_D=ssd_D, ssd_norm_w=ssd_norm_w, ssd_w_out=ssd_w_out, sc_w_in=sc_w_in, sc_conv_w=sc_conv_w,
             sc_w_out=sc_w_out, router_w=router_w, router_b=router_b, moe_w_gate_up=moe_w_gate_up,
             moe_b_gate_up=moe_b_gate_up, moe_w_down=moe_w_down, moe_b_down=moe_b_down,
             final_norm_w=final_norm_w)
    bp = x_prompt.shape[0]
    ssm0 = jnp.zeros((bp, SSD_HEADS, SSD_HEAD_DIM, SSD_STATE), x_prompt.dtype)
    ssm_conv0 = jnp.zeros((bp, SSD_CONV - 1, SSD_CONV_DIM), x_prompt.dtype)
    sconv0 = jnp.zeros((bp, SC_WIDTH - 1, D_MODEL), x_prompt.dtype)
    y_prompt, ssm_p, ssm_conv_p, sconv_p = trunk(x_prompt, c_prompt, ssm_conv0, ssm0, sconv0, p)
    y_sample, ssm_s, ssm_conv_s, sconv_s = trunk(x_sample, c_sample, state_ssm_conv, state_ssm, state_sconv, p)
    return (y_prompt, y_sample, ssm_p, ssm_conv_p, sconv_p, ssm_s, ssm_conv_s, sconv_s)


_drawn_inputs = setup_inputs


def setup_inputs(seed=0):
    import zlib

    import numpy as np

    out = dict(_drawn_inputs(seed))
    spreads = {}
    factors = {'norm2_w': 3.475,
     'ssd_D': 6.167,
     'ssd_norm_w': 5.015,
     'router_b': 3.309,
     'moe_b_gate_up': 8.0,
     'moe_b_down': 64.0,
     'final_norm_w': 7.339}
    for name, (base, spread) in spreads.items():
        noise = np.random.default_rng([zlib.crc32(name.encode()), seed]).standard_normal(out[name].shape)
        drawn = base * np.exp(spread * noise) if base else spread * noise
        out[name] = __import__('jax').numpy.asarray(drawn.astype(out[name].dtype))
    for name, factor in factors.items():
        out[name] = (out[name] * factor).astype(out[name].dtype)
    return out
```

```python
from contextlib import ExitStack

import concourse.bass as bass
from concourse import mybir

F32 = mybir.dt.float32
I32 = mybir.dt.int32
U32 = mybir.dt.uint32
ALU = mybir.AluOpType
ACT = mybir.ActivationFunctionType
AX = mybir.AxisListType

P = 128
D = 1024
KT = D // P
NP = 256
NS = 8
NT = NP + NS
ROWS = (128, 128, NS)
INNER = 2 * D
HEADS, HD = 32, 64
GROUPS, HPG, STATE = 8, 4, 128
CONV = 4
XC = INNER // P
GC = GROUPS
NCH = XC + 2 * GC
CDIM = NCH * P
CH = 128
NE = 32
TOPK = 4
CAP = 64
MAXPASS = -(-NT // CAP)
LIMIT = 7.0
ALPHA = 1.702
EPS = 1e-5
SEQR = 3 + NP + 4 * NS
SEQC = SEQR - 3

ADA, WIN = "ada", "win"
UNITS = [(ADA, 0), (ADA, 1), (WIN, 4096), (WIN, 5120), (ADA, 2), (WIN, 2048), (ADA, 3), (WIN, 3072),
         (ADA, 4), (ADA, 5), (WIN, 0), (WIN, 1024)]
CHUNKS = []
for _u, (_kind, _col) in enumerate(UNITS):
    if _kind == WIN:
        for _j in range(8):
            _c = _col // P + _j
            CHUNKS.append((_u, _j, "z", _c) if _c < XC else (_u, _j, "c", _c - XC))
NCONV = NCH
UNIT_A = [u for u, (k, _) in enumerate(UNITS) if k == ADA]


def build(nc, io):
    with ExitStack() as ctx:
        def sb(name, shape, dt=F32):
            return ctx.enter_context(nc.sbuf_tensor(name, shape, dt))

        def sem(name):
            return ctx.enter_context(nc.semaphore(name))

        mod_d = nc.dram_tensor("mod_d", (9, 4, D), F32, kind="Internal").ap()
        dd_d = nc.dram_tensor("dd_d", (HEADS, 2, NS), F32, kind="Internal").ap()
        acs_d = nc.dram_tensor("acs_d", (HEADS, 2, CH), F32, kind="Internal").ap()
        bc_d = nc.dram_tensor("bc_d", (P, P), F32, kind="Internal").ap()

        BIG = sb("BIG", [P, 24, D])
        XBr = sb("XBr", [P, NCH * NT])
        XT = sb("XT", [P, 3, D])
        SZr = sb("SZr", [P, XC * NT])
        U = sb("U", [P, 10496])

        def cut(base, a, n, **kw):
            v = base[:, a:a + n]
            if kw:
                (k, m), = kw.items()
                v = v.rearrange(f"p ({k} x) -> p {k} x", **{k: m})
            return v

        W = [BIG[:, 8 * i:8 * i + 8, :] for i in range(3)]
        XB = XBr[:, :].rearrange("p (c t) -> p c t", t=NT)
        SZ = SZr[:, :].rearrange("p (c t) -> p c t", t=NT)
        xn = cut(XBr, 0, 3072, t=3)
        CR = XBr[0:9, 3072:4096]
        junk = cut(XBr, 4096, 1024)
        AB = cut(SZr, 0, 1536, u=6)
        MS = cut(SZr, 1536, 1536, u=6)
        dtt = [SZr[0:HEADS, 3072 + i * NT:3072 + (i + 1) * NT] for i in range(4)]
        h1T = cut(U, 0, KT * NT, k=KT)
        RW = cut(U, 2112, 4 * SEQR, k=4)
        HT = cut(U, 3276, NCH * 24, c=NCH)
        CV = cut(U, 4044, 3 * SEQC, k=3)
        HI = U[0:24, 4908:4908 + CDIM]
        SR = U[:, 4908:4908 + 3072].rearrange("p (r c n) -> p r c n", r=3, c=8)
        BCb = [U[:, 7980:7980 + 2048].rearrange("p (j n) -> p j n", n=P),
               U[:, 2112:2112 + 2048].rearrange("p (j n) -> p j n", n=P)]
        TT = sb("TT", [P, 4, 11, 8])
        ident = sb("ident", [P, P])
        utri = sb("utri", [P, P])
        ones = sb("ones", [P, P])
        PR1 = XBr[:, 5120:5248]
        PR2 = XBr[0:56, 5248:5376]
        zeros = XBr[0:2, 7000:8024]
        bcs = U[:, 10028:10156]
        bcT = U[:, 10156:10284]
        acsT = dtt[2][:, 0:2 * CH].rearrange("p (c l) -> p c l", c=2)
        cw = sb("cw", [P, P])
        pv = sb("pv", [P, 56])
        m1 = sb("m1", [P, 2, KT, 9])
        scT = sb("scT", [P, KT, 32])
        WDT = sb("WDT", [P, KT, 32])
        DDc = WDT[:, :, :].rearrange("p k h -> p (k h)").rearrange("p (c q s) -> p c q s", c=XC, q=2)
        dd = sb("dd", [HEADS, 2, NS])
        dtok = sb("dtok", [P, 4, 32])
        acst = sb("acst", [P, 2, 32])
        dcy = sb("dcy", [P, 2, 32])
        dec1 = sb("dec1", [P, 32])
        Dbc = sb("Dbc", [P, 32])
        Dcol = sb("Dcol", [P, XC])
        st = sb("st", [P, 16])
        hsc = sb("hsc", [HEADS, 4])
        npi = sb("npi", [1, 1], I32)
        xdtS = sb("xdtS", [P, XC, NS])
        yS = sb("yS", [P, XC, NS])

        BF = BIG[:, :, :].rearrange("p a b -> p (a b)")
        bcA = [BF[:, o:o + 4096].rearrange("p (h l) -> p h l", h=HEADS) for o in (0, 8192)]
        prevT = BF[:, 4096:6144]
        LT = [BF[:, 6144 + 512 * i:6656 + 512 * i].rearrange("p (r l) -> p r l", r=4) for i in range(2)]
        Btok = BF[:, 7168:8192]
        xdt = BF[:, 12288:14336]
        xdec = BF[:, 14336:16384]
        TLs = BF[0:88, 4096:4608].rearrange("p (u f) -> p u f", u=4)
        MT = [U[:, 8192 + 512 * i:8704 + 512 * i].rearrange("p (r l) -> p r l", r=4) for i in range(2)]
        CTs = [U[:, 9216 + 512 * i:9728 + 512 * i].rearrange("p (r l) -> p r l", r=4) for i in range(2)]
        CBm = [U[:, 10240 + 128 * i:10368 + 128 * i] for i in range(2)]
        sq = [U[:, 8192 + 528 * i:8720 + 528 * i].rearrange("p (r l) -> p r l", r=2) for i in range(2)]
        rs = [U[:, 9248 + 264 * i:9512 + 264 * i] for i in range(2)]
        MB = U[:, 0:8192].rearrange("p (q u f) -> p q u f", q=2, u=4)
        wo1 = XBr[:, 0:8192].rearrange("p (k f) -> p k f", k=8)
        h2 = cut(XBr, 0, 3072, t=3)
        acc = cut(XBr, 3072, 3072, t=3)
        BR = XBr[:, 6144:8192]
        h2T = SZr[:, 0:2112].rearrange("p (k t) -> p k t", k=KT)
        BD = SZr[0:NE, 2112:3136]
        combT = SZr[0:NE, 3136:3136 + NT]
        n2b = SZr[:, 3136:4160]
        hg, gg, uu, sg, aa, osb = [SZr[:, 512 * i:512 * i + 512] for i in range(6)]
        hgT = SZr[:, 3072:3584].rearrange("p (c s) -> p c s", c=4)
        actT = SZr[:, 3584:4096].rearrange("p (c s) -> p c s", c=4)
        o = 8192

        def small(n):
            nonlocal o
            o += n
            return U[:, o - n:o]
        G = small(192).rearrange("p (t j) -> p t j", t=3)
        Gw = small(384).rearrange("p (t d j) -> p t d j", t=3, d=2)
        SwT = small(3 * P)
        bsel = SZr[:, 4096:4160]
        eye = SZr[:, 4160:4160 + NE + 1]
        posx = small(3 * (MAXPASS * NE + 1)).rearrange("p (i t) -> p i t", t=3)
        comb = small(96).rearrange("p (e t) -> p e t", t=3)
        mask = small(96).rearrange("p (t e) -> p t e", t=3)
        RWt = small(KT * NE).rearrange("p (k e) -> p k e", k=KT)
        lg = small(NE)
        rb = small(NE)
        oh = small(4 * NE).rearrange("p (k e) -> p k e", k=4)
        pw = small(4 * NE).rearrange("p (k e) -> p k e", k=4)
        m8 = small(8)
        ixf = small(8)
        ex = small(8)
        assert o <= 10496
        ix = sb("ix", [P, 8], U32)
        iota = sb("iota", [P, 64])
        thr = sb("thr", [1, 4])
        cnt = sb("cnt", [1, 8])

        PSB = [ctx.enter_context(nc.psum_tensor(f"PS{i}", [P, 512], F32)) for i in range(6)]
        PGU = ctx.enter_context(nc.psum_tensor("PGU", [P, 2, 512], F32))
        PS = [PGU[:, 0, :], PGU[:, 1, :]] + [b[:, :] for b in PSB]

        names = """ld_x ld_c ld_par ld_hist ld_wdt ld_ab ld_hs ld_D ld_rt ld_n2 ld_bd ld_br ld_fn
        consts_pool consts_dve silu_c cT_ps scT_ok par_ps par_ok hist_ps hist_ok ada_ps ms_ok xn_ok xnT_ps h1_act
        h1_dve m1_ps m1_ok dt_ps chunk_ps chunk_evac conv_done silu_done dtTok_ps dtok_ok acs_ps acs_ok
        bcs_ok bcs_ps bcT_ok dt_t dt_e dt_u dt_l dt_ok dec_ok dd_ok s_dd s_ddl s_acs s_bcd tl_ps tl_ok s_tl s_mod s_mb
        s_scaled item_done samp_ok
        xtok_ps xtok_ok btok_ok cb_ps lt_ok exp_ok mt_ok ce_ok cts_ok y_ps y_ok st_ps st_ok dcy_ok xdec_ok lastx
        hf_ps hf_ok s_hf sq_ok gn_ps gn_ok gn_rt ss_ok rt3_ok wo_ps xm_ok h2_ok h2T_ps h2T_ok lg_ps rt_m rt_e rt_p pos_ps np_ok cmb_ps cmb_ok
        ai_ps acc_ok moe_ready
        gu_used gath_ps sc_ps actT_ps hgT_ps swT_ps dn_used d_bs d_guf d_G d_g d_act d_add d_actT d_gw
        a_sig a_hg a_hgT a_swT a_o y_done s_out s_y ch_dve ch_act ch_pool""".split()
        S = {n: sem(n) for n in names}
        ld_w = [sem(f"ld_w{i}") for i in range(3)]
        ld_wo = [sem(f"ld_wo{i}") for i in range(2)]
        ld_bc = [sem(f"ld_bc{i}") for i in range(2)]
        ld_s = [sem(f"ld_s{i}") for i in range(3)]
        st_s = [sem(f"st_s{i}") for i in range(3)]
        ld_bcb = [sem(f"ld_bcb{i}") for i in range(2)]
        gu_ld = [sem(f"gu_ld{i}") for i in range(4)]
        dn_ld = [sem(f"dn_ld{i}") for i in range(2)]

        gu_w = io["moe_w_gate_up"]
        dn_w = io["moe_w_down"]
        state_rows = io["state_ssm"].rearrange("s h p n -> s (h p) n")
        state_out = io["new_ssm_sample"].rearrange("s h p n -> s (h p) n")

        def gu_src(e, j):
            return gu_w[0, e, 256 * j:256 * j + 256, :] if isinstance(e, int) else \
                gu_w[0, bass.ds(e, 1), 256 * j:256 * j + 256, :].rearrange("o r f -> (o r) f")

        def dn_src(e, j):
            return dn_w[0, e, 512 * j:512 * j + 512, :] if isinstance(e, int) else \
                dn_w[0, bass.ds(e, 1), 512 * j:512 * j + 512, :].rearrange("o r f -> (o r) f")

        def used(eng, u):
            if UNITS[u][0] == ADA:
                eng.wait_ge(S["ada_ps"], UNIT_A.index(u) + 1)
            else:
                eng.wait_ge(S["chunk_ps"], max(n for n, c in enumerate(CHUNKS) if c[0] == u) + 1)

        block = ctx.enter_context(nc.Block())

        @block.sync
        def _(sp):
            def wait(name, v):
                sp.wait_ge(S[name], v)

            for u, (kind, col) in enumerate(UNITS):
                if u >= 3:
                    used(sp, u - 3)
                if kind == ADA:
                    src = io["ada_w"][0, :, col * D:(col + 1) * D]
                else:
                    src = io["ssd_w_in"][:, col:col + D]
                sp.dma_start(W[u % 3], src.rearrange("(k p) f -> p k f", p=P)).then_inc(ld_w[u % 3], 16)
            used(sp, len(UNITS) - 1)
            sp.dma_start(W[2], io["ssd_w_out"][0:D, :].rearrange("(k p) f -> p k f", p=P)).then_inc(ld_wo[0], 16)
            wait("y_ok", 16)
            wait("hf_ok", 4)
            wait("s_hf", 16)
            sp.dma_start(wo1, io["ssd_w_out"][D:2 * D, :].rearrange("(k p) f -> p k f", p=P)).then_inc(ld_wo[1], 16)
            for j in range(4):
                sp.dma_start(BIG[:, 4 * j:4 * j + 4, :].rearrange("p (k h) f -> p k (h f)", k=2),
                             gu_src(0, j).rearrange("(k p) f -> p k f", p=P)).then_inc(gu_ld[j], 16)
            wait("wo_ps", 1)
            for j in range(2):
                sp.dma_start(BIG[:, 16 + 4 * j:20 + 4 * j, :],
                             dn_src(0, j).rearrange("(k p) f -> p k f", p=P)).then_inc(dn_ld[j], 16)
            wait("np_ok", 1)
            npass = sp.value_load(npi[0:1, 0:1], min_val=1, max_val=MAXPASS)

            def load_expert(e, it):
                for j in range(4):
                    sp.wait_ge(S["gu_used"], it * 4 + (j - 3))
                    sp.dma_start(BIG[:, 4 * j:4 * j + 4, :].rearrange("p (k h) f -> p k (h f)", k=2),
                                 gu_src(e, j).rearrange("(k p) f -> p k f", p=P)).then_inc(gu_ld[j], 16)
                for j in range(2):
                    sp.wait_ge(S["dn_used"], it * 2 + (j - 1))
                    sp.dma_start(BIG[:, 16 + 4 * j:20 + 4 * j, :],
                                 dn_src(e, j).rearrange("(k p) f -> p k f", p=P)).then_inc(dn_ld[j], 16)

            with sp.Fori(0, npass) as ps:
                with sp.Fori(1, NE) as e:
                    load_expert(e, ps * NE + e)
                with sp.If(ps + 1 < npass):
                    load_expert(0, ps * NE + NE)
            wait("y_done", 3)
            yo = io["y_prompt"][0].rearrange("(t p) f -> p t f", p=P)
            sp.dma_start(yo, XT[:, 0:2, :]).then_inc(S["s_y"], 16)
            sp.dma_start(io["y_sample"][:, 0, :], XT[0:NS, 2, :]).then_inc(S["s_y"], 16)
            wait("s_y", 32)

        @block.gpsimd
        def _(pool):
            g = nc.gpsimd

            def wait(name, v):
                pool.wait_ge(S[name], v)

            g.memset(zeros, 0.0).then_inc(S["ch_pool"], 1)
            g.memset(ident[:], 0.0)
            g.memset(utri[:], 1.0)
            g.memset(ones[:], 1.0)
            g.memset(TT[:], 0.0)
            g.iota(iota[:], [[1, 64]], base=0, channel_multiplier=0,
                   allow_small_or_imprecise_dtypes=True)
            g.iota(thr[:], [[CAP, 4]], base=CAP, channel_multiplier=0,
                   allow_small_or_imprecise_dtypes=True).then_inc(S["ch_pool"], 1)
            wait("ch_pool", 2)
            g.affine_select(out=ident[:], in_=ident[:], pattern=[[-1, P]], compare_op=ALU.not_equal, fill=1.0,
                            base=0, channel_multiplier=1)
            g.affine_select(out=utri[:], in_=utri[:], pattern=[[1, P]], compare_op=ALU.is_ge, fill=0.0,
                            base=0, channel_multiplier=-1).then_inc(S["consts_pool"], 1)
            g.dma_start(io["new_sconv_prompt"][0], zeros).then_inc(S["s_out"], 16)
            g.dma_start(io["new_sconv_sample"].rearrange("s k f -> (s k) f"),
                        io["state_sconv"].rearrange("s k f -> (s k) f")).then_inc(S["s_out"], 16)
            g.dma_start(io["new_ssm_conv_sample"][:, 0:2, :], io["state_ssm_conv"][:, 1:3, :]).then_inc(S["s_out"], 16)
            wait("dd_ok", 1)
            g.dma_start(dd_d, dd[:]).then_inc(S["s_dd"], 16)
            wait("s_dd", 16)
            for half in range(2):
                src = bass.AP(tensor=dd_d.tensor, offset=half * 16, ap=[[0, 64], [32, 16], [1, 16]])
                g.dma_start(WDT[64 * half:64 * half + 64, :, :].rearrange("p k (a b) -> p (k a) b", a=2), src)\
                 .then_inc(S["s_ddl"], 16)
            wait("acs_ok", 1)
            g.dma_start(acs_d, acsT).then_inc(S["s_acs"], 16)
            wait("bcT_ok", 1)
            g.dma_start(bc_d, bcT).then_inc(S["s_bcd"], 16)
            wait("s_bcd", 16)
            wait("s_acs", 16)

            def load_bcb(s):
                if s >= 2:
                    wait("item_done", 2 * (s - 1))
                if s == 1:
                    wait("silu_done", NCONV)
                src = bass.AP(tensor=bc_d.tensor, offset=s * 2048, ap=[[0, P], [1, 2048]])
                g.dma_start(BCb[s % 2].rearrange("p j n -> p (j n)"), src).then_inc(ld_bcb[s % 2], 16)

            def load_state(j):
                s, half = divmod(j, 2)
                if j >= 3:
                    pool.wait_ge(st_s[j % 3], 16 * (j // 3))
                g.dma_start(SR[:, j % 3, :, :],
                            state_rows[s, D * half:D * half + D, :].rearrange("(c p) n -> p c n", p=P))\
                 .then_inc(ld_s[j % 3], 16)

            def store_state(j):
                s, half = divmod(j, 2)
                wait("item_done", j + 1)
                g.dma_start(state_out[s, D * half:D * half + D, :].rearrange("(c p) n -> p c n", p=P),
                            SR[:, j % 3, :, :]).then_inc(st_s[j % 3], 16)

            wait("silu_done", NCONV)
            load_bcb(0)
            load_bcb(1)
            for j in range(3):
                load_state(j)
            wait("ms_ok", 6)
            for q in range(4):
                g.dma_start(mod_d[:, :, 256 * q:256 * q + 256], MS[32 * q:32 * q + 9, 2:6, :])\
                 .then_inc(S["s_mod"], 16)
            def load_acs(c):
                used(pool, 9 + c)
                src = bass.AP(tensor=acs_d.tensor, offset=c * CH, ap=[[0, P], [2 * CH, HEADS], [1, CH]])
                g.dma_start(bcA[c], src).then_inc(ld_bc[c], 16)

            load_acs(0)
            for j in range(16):
                store_state(j)
                if j + 3 < 16:
                    load_state(j + 3)
                if j % 2 == 1 and j // 2 + 2 < NS:
                    load_bcb(j // 2 + 2)
                if j == 9:
                    load_acs(1)
                if j == 13:
                    wait("tl_ok", 1)
                    cp = io["new_ssm_conv_prompt"][0]
                    cs = io["new_ssm_conv_sample"]
                    for t in range(3):
                        g.dma_start(cp[t, :].rearrange("(u c f) -> c u f", u=4, c=8),
                                    TLs[8 * t:8 * t + 8, :, :]).then_inc(S["s_tl"], 16)
                    for s in range(NS):
                        g.dma_start(cs[s, 2, :].rearrange("(u c f) -> c u f", u=4, c=8),
                                    TLs[24 + 8 * s:32 + 8 * s, :, :]).then_inc(S["s_tl"], 16)
            for r in range(3):
                pool.wait_ge(st_s[r], 16 * len(range(r, 16, 3)))
            wait("s_mod", 64)
            used(pool, len(UNITS) - 1)
            wait("item_done", 16)
            src = bass.AP(tensor=mod_d.tensor, offset=0, ap=[[0, P], [1, 4 * D]])
            g.dma_start(MB[:, 0, :, :].rearrange("p u f -> p (u f)"), src).then_inc(S["s_mb"], 16)
            g.dma_start(MB[0:NS, 1, :, :], mod_d[1:9, :, :]).then_inc(S["s_mb"], 16)
            for q in range(16):
                c, gr = divmod(q, GROUPS)
                if gr == 0:
                    pool.wait_ge(ld_bc[c], 16)
                if q >= 2:
                    wait("mt_ok", q - 1)
                for r in range(HPG):
                    h = gr * HPG + r
                    i = g.tensor_scalar(LT[q % 2][:, r, :], bcA[c][:, h, :], acst[:, c, h:h + 1], 0.0,
                                        ALU.subtract, ALU.min)
                i.then_inc(S["lt_ok"], 1)
                if gr == 0:
                    wait("dcy_ok", c + 1)
                    wait("xtok_ok", 4 * (c + 1))
                    if c == 1:
                        wait("st_ps", GROUPS)
                    v = xdec.rearrange("p (h d) -> p h d", h=HEADS)
                    g.tensor_tensor(v, xdt.rearrange("p (h d) -> p h d", h=HEADS),
                                    dcy[:, c, :].unsqueeze(2).to_broadcast([P, HEADS, HD]), ALU.mult)\
                     .then_inc(S["xdec_ok"], 1)
            wait("gn_ok", GROUPS)
            g.dma_start(RWt[:, :, :], io["router_w"][0].rearrange("(k p) e -> p k e", p=P)).then_inc(S["ld_rt"], 16)
            g.dma_start(rb, io["router_b"][0:1, :].to_broadcast([P, NE])).then_inc(S["ld_rt"], 16)
            wait("wo_ps", 2)
            g.dma_start(n2b, io["norm2_w"][0:1, :].to_broadcast([P, D])).then_inc(S["ld_n2"], 16)
            g.dma_start(BD, io["moe_b_down"][0]).then_inc(S["ld_bd"], 16)
            g.memset(BR, 0.0).then_inc(S["ch_pool"], 1)
            wait("ch_pool", 3)
            g.dma_start(BR[0:NE, :], io["moe_b_gate_up"][0]).then_inc(S["ld_br"], 16)
            wait("h2_ok", 3)
            g.dma_start(MB[:, 0, 1, :], io["final_norm_w"].rearrange("(o f) -> o f", o=1).to_broadcast([P, D]))\
             .then_inc(S["ld_fn"], 16)
            wait("s_out", 48)
            wait("s_tl", 11 * 16)

        @block.scalar
        def _(act):
            a = nc.scalar

            def wait(name, v):
                act.wait_ge(S[name], v)

            def link(ins, k=[0]):
                k[0] += 1
                ins.then_inc(S["ch_act"], 1)
                act.wait_ge(S["ch_act"], k[0])

            act.dma_start(XBr[0:1, 3072:4096], io["c_prompt"]).then_inc(S["ld_c"], 16)
            act.dma_start(XBr[1:9, 3072:4096], io["c_sample"]).then_inc(S["ld_c"], 16)
            act.dma_start(XT[:, 0:2, :], io["x_prompt"][0].rearrange("(t p) f -> p t f", p=P)).then_inc(S["ld_x"], 16)
            act.dma_start(XT[0:NS, 2, :], io["x_sample"][:, 0, :]).then_inc(S["ld_x"], 16)
            act.dma_start(PR1, io["ssd_conv_w"].rearrange("k (c f) -> (k c) f", f=P)).then_inc(S["ld_par"], 16)
            act.dma_start(PR2[0:32, :], io["ssd_conv_b"].rearrange("(c f) -> c f", f=P)).then_inc(S["ld_par"], 16)
            act.dma_start(PR2[32:40, :], io["norm1_w"][0].rearrange("(c f) -> c f", f=P)).then_inc(S["ld_par"], 16)
            act.dma_start(PR2[40:56, :], io["ssd_norm_w"].rearrange("(c f) -> c f", f=P)).then_inc(S["ld_par"], 16)
            act.dma_start(HI, io["state_ssm_conv"].rearrange("s k f -> (s k) f")).then_inc(S["ld_hist"], 16)
            act.dma_start(WDT[:], io["ssd_w_in"][:, INNER + CDIM:].rearrange("(k p) h -> p k h", p=P))\
               .then_inc(S["ld_wdt"], 16)
            with nc.allow_non_contiguous_dma(reason="one value per head"):
                act.dma_start(hsc[:, 0:1], io["ssd_dt_bias"].rearrange("(h o) -> h o", o=1)).then_inc(S["ld_hs"], 16)
                act.dma_start(hsc[:, 1:2], io["ssd_A_log"].rearrange("(h o) -> h o", o=1)).then_inc(S["ld_hs"], 16)
            act.dma_start(Dbc[:], io["ssd_D"].rearrange("(o h) -> o h", o=1).to_broadcast([P, HEADS]))\
               .then_inc(S["ld_D"], 16)
            wait("consts_dve", 1)
            for q in range(4):
                src = bass.AP(tensor=io["ada_b"].tensor, offset=io["ada_b"].offset + 256 * q,
                              ap=[[0, 9], [D, 6], [1, 256]])
                act.dma_start(AB[32 * q:32 * q + 9, :, :], src).then_inc(S["ld_ab"], 16)
            wait("ld_c", 32)
            a.activation(CR, CR, ACT.Silu).then_inc(S["silu_c"], 1)

            def root(at, n):
                wait("ss_ok", n)
                a.activation(st[:, at:at + 3], st[:, at:at + 3], ACT.Sqrt, bias=st[:, 15:16], scale=1.0 / D)\
                 .then_inc(S["rt3_ok"], 1)

            root(0, 1)
            wait("par_ps", 1)
            a.copy(cw[:], PS[7][:, 0:128])
            a.copy(pv[:], PS[7][:, 128:184]).then_inc(S["par_ok"], 1)
            wait("hist_ps", 1)
            a.copy(HT[:, 0:16, :].rearrange("p c k -> p (c k)"), PS[6][:, 0:384])
            a.copy(HT[:, 16:32, :].rearrange("p c k -> p (c k)"), PS[7][:, 0:384]).then_inc(S["hist_ok"], 1)
            wait("xnT_ps", 1)
            wait("m1_ok", 1)
            for k in range(KT):
                i = a.activation(h1T[:, k, 0:NP], PS[k // 2][:, 256 * (k % 2):256 * (k % 2) + 256], ACT.Identity,
                                 bias=m1[:, 0, k, 0:1], scale=m1[:, 1, k, 0:1])
            i.then_inc(S["h1_act"], 1)
            wait("ld_hs", 32)
            a.activation(hsc[:, 2:3], hsc[:, 1:2], ACT.Exp)
            wait("dt_t", 1)
            a.activation(dtt[1], dtt[1], ACT.Exp).then_inc(S["dt_e"], 1)
            wait("dt_u", 1)
            a.activation(dtt[3], dtt[2], ACT.Ln).then_inc(S["dt_l"], 1)
            wait("dt_ok", 1)
            a.activation(dd[:, 1, :], dtt[1][:, NP:NT], ACT.Exp).then_inc(S["dec_ok"], 1)

            def conv_silu(n):
                c = CHUNKS[n][3]
                wait("conv_done", n + 1)
                a.activation(XB[:, c, 0:NP], CV[:, n % 3, 0:NP], ACT.Silu, bias=pv[:, c:c + 1])
                a.activation(XB[:, c, NP:NT], CV[:, n % 3, 259:SEQC:4], ACT.Silu, bias=pv[:, c:c + 1])\
                 .then_inc(S["silu_done"], 1)

            def scale_states(j):
                s, half = divmod(j, 2)
                act.wait_ge(ld_s[j % 3], 16 * (j // 3 + 1))
                if j == 0:
                    wait("s_ddl", 32)
                for c in range(8):
                    i = a.mul(SR[:, j % 3, c, :], SR[:, j % 3, c, :], DDc[:, 8 * half + c, 1, s:s + 1])
                i.then_inc(S["s_scaled"], 1)

            for n, (u, j, kind, c) in enumerate(CHUNKS):
                wait("chunk_ps", n + 1)
                ps = PS[n % 4][:, 0:NT]
                if kind == "z":
                    if n == NCONV:
                        wait("s_mod", 64)
                        wait("s_acs", 16)
                        wait("dtTok_ps", 1)
                    a.activation(SZ[:, c, :], ps, ACT.Silu).then_inc(S["chunk_evac"], 1)
                    scale_states(n - NCONV)
                else:
                    if n == 0:
                        wait("consts_dve", 1)
                        wait("s_out", 48)
                    if n >= 4:
                        wait("conv_done", n - 3)
                    a.copy(RW[:, n % 4, 3:3 + NP], ps[:, 0:NP])
                    a.copy(RW[:, n % 4, 262:SEQR:4], ps[:, NP:NT]).then_inc(S["chunk_evac"], 1)
                    if n >= 1:
                        conv_silu(n - 1)
                    if n == NCONV - 1:
                        conv_silu(n)
            for c in range(2):
                act.wait_ge(ld_bc[c], 16)
                wait("lastx", c + 1)
                a.activation(dcy[:, c, :], dcy[:, c, :], ACT.Exp).then_inc(S["dcy_ok"], 1)
                if c == 1:
                    link(a.activation(dec1[:], bcA[1][:, :, CH - 1], ACT.Exp))
                wait("xtok_ps", 6 * c + 6)
                if c == 1:
                    wait("st_ps", GROUPS)
                a.copy(Btok[:, 0:512], PS[0])
                a.copy(Btok[:, 512:1024], PS[1]).then_inc(S["btok_ok"], 1)
                for gr in range(GROUPS):
                    q = c * GROUPS + gr
                    wait("lt_ok", q + 1)
                    a.activation(LT[q % 2], LT[q % 2], ACT.Exp).then_inc(S["exp_ok"], 1)
                    if c == 1:
                        if gr >= 2:
                            wait("y_ps", q - 1)
                        else:
                            wait("y_ps", GROUPS)
                        a.activation(CTs[gr % 2], bcA[1][:, HPG * gr:HPG * gr + HPG, :], ACT.Exp)\
                         .then_inc(S["ce_ok"], 1)
            for b in range(4):
                wait("hf_ps", b + 1)
                a.copy(xdt[:, 512 * b:512 * b + 512], PS[b % 2]).then_inc(S["hf_ok"], 1)
            act.wait_ge(S["hf_ok"], 4)
            act.dma_start(io["new_ssm_prompt"][0].rearrange("h p n -> (h p) n").rearrange("(c q) n -> q c n", q=P),
                          xdt.rearrange("p (c n) -> p c n", n=P)).then_inc(S["s_hf"], 16)
            def gn_root(gr):
                wait("gn_ps", gr + 1)
                if gr >= 2:
                    wait("gn_ok", gr - 1)
                a.activation(rs[gr % 2], PS[2 + gr % 2][:, 0:NT], ACT.Sqrt, bias=st[:, 15:16], scale=1.0 / 256)\
                 .then_inc(S["gn_rt"], 1)

            for gr in range(GROUPS):
                if gr == 0:
                    wait("y_ok", 16)
                    wait("samp_ok", 1)
                a.activation(sq[gr % 2], SZ[:, 2 * gr:2 * gr + 2, :], ACT.Square).then_inc(S["sq_ok"], 1)
                if gr >= 1:
                    gn_root(gr - 1)
            gn_root(GROUPS - 1)
            root(4, 2)
            for t in range(3):
                wait("h2T_ps", t + 1)
                R = ROWS[t]
                for b in range(2):
                    i = a.copy(h2T[:, 4 * b:4 * b + 4, 128 * t:128 * t + R],
                               PS[2 * (t % 2) + b][:, 0:512].rearrange("p (k r) -> p k r", k=4)[:, :, 0:R])
                i.then_inc(S["h2T_ok"], 1)
            for t in range(3):
                R = ROWS[t]
                wait("rt_m", t + 1)
                a.activation(ex[0:R, 0:4], m8[0:R, 0:4], ACT.Exp, bias=m8[0:R, 7:8]).then_inc(S["rt_e"], 1)
            wait("moe_ready", 1)
            wait("np_ok", 1)
            npass = act.value_load(npi[0:1, 0:1], min_val=1, max_val=MAXPASS)
            wait("gath_ps", 1)
            a.copy(hg, PS[2]).then_inc(S["a_hg"], 1)
            wait("hgT_ps", 1)
            a.copy(hgT.rearrange("p c s -> p (c s)"), PS[3]).then_inc(S["a_hgT"], 1)
            with act.Fori(0, npass * NE) as it:
                act.wait_ge(S["d_g"], it + 1)
                a.activation(sg, gg, ACT.Sigmoid, scale=ALPHA).then_inc(S["a_sig"], 1)
                act.wait_ge(S["gath_ps"], it + 2)
                a.copy(hg, PS[2]).then_inc(S["a_hg"], 1)
                act.wait_ge(S["hgT_ps"], it + 2)
                a.copy(hgT.rearrange("p c s -> p (c s)"), PS[3]).then_inc(S["a_hgT"], 1)
                act.wait_ge(S["swT_ps"], it + 1)
                a.copy(SwT, PS[2][:, 0:3 * P]).then_inc(S["a_swT"], 1)
                act.wait_ge(S["dn_used"], it * 2 + 2)
                a.copy(osb, PS[5]).then_inc(S["a_o"], 1)
            root(8, 3)

        @block.tensor
        def _(pe):
            t_ = nc.tensor

            def wait(name, v):
                pe.wait_ge(S[name], v)

            def mm(out, lhsT, rhs, start=True, stop=True):
                return t_.matmul(out, lhsT, rhs, start=start, stop=stop)

            wait("consts_pool", 1)
            wait("silu_c", 1)
            for k in range(KT):
                i = t_.transpose(PS[6][:, 9 * k:9 * k + 9], CR[:, P * k:P * k + P], ident[0:9, 0:9])
            i.then_inc(S["cT_ps"], 1)
            wait("ld_par", 64)
            t_.transpose(PS[7][:, 0:128], PR1, ident[:])
            t_.transpose(PS[7][:, 128:184], PR2, ident[0:56, 0:56]).then_inc(S["par_ps"], 1)
            wait("ld_hist", 16)
            wait("scT_ok", 1)
            wait("par_ok", 1)
            for c in range(NCH):
                i = t_.transpose(PS[6 + c // 16][:, 24 * (c % 16):24 * (c % 16) + 24], HI[:, P * c:P * c + P],
                                 ident[0:24, 0:24])
            i.then_inc(S["hist_ps"], 1)

            def loaded(u):
                pe.wait_ge(ld_w[u % 3], 16 * (u // 3 + 1))

            def ada(u):
                a = UNIT_A.index(u)
                loaded(u)
                if a >= 2:
                    wait("ms_ok", a - 1)
                if a == 1:
                    wait("hist_ok", 1)
                for k in range(KT):
                    for q in range(4):
                        i = t_.matmul(PS[5 + 2 * (a % 2)][32 * q:32 * q + 32, 0:256], scT[:, k, :],
                                      W[u % 3][:, k, 256 * q:256 * q + 256], start=(k == 0), stop=(k == KT - 1),
                                      tile_position=(0, 32 * q))
                i.then_inc(S["ada_ps"], 1)

            wait("xn_ok", 3)
            for k in range(KT):
                for t in range(2):
                    t_.transpose(PS[k // 2][:, 256 * (k % 2) + 128 * t:256 * (k % 2) + 128 * t + 128],
                                 xn[:, t, P * k:P * k + P], ident[:])
            for k in range(KT):
                i = t_.transpose(PS[4][:, 8 * k:8 * k + 8], xn[0:NS, 2, P * k:P * k + P], ident[0:NS, 0:NS])
            i.then_inc(S["xnT_ps"], 1)
            ada(0)
            ada(1)
            wait("ms_ok", 2)
            wait("hist_ok", 1)
            for u in range(2):
                for hf in range(2):
                    i = t_.transpose(PS[6][:, 128 * (2 * u + hf):128 * (2 * u + hf) + 128],
                                     MS[:, u, 128 * hf:128 * hf + 128], ident[:])
            i.then_inc(S["m1_ps"], 1)
            wait("h1_act", 1)
            wait("h1_dve", 1)
            wait("ld_wdt", 16)
            for k in range(KT):
                i = mm(PS[7][0:32, 0:NT], WDT[:, k, :], h1T[:, k, :], k == 0, k == KT - 1)
            i.then_inc(S["dt_ps"], 1)
            n = 0
            for u, (kind, col) in enumerate(UNITS):
                if u < 2:
                    continue
                if u == 11:
                    wait("bcT_ok", 1)
                    wait("conv_done", NCONV)
                    for q in range(4):
                        i = t_.transpose(PS[4][0:88, P * q:P * q + P],
                                         TT[:, q, :, :].rearrange("p t c -> p (t c)"), ident[:])
                    i.then_inc(S["tl_ps"], 1)
                if kind == ADA:
                    ada(u)
                else:
                    loaded(u)
                    for j in range(8):
                        if n >= 4:
                            wait("chunk_evac", n - 3)
                        for k in range(KT):
                            i = mm(PS[n % 4][:, 0:NT], W[u % 3][:, k, P * j:P * j + P], h1T[:, k, :],
                                   k == 0, k == KT - 1)
                        i.then_inc(S["chunk_ps"], 1)
                        n += 1
                if u == 2:
                    wait("dt_ok", 1)
                    for q in range(4):
                        i = t_.transpose(PS[4][:, 32 * q:32 * q + 32], dtt[q // 2][:, CH * (q % 2):CH * (q % 2) + CH],
                                         ident[0:32, 0:32])
                    i.then_inc(S["dtTok_ps"], 1)
                if u == 3:
                    wait("dtok_ok", 1)
                    for c in range(2):
                        mm(PS[6][:, 32 * c:32 * c + 32], utri[:], dtok[:, 2 + c, :])
                    for c in range(2):
                        i = mm(PS[6][0:32, 128 + 128 * c:256 + 128 * c], dtok[:, 2 + c, :], utri[:])
                    i.then_inc(S["acs_ps"], 1)
                if u == 5:
                    wait("bcs_ok", 1)
                    t_.transpose(PS[4][:, 0:128], bcs, ident[:]).then_inc(S["bcs_ps"], 1)

            def cb(q):
                c, gr = divmod(q, GROUPS)
                if q >= 2:
                    wait("mt_ok", q - 1)
                i = mm(PS[2 + q % 2][:, 0:CH], XB[:, XC + gr, CH * c:CH * c + CH],
                       XB[:, XC + GC + gr, CH * c:CH * c + CH])
                i.then_inc(S["cb_ps"], 1)

            for c in range(2):
                for b in range(6):
                    first = XC if b >= 4 else 0
                    if c == 0 and b < 2:
                        wait("chunk_evac", 48)
                    if c == 1 and b < 2:
                        wait("btok_ok", 1)
                    if 2 <= b:
                        wait("xtok_ok", 4 * c + b - 1)
                    for m in range(4):
                        i = t_.transpose(PS[b % 2][:, P * m:P * m + P],
                                         XB[:, first + 4 * (b - 4 if b >= 4 else b) + m, CH * c:CH * c + CH], ident[:])
                    i.then_inc(S["xtok_ps"], 1)
                if c == 0:
                    cb(0)
                for gr in range(GROUPS):
                    q = c * GROUPS + gr
                    if q + 1 < 16:
                        cb(q + 1)
                    if gr == 0:
                        wait("btok_ok", c + 1)
                        wait("xdec_ok", c + 1)
                    if q == 0:
                        wait("samp_ok", 1)
                    if q >= 2:
                        wait("st_ok", q - 1)
                    mm(PS[6 + q % 2][:, 0:256], Btok[:, P * gr:P * gr + P], xdec[:, 256 * gr:256 * gr + 256])\
                        .then_inc(S["st_ps"], 1)
                    wait("mt_ok", q + 1)
                    if c == 1:
                        wait("cts_ok", gr + 1)
                    if q >= 2:
                        wait("y_ok", q - 1)
                    if q == 0:
                        wait("tl_ok", 1)
                    for pair in range(2):
                        for r in (2 * pair, 2 * pair + 1):
                            h = HPG * gr + r
                            out = PS[4 + q % 2][64 * (r % 2):64 * (r % 2) + 64, CH * pair:CH * pair + CH]
                            i = mm(out, xdt[:, HD * h:HD * h + HD], MT[q % 2][:, r, :], True, c == 0)
                            if c == 1:
                                i = mm(out, prevT[:, HD * h:HD * h + HD], CTs[gr % 2][:, r, :], False, True)
                    i.then_inc(S["y_ps"], 1)
            wait("st_ok", 16)
            for b in range(4):
                if b >= 2:
                    wait("hf_ok", b - 1)
                for m in range(4):
                    i = t_.transpose(PS[b % 2][:, P * m:P * m + P], prevT[:, 512 * b + P * m:512 * b + P * m + P],
                                     ident[:])
                i.then_inc(S["hf_ps"], 1)
            for gr in range(GROUPS):
                wait("sq_ok", gr + 1)
                if gr >= 2:
                    wait("gn_ok", gr - 1)
                for m in range(2):
                    i = mm(PS[2 + gr % 2][:, 0:NT], ones[:], sq[gr % 2][:, m, :], m == 0, m == 1)
                i.then_inc(S["gn_ps"], 1)
            wait("hf_ok", 4)
            wait("gn_ok", GROUPS)
            for half in range(2):
                pe.wait_ge(ld_wo[half], 16)
                w = W[2] if half == 0 else wo1
                for k8 in range(8):
                    k = 8 * half + k8
                    for t in range(2):
                        for nh in range(2):
                            mm(PS[2 * t + nh], SZ[:, k, CH * t:CH * t + CH], w[:, k8, 512 * nh:512 * nh + 512],
                               k == 0, k == XC - 1)
                for k8 in range(8):
                    k = 8 * half + k8
                    for q in range(4):
                        i = t_.matmul(PS[4][32 * q:32 * q + NS, 0:256], SZ[:, k, NP:NT], w[:, k8, 256 * q:256 * q + 256],
                                      start=(k == 0), stop=(k == XC - 1), tile_position=(0, 32 * q))
                i.then_inc(S["wo_ps"], 1)
            for t in range(3):
                R = ROWS[t]
                wait("h2_ok", t + 1)
                if t == 0:
                    wait("xm_ok", 3)
                if t == 2:
                    wait("h2T_ok", 1)
                for k in range(KT):
                    i = t_.transpose(PS[2 * (t % 2) + k // 4][:, P * (k % 4):P * (k % 4) + R],
                                     h2[0:R, t, P * k:P * k + P], ident[0:R, 0:R])
                i.then_inc(S["h2T_ps"], 1)
            wait("ld_rt", 32)
            for t in range(3):
                R = ROWS[t]
                wait("h2T_ok", t + 1)
                for k in range(KT):
                    i = mm(PS[4][0:R, 32 * t:32 * t + 32], h2T[:, k, CH * t:CH * t + R], RWt[:, k, :],
                           k == 0, k == KT - 1)
                i.then_inc(S["lg_ps"], 1)
            wait("rt_p", 3)
            for t in range(3):
                R = ROWS[t]
                for t2 in range(t):
                    mm(PS[5][0:R, 32 * t:32 * t + 32], ones[:, 0:R], mask[:, t2, :], t2 == 0, False)
                mm(PS[5][0:R, 32 * t:32 * t + 32], utri[0:R, 0:R], mask[0:R, t, :], t == 0, True)
            for t in range(3):
                R = ROWS[t]
                i = mm(PS[5][0:1, 96:128], ones[0:R, 0:1], mask[0:R, t, :], t == 0, t == 2)
            i.then_inc(S["pos_ps"], 1)
            for t in range(3):
                R = ROWS[t]
                i = t_.transpose(PS[6][0:NE, CH * t:CH * t + R], comb[0:R, :, t], ident[0:R, 0:R])
            i.then_inc(S["cmb_ps"], 1)
            wait("cmb_ok", 1)
            wait("ld_bd", 16)
            for t in range(3):
                R = ROWS[t]
                for nh in range(2):
                    i = mm(PS[2 * (t % 2) + nh][0:R, :], combT[:, CH * t:CH * t + R], BD[:, 512 * nh:512 * nh + 512])
                i.then_inc(S["ai_ps"], 1)
                if t == 1:
                    wait("acc_ok", 1)
            wait("moe_ready", 1)
            wait("np_ok", 1)
            npass = pe.value_load(npi[0:1, 0:1], min_val=1, max_val=MAXPASS)

            def gather():
                for t in range(3):
                    for hf in range(2):
                        i = mm(PS[2][64 * hf:64 * hf + 64, :], G[:, t, :], h2[:, t, 512 * hf:512 * hf + 512],
                               t == 0, t == 2)
                i.then_inc(S["gath_ps"], 1)

            def turn_rows():
                for c in range(4):
                    i = t_.transpose(PS[3][:, P * c:P * c + P], hg[:, P * c:P * c + P], ident[:])
                i.then_inc(S["hgT_ps"], 1)

            def scatter(it):
                for t in range(3):
                    pe.wait_ge(S["d_add"], it * 3 + (t + 1))
                    for nh in range(2):
                        i = mm(PS[6 + nh], SwT[64 * nh:64 * nh + 64, P * t:P * t + P], osb[64 * nh:64 * nh + 64, :])
                    i.then_inc(S["sc_ps"], 1)

            wait("d_G", 1)
            gather()
            wait("a_hg", 1)
            turn_rows()
            with pe.Fori(0, npass * NE) as it:
                pe.wait_ge(S["d_bs"], it + 1)
                pe.wait_ge(S["a_hgT"], it + 1)
                pe.wait_ge(S["d_guf"], it + 1)
                for n2 in range(2):
                    for hf in range(2):
                        mm(PGU[64 * hf:64 * hf + 64, n2, :], bsel,
                           BR[:, 1024 * hf + 512 * n2:1024 * hf + 512 * n2 + 512], True, False)
                for j in range(4):
                    pe.wait_ge(gu_ld[j], it * 16 + 16)
                    for k in (2 * j, 2 * j + 1):
                        for n2 in range(2):
                            for hf in range(2):
                                i = mm(PGU[64 * hf:64 * hf + 64, n2, :], hgT[:, k % 4, 64 * (k // 4):64 * (k // 4) + 64],
                                       BIG[:, 2 * k + hf, 512 * n2:512 * n2 + 512], False, k == KT - 1)
                    i.then_inc(S["gu_used"], 1)
                pe.wait_ge(S["a_o"], it + 1)
                pe.wait_ge(S["a_swT"], it + 1)
                scatter(it)
                pe.wait_ge(S["d_G"], it + 2)
                gather()
                pe.wait_ge(S["d_act"], it + 1)
                pe.wait_ge(S["d_actT"], it + 1)
                for c in range(4):
                    i = t_.transpose(PS[4][:, P * c:P * c + P], aa[:, P * c:P * c + P], ident[:])
                i.then_inc(S["actT_ps"], 1)
                pe.wait_ge(S["a_hg"], it + 2)
                turn_rows()
                pe.wait_ge(S["d_gw"], it + 1)
                for t in range(3):
                    i = t_.transpose(PS[2][:, P * t:P * t + P], Gw[:, t, :, :].rearrange("p d j -> p (d j)"), ident[:])
                i.then_inc(S["swT_ps"], 1)
                pe.wait_ge(S["d_actT"], it + 2)
                for j in range(2):
                    pe.wait_ge(dn_ld[j], it * 16 + 16)
                    for k in range(4 * j, 4 * j + 4):
                        for nh in range(2):
                            i = mm(PS[5][64 * nh:64 * nh + 64, :], actT[:, k % 4, 64 * (k // 4):64 * (k // 4) + 64],
                                   BIG[:, 16 + k, 512 * nh:512 * nh + 512], k == 0, k == KT - 1)
                    i.then_inc(S["dn_used"], 1)
            pe.wait_ge(S["a_o"], npass * NE + 1)
            pe.wait_ge(S["a_swT"], npass * NE + 1)
            scatter(npass * NE)

        @block.vector
        def _(dve):
            v = nc.vector

            def wait(name, val):
                dve.wait_ge(S[name], val)

            k_ = [0]

            def link(ins):
                k_[0] += 1
                ins.then_inc(S["ch_dve"], 1)
                dve.wait_ge(S["ch_dve"], k_[0])

            v.memset(AB, 0.0)
            v.memset(scT[:], 0.0)
            v.memset(RW[:, :, 0:3], 0.0).then_inc(S["consts_dve"], 1)
            wait("ld_x", 32)

            def rstd(x, at, jk, n):
                for t in range(3):
                    R = ROWS[t]
                    i = v.tensor_tensor_reduce(jk[0:R, :], x[0:R, t, :], x[0:R, t, :], 1.0, 0.0, ALU.mult, ALU.add,
                                               st[0:R, at + t:at + t + 1])
                    if t < 2:
                        link(i)
                i.then_inc(S["ss_ok"], 1)
                wait("rt3_ok", n)
                link(v.reciprocal(st[:, at:at + 3], st[:, at:at + 3]))

            link(v.memset(st[:], 1.0))
            link(v.memset(st[:, 15:16], EPS))
            rstd(XT, 0, junk, 1)
            for t in range(3):
                R = ROWS[t]
                v.tensor_scalar(xn[0:R, t, :], XT[0:R, t, :], st[0:R, t:t + 1], None, ALU.mult).then_inc(S["xn_ok"], 1)
            wait("cT_ps", 1)
            v.tensor_copy(scT[:, :, 0:9], PS[6][:, 0:72].rearrange("p (k r) -> p k r", k=KT)).then_inc(S["scT_ok"], 1)

            def mod_rows(a):
                if a == 0:
                    wait("ld_ab", 64)
                wait("ada_ps", a + 1)
                v.tensor_tensor(MS[:, a, :], PS[5 + 2 * (a % 2)][:, 0:256], AB[:, a, :], ALU.add)\
                 .then_inc(S["ms_ok"], 1)

            mod_rows(0)
            mod_rows(1)
            wait("m1_ps", 1)
            wait("par_ok", 1)
            src = PS[6].rearrange("p (u hf q r) -> p u hf q r", u=2, hf=2, q=4)
            for u in range(2):
                for hf in range(2):
                    i = v.tensor_copy(m1[:, u, hf::2, :], src[:, u, hf, :, 0:9])
            link(i)
            link(v.tensor_scalar(m1[:, 1, :, :], m1[:, 1, :, :], 1.0, None, ALU.add))
            v.tensor_tensor(m1[:, 1, :, :], m1[:, 1, :, :], pv[:, 32:40].unsqueeze(2).to_broadcast([P, KT, 9]),
                            ALU.mult).then_inc(S["m1_ok"], 1)
            dve.wait_ge(S["m1_ok"], 1)
            wait("xnT_ps", 1)
            hs = h1T[:, :, NP:NT]
            link(v.tensor_tensor(hs, PS[4][:, 0:64].rearrange("p (k s) -> p k s", k=KT), m1[:, 1, :, 1:9], ALU.mult))
            v.tensor_tensor(hs, hs, m1[:, 0, :, 1:9], ALU.add).then_inc(S["h1_dve"], 1)
            wait("dt_ps", 1)
            wait("ld_hs", 32)
            link(v.tensor_scalar(dtt[0], PS[7][0:32, 0:NT], hsc[:, 0:1], None, ALU.add))
            v.scalar_tensor_tensor(dtt[1], dtt[0], -1.0, dtt[0], ALU.mult, ALU.min).then_inc(S["dt_t"], 1)
            wait("dt_e", 1)
            v.tensor_scalar(dtt[2], dtt[1], 1.0, None, ALU.add).then_inc(S["dt_u"], 1)
            wait("dt_l", 1)
            link(v.tensor_scalar(dtt[2], dtt[2], -1.0, None, ALU.add))
            tz = xn[0:32, 0, 0:NT]
            wait("xnT_ps", 1)
            link(v.tensor_scalar(tz, dtt[2], 0.0, None, ALU.is_equal))
            link(v.tensor_tensor(dtt[2], dtt[2], tz, ALU.add))
            link(v.reciprocal(dtt[2], dtt[2]))
            link(v.tensor_tensor(dtt[2], dtt[1], dtt[2], ALU.mult))
            link(v.tensor_tensor(dtt[3], dtt[3], dtt[2], ALU.mult))
            link(v.tensor_tensor(dtt[1], dtt[1], tz, ALU.mult))
            link(v.tensor_tensor(dtt[3], dtt[3], dtt[1], ALU.add))
            link(v.tensor_scalar(hsc[:, 3:4], hsc[:, 2:3], -1.0, None, ALU.mult))
            link(v.scalar_tensor_tensor(dtt[0], dtt[0], 0.0, dtt[3], ALU.max, ALU.add))
            v.tensor_scalar(dtt[1], dtt[0], hsc[:, 3:4], None, ALU.mult).then_inc(S["dt_ok"], 1)
            wait("dec_ok", 1)
            v.tensor_copy(dd[:, 0, :], dtt[0][:, NP:NT]).then_inc(S["dd_ok"], 1)
            wait("ld_D", 16)
            v.tensor_copy(Dcol[0:64, :], Dbc[0:64, 0::2])
            link(v.tensor_copy(Dcol[64:128, :], Dbc[64:128, 1::2]))
            wait("hist_ok", 1)

            for n in range(NCONV):
                u, j, _, c = CHUNKS[n]
                if n == 16:
                    mod_rows(2)
                if n == 24:
                    mod_rows(3)
                raw = RW[:, n % 4, :]
                wait("chunk_evac", n + 1)
                link(v.tensor_copy(raw[:, 259:SEQR].rearrange("p (s k) -> p s k", k=4)[:, :, 0:3],
                                   HT[:, c, :].rearrange("p (s k) -> p s k", k=3)))
                if n >= 3:
                    wait("silu_done", n - 2)
                link(v.tensor_scalar(CV[:, n % 3, :], raw[:, 0:SEQC], cw[:, c:c + 1], None, ALU.mult))
                for k in range(1, CONV):
                    i = v.scalar_tensor_tensor(CV[:, n % 3, :], raw[:, k:k + SEQC], cw[:, NCH * k + c:NCH * k + c + 1],
                                               CV[:, n % 3, :], ALU.mult, ALU.add)
                    if k < CONV - 1:
                        link(i)
                    if k == 1:
                        v.tensor_copy(TT[:, c // 8, 0:3, c % 8], raw[:, NP:NP + 3])
                        v.tensor_copy(TT[:, c // 8, 3:11, c % 8], raw[:, 262:SEQR:4])
                i.then_inc(S["conv_done"], 1)
                if n == 9:
                    wait("dtTok_ps", 1)
                    v.tensor_copy(dtok[:].rearrange("p a b -> p (a b)"), PS[4][:, 0:128]).then_inc(S["dtok_ok"], 1)
                if n == 17:
                    wait("acs_ps", 1)
                    v.tensor_copy(acst[:].rearrange("p a b -> p (a b)"), PS[6][:, 0:64])
                    v.tensor_copy(acsT, PS[6][0:32, 128:384].rearrange("p (c l) -> p c l", c=2))\
                     .then_inc(S["acs_ok"], 1)
                    wait("silu_done", 16)
                    dve.wait_ge(S["acs_ok"], 1)
                    v.tensor_copy(bcs.rearrange("p (s j) -> p s j", j=16),
                                  XB[:, XC:NCH, NP:NT].rearrange("p j s -> p s j")).then_inc(S["bcs_ok"], 1)
                if n == 25:
                    wait("bcs_ps", 1)
                    v.tensor_copy(bcT, PS[4][:, 0:128]).then_inc(S["bcT_ok"], 1)
            mod_rows(4)
            mod_rows(5)
            wait("silu_done", NCONV)
            wait("s_ddl", 32)
            link(v.tensor_tensor(xdtS[:], XB[:, 0:XC, NP:NT], DDc[:, :, 0, :], ALU.mult))
            wait("m1_ok", 1)
            junkp = [PS[6], PS[7]]
            for j in range(16):
                s, half = divmod(j, 2)
                if half == 0:
                    dve.wait_ge(ld_bcb[s % 2], 16 * (s // 2 + 1))
                wait("s_scaled", j + 1)
                for c in range(8):
                    cc = 8 * half + c
                    i = v.scalar_tensor_tensor(SR[:, j % 3, c, :], BCb[s % 2][:, cc // 2, :], xdtS[:, cc, s:s + 1],
                                               SR[:, j % 3, c, :], ALU.mult, ALU.add)
                link(i)
                for c in range(8):
                    cc = 8 * half + c
                    i = v.tensor_tensor_reduce(junkp[c // 4][:, P * (c % 4):P * (c % 4) + P], SR[:, j % 3, c, :],
                                               BCb[s % 2][:, 8 + cc // 2, :], 1.0, 0.0, ALU.mult, ALU.add,
                                               yS[:, cc, s:s + 1])
                i.then_inc(S["item_done"], 1)
                dve.wait_ge(S["item_done"], j + 1)
                if j == 12:
                    wait("tl_ps", 1)
                    v.tensor_copy(TLs.rearrange("p u f -> p (u f)"), PS[4][0:88, :]).then_inc(S["tl_ok"], 1)
            link(v.tensor_tensor(xdtS[:], XB[:, 0:XC, NP:NT], Dcol[:].unsqueeze(2).to_broadcast([P, XC, NS]), ALU.mult))
            link(v.tensor_tensor(yS[:], yS[:], xdtS[:], ALU.add))
            wait("chunk_evac", 48)
            v.tensor_tensor(SZ[:, :, NP:NT], yS[:], SZ[:, :, NP:NT], ALU.mult).then_inc(S["samp_ok"], 1)

            def y_rows(q):
                c, gr = divmod(q, GROUPS)
                wait("y_ps", q + 1)
                for m in range(2):
                    i = v.scalar_tensor_tensor(PS[4 + q % 2][:, CH * m:CH * m + CH], XB[:, 2 * gr + m, CH * c:CH * c + CH],
                                               Dcol[:, 2 * gr + m:2 * gr + m + 1], PS[4 + q % 2][:, CH * m:CH * m + CH],
                                               ALU.mult, ALU.add)
                link(i)
                z = SZ[:, 2 * gr:2 * gr + 2, CH * c:CH * c + CH]
                v.tensor_tensor(z, PS[4 + q % 2][:, 0:256].rearrange("p (m l) -> p m l", m=2), z, ALU.mult)\
                 .then_inc(S["y_ok"], 1)

            wait("s_tl", 11 * 16)
            for c in range(2):
                dve.wait_ge(ld_bc[c], 16)
                v.tensor_tensor(dcy[:, c, :], bcA[c][:, :, CH - 1], acst[:, c, :], ALU.subtract)\
                 .then_inc(S["lastx"], 1)
                if c == 1:
                    wait("y_ps", GROUPS)
                for b in range(4):
                    wait("xtok_ps", 6 * c + b + 1)
                    v.tensor_tensor(xdt[:, 512 * b:512 * b + 512].rearrange("p (h d) -> p h d", d=HD),
                                    PS[b % 2].rearrange("p (h d) -> p h d", d=HD),
                                    dtok[:, c, 8 * b:8 * b + 8].unsqueeze(2).to_broadcast([P, 8, HD]), ALU.mult)\
                     .then_inc(S["xtok_ok"], 1)
                for gr in range(GROUPS):
                    q = c * GROUPS + gr
                    wait("cb_ps", q + 1)
                    if q >= 2:
                        wait("y_ps", q - 1)
                    link(v.tensor_tensor(CBm[q % 2], PS[2 + q % 2][:, 0:CH], utri[:], ALU.mult))
                    wait("exp_ok", q + 1)
                    v.tensor_tensor(MT[q % 2], LT[q % 2], CBm[q % 2].unsqueeze(1).to_broadcast([P, HPG, CH]),
                                    ALU.mult).then_inc(S["mt_ok"], 1)
                    if c == 1:
                        wait("ce_ok", gr + 1)
                        v.tensor_tensor(CTs[gr % 2], CTs[gr % 2],
                                        XB[:, XC + GC + gr, CH:2 * CH].unsqueeze(1).to_broadcast([P, HPG, CH]),
                                        ALU.mult).then_inc(S["cts_ok"], 1)
                    if q >= 1:
                        y_rows(q - 1)
                    wait("st_ps", q + 1)
                    pr = prevT[:, 256 * gr:256 * gr + 256]
                    if c == 0:
                        v.tensor_copy(pr, PS[6 + q % 2][:, 0:256]).then_inc(S["st_ok"], 1)
                    else:
                        wait("y_ps", q + 1)
                        p3 = pr.rearrange("p (h d) -> p h d", d=HD)
                        link(v.tensor_tensor(p3, p3, dec1[:, HPG * gr:HPG * gr + HPG].unsqueeze(2)
                                             .to_broadcast([P, HPG, HD]), ALU.mult))
                        v.tensor_tensor(pr, pr, PS[6 + q % 2][:, 0:256], ALU.add).then_inc(S["st_ok"], 1)
            y_rows(15)
            dve.wait_ge(S["y_ok"], 16)
            for gr in range(GROUPS):
                wait("gn_rt", gr + 1)
                r = rs[gr % 2]
                link(v.reciprocal(r, r))
                for m in range(2):
                    i = v.scalar_tensor_tensor(SZ[:, 2 * gr + m, :], SZ[:, 2 * gr + m, :],
                                               pv[:, 40 + 2 * gr + m:41 + 2 * gr + m], r, ALU.mult, ALU.mult)
                i.then_inc(S["gn_ok"], 1)
            wait("s_mb", 32)
            wait("wo_ps", 2)
            for t in range(2):
                for nh in range(2):
                    i = v.tensor_tensor(PS[2 * t + nh], PS[2 * t + nh], MB[:, 0, 0, 512 * nh:512 * nh + 512], ALU.mult)
            for q in range(4):
                i = v.tensor_copy(acc[0:NS, 2, 256 * q:256 * q + 256], PS[4][32 * q:32 * q + NS, 0:256])
            link(i)
            for t in range(2):
                for nh in range(2):
                    xx = XT[:, t, 512 * nh:512 * nh + 512]
                    i = v.tensor_tensor(xx, xx, PS[2 * t + nh], ALU.add)
            link(v.tensor_tensor(acc[0:NS, 2, :], acc[0:NS, 2, :], MB[0:NS, 1, 0, :], ALU.mult))
            i = v.tensor_tensor(XT[0:NS, 2, :], XT[0:NS, 2, :], acc[0:NS, 2, :], ALU.add)
            i.then_inc(S["xm_ok"], 3)
            dve.wait_ge(S["xm_ok"], 3)
            wait("ld_n2", 16)
            link(v.scalar_tensor_tensor(MB[:, 0, 2, :], MB[:, 0, 2, :], 1.0, n2b, ALU.add, ALU.mult))
            link(v.scalar_tensor_tensor(MB[0:NS, 1, 2, :], MB[0:NS, 1, 2, :], 1.0, n2b[0:NS, :], ALU.add, ALU.mult))
            link(v.memset(h2[:, 2, :], 0.0))
            rstd(XT, 4, acc[:, 0, :], 2)
            for t in range(3):
                R = ROWS[t]
                q = t // 2
                link(v.scalar_tensor_tensor(h2[0:R, t, :], XT[0:R, t, :], st[0:R, 4 + t:5 + t], MB[0:R, q, 2, :],
                                            ALU.mult, ALU.mult))
                v.tensor_tensor(h2[0:R, t, :], h2[0:R, t, :], MB[0:R, q, 1, :], ALU.add).then_inc(S["h2_ok"], 1)
            wait("ld_rt", 32)
            wait("wo_ps", 2)
            v.memset(posx, -1.0)
            v.memset(comb, 0.0)
            v.memset(SwT, 0.0)
            v.memset(G, 0.0)
            v.memset(Gw, 0.0)
            link(v.memset(mask, 0.0))
            for t in range(3):
                R = ROWS[t]
                wait("lg_ps", 3)
                link(v.tensor_tensor(lg[0:R, :], PS[4][0:R, 32 * t:32 * t + 32], rb[0:R, :], ALU.add))
                link(v.max(m8[0:R, :], lg[0:R, :]))
                link(v.max_index(ix[0:R, :], m8[0:R, :], lg[0:R, :]))
                link(v.tensor_copy(ixf[0:R, :], ix[0:R, :]))
                v.tensor_scalar(m8[0:R, 7:8], m8[0:R, 0:1], -1.0, None, ALU.mult).then_inc(S["rt_m"], 1)
                wait("rt_e", t + 1)
                link(v.tensor_reduce(ex[0:R, 4:5], ex[0:R, 0:4], AX.X, ALU.add))
                link(v.reciprocal(ex[0:R, 4:5], ex[0:R, 4:5]))
                link(v.tensor_scalar(ex[0:R, 0:4], ex[0:R, 0:4], ex[0:R, 4:5], None, ALU.mult))
                for k in range(TOPK):
                    v.tensor_scalar(oh[0:R, k, :], iota[0:R, 0:NE], ixf[0:R, k:k + 1], None, ALU.is_equal)
                    i = v.tensor_scalar(pw[0:R, k, :], iota[0:R, 0:NE], ixf[0:R, k:k + 1], ex[0:R, k:k + 1],
                                        ALU.is_equal, ALU.mult)
                link(i)
                v.tensor_reduce(mask[0:R, t, :], oh[0:R, :, :].rearrange("p k e -> p e k"), AX.X, ALU.add)
                v.tensor_reduce(comb[0:R, :, t], pw[0:R, :, :].rearrange("p k e -> p e k"), AX.X, ALU.add)\
                 .then_inc(S["rt_p"], 1)
                dve.wait_ge(S["rt_p"], t + 1)
            wait("pos_ps", 1)
            link(v.tensor_reduce(cnt[:, 0:1], PS[5][0:1, 96:128], AX.X, ALU.max))
            link(v.tensor_scalar(cnt[:, 1:5], thr[:], cnt[:, 0:1], None, ALU.is_lt))
            link(v.tensor_reduce(cnt[:, 5:6], cnt[:, 1:5], AX.X, ALU.add))
            v.tensor_scalar(npi[:], cnt[:, 5:6], 1.0, None, ALU.add).then_inc(S["np_ok"], 1)
            for t in range(3):
                R = ROWS[t]
                i = v.tensor_tensor(mask[0:R, t, :], mask[0:R, t, :], PS[5][0:R, 32 * t:32 * t + 32], ALU.mult)
            link(i)
            for t in range(3):
                R = ROWS[t]
                for p_ in range(MAXPASS):
                    i = v.tensor_scalar(posx[0:R, NE * p_:NE * p_ + NE, t], mask[0:R, t, :], -1.0 - CAP * p_, None,
                                        ALU.add)
            link(i)
            wait("cmb_ps", 1)
            v.tensor_copy(combT, PS[6][0:NE, 0:NT]).then_inc(S["cmb_ok"], 1)
            for t in range(3):
                R = ROWS[t]
                wait("ai_ps", t + 1)
                for nh in range(2):
                    i = v.tensor_copy(acc[0:R, t, 512 * nh:512 * nh + 512], PS[2 * (t % 2) + nh][0:R, :])
                i.then_inc(S["acc_ok"], 1)
            dve.wait_ge(S["acc_ok"], 3)
            wait("ld_br", 16)
            link(v.memset(osb, 0.0))

            def gather_matrix(i):
                return v.tensor_tensor(G, iota[:].unsqueeze(1).to_broadcast([P, 3, CAP]),
                                       posx[:, i, :].unsqueeze(2).to_broadcast([P, 3, CAP])
                                       if isinstance(i, int) else
                                       posx[:, bass.ds(i, 1), :].rearrange("p o t -> p (o t)").unsqueeze(2)
                                       .to_broadcast([P, 3, CAP]), ALU.is_equal)

            def bias_select(e):
                col = eye[:, 0:1] if isinstance(e, int) else eye[:, bass.ds(e, 1)]
                return v.tensor_copy(bsel, col.to_broadcast([P, 64]))

            v.tensor_copy(eye[:, 0:NE], ident[:, 0:NE])
            link(v.tensor_copy(eye[:, NE:NE + 1], ident[:, 0:1]))
            gather_matrix(0).then_inc(S["d_G"], 1)
            bias_select(0).then_inc(S["d_bs"], 1)
            v.tensor_copy(cnt[:, 6:7], cnt[:, 5:6]).then_inc(S["moe_ready"], 1)
            for nm in ("d_guf", "d_add", "d_actT", "a_o", "a_swT"):
                dve.sem_inc(S[nm], 1)
            wait("np_ok", 1)
            wait("moe_ready", 1)
            npass = dve.value_load(npi[0:1, 0:1], min_val=1, max_val=MAXPASS)
            flat = PGU[:, :, :].rearrange("p a b -> p (a b)")

            def adds(it):
                for t in range(3):
                    R = ROWS[t]
                    dve.wait_ge(S["sc_ps"], it * 3 + (t + 1))
                    for nh in range(2):
                        y = acc[0:R, t, 512 * nh:512 * nh + 512]
                        i = v.tensor_tensor(y, y, PS[6 + nh][0:R, :], ALU.add)
                    i.then_inc(S["d_add"], 1)

            with dve.Fori(0, npass) as ps:
                with dve.Fori(0, NE) as e:
                    it = ps * NE + e
                    dve.wait_ge(S["gu_used"], it * 4 + 4)
                    v.tensor_scalar(gg, flat[:, 0::2], LIMIT, None, ALU.min).then_inc(S["d_g"], 1)
                    v.tensor_scalar(uu, flat[:, 1::2], -LIMIT, LIMIT, ALU.max, ALU.min).then_inc(S["d_guf"], 1)
                    dve.wait_ge(S["d_guf"], it + 2)
                    v.scalar_tensor_tensor(uu, uu, 1.0, gg, ALU.add, ALU.mult)
                    for d_ in range(2):
                        i = v.tensor_tensor(Gw[:, :, d_, :], G, comb[:, bass.ds(e, 1), :].rearrange("p o t -> p (o t)")
                                            .unsqueeze(2).to_broadcast([P, 3, CAP]), ALU.mult)
                    i.then_inc(S["d_gw"], 1)
                    dve.wait_ge(S["d_gw"], it + 1)
                    gather_matrix(it + 1).then_inc(S["d_G"], 1)
                    dve.wait_ge(S["a_sig"], it + 1)
                    v.tensor_tensor(aa, uu, sg, ALU.mult).then_inc(S["d_act"], 1)
                    bias_select(e + 1).then_inc(S["d_bs"], 1)
                    adds(it)
                    dve.wait_ge(S["actT_ps"], it + 1)
                    v.tensor_copy(actT.rearrange("p c s -> p (c s)"), PS[4]).then_inc(S["d_actT"], 1)
            adds(npass * NE)
            dve.wait_ge(S["d_add"], npass * (NE * 3) + 4)
            wait("ld_fn", 16)
            for t in range(3):
                R = ROWS[t]
                link(v.tensor_tensor(acc[0:R, t, :], acc[0:R, t, :], MB[0:R, t // 2, 3, :], ALU.mult))
                link(v.tensor_tensor(acc[0:R, t, :], acc[0:R, t, :], XT[0:R, t, :], ALU.add))
            rstd(acc, 8, h2[:, 0, :], 3)
            for t in range(3):
                R = ROWS[t]
                v.scalar_tensor_tensor(XT[0:R, t, :], acc[0:R, t, :], st[0:R, 8 + t:9 + t], MB[0:R, 0, 1, :],
                                       ALU.mult, ALU.mult).then_inc(S["y_done"], 1)



_UNUSED = ("sc_w_in", "sc_conv_w", "sc_w_out")
_OUTS = [("y_prompt", (1, NP, D)), ("y_sample", (NS, 1, D)), ("new_ssm_prompt", (1, HEADS, HD, STATE)),
         ("new_ssm_conv_prompt", (1, CONV - 1, CDIM)), ("new_sconv_prompt", (1, 2, D)),
         ("new_ssm_sample", (NS, HEADS, HD, STATE)), ("new_ssm_conv_sample", (NS, CONV - 1, CDIM)),
         ("new_sconv_sample", (NS, 2, D))]


def kernel(**inputs):
    import numpy as _np
    import concourse.bacc as _bacc
    from concourse import mybir as _mybir
    from concourse.bass_utils import run_bass_kernel_spmd as _run

    nc = _bacc.Bacc("TRN2", target_bir_lowering=False, num_devices=1)
    arrays, io = {}, {}
    for name, x in inputs.items():
        if name in _UNUSED:
            continue
        x = _np.ascontiguousarray(x)
        arrays[f"in_{name}"] = x
        io[name] = nc.dram_tensor(f"in_{name}", x.shape, _mybir.dt.from_np(x.dtype), kind="ExternalInput").ap()
    for name, shape in _OUTS:
        io[name] = nc.dram_tensor(f"out_{name}", shape, _mybir.dt.float32, kind="ExternalOutput").ap()
    build(nc, io)
    r = _run(nc, [arrays], core_ids=[0])
    return tuple(r.results[0][f"out_{name}"] for name, _ in _OUTS)
```

```python
from contextlib import ExitStack

import concourse.bass as bass
from concourse import mybir

F32 = mybir.dt.float32
I32 = mybir.dt.int32
U32 = mybir.dt.uint32
ALU = mybir.AluOpType
ACT = mybir.ActivationFunctionType
AX = mybir.AxisListType

P = 128
D = 1024
KT = D // P
NP = 256
NS = 8
NT = NP + NS
ROWS = (128, 128, NS)
INNER = 2 * D
HEADS, HD = 32, 64
GROUPS, HPG, STATE = 8, 4, 128
CONV = 4
XC = INNER // P
GC = GROUPS
NCH = XC + 2 * GC
CDIM = NCH * P
CH = 128
NSLOT = 5
NE = 32
TOPK = 4
CAP = 64
MAXPASS = -(-NT // CAP)
LIMIT = 7.0
ALPHA = 1.702
EPS = 1e-5
SEQR = 3 + NP + 4 * NS
SEQC = SEQR - 3

ADA, WIN = "ada", "win"
UNITS = [(ADA, 0), (ADA, 1), (WIN, 4096), (ADA, 2), (WIN, 5120), (ADA, 3), (WIN, 2048), (ADA, 4), (WIN, 3072),
         (ADA, 5), (WIN, 1024), (WIN, 0)]
CHUNKS = []
for _u, (_kind, _col) in enumerate(UNITS):
    if _kind == WIN:
        for _j in ((4, 5, 6, 7, 0, 1, 2, 3) if _col == D else range(8)):
            _c = _col // P + _j
            CHUNKS.append((_u, _j, "z", _c) if _c < XC else (_u, _j, "c", _c - XC))
NCONV = NCH
UNIT_A = [u for u, (k, _) in enumerate(UNITS) if k == ADA]


def build(nc, io):
    with ExitStack() as ctx:
        def sb(name, shape, dt=F32):
            return ctx.enter_context(nc.sbuf_tensor(name, shape, dt))

        def sem(name):
            return ctx.enter_context(nc.semaphore(name))

        mod_d = nc.dram_tensor("mod_d", (9, 4, D), F32, kind="Internal").ap()
        dd_d = nc.dram_tensor("dd_d", (HEADS, 2, NS), F32, kind="Internal").ap()
        acs_d = nc.dram_tensor("acs_d", (HEADS, 2, CH), F32, kind="Internal").ap()
        bc_d = nc.dram_tensor("bc_d", (P, P), F32, kind="Internal").ap()

        BIG = sb("BIG", [P, 24, D])
        XBr = sb("XBr", [P, NCH * NT])
        XT = sb("XT", [P, 3, D])
        SZr = sb("SZr", [P, XC * NT])
        U = sb("U", [P, 10496])

        def cut(base, a, n, **kw):
            v = base[:, a:a + n]
            if kw:
                (k, m), = kw.items()
                v = v.rearrange(f"p ({k} x) -> p {k} x", **{k: m})
            return v

        W = [BIG[:, 8 * i:8 * i + 8, :] for i in range(3)]
        XB = XBr[:, :].rearrange("p (c t) -> p c t", t=NT)
        SZ = SZr[:, :].rearrange("p (c t) -> p c t", t=NT)
        xn = cut(XBr, 0, 3072, t=3)
        CR = XBr[0:9, 3072:4096]
        junk = cut(XBr, 4096, 1024)
        AB = cut(SZr, 0, 1536, u=6)
        MS = cut(SZr, 1536, 1536, u=6)
        dtt = [SZr[0:HEADS, 3072 + i * NT:3072 + (i + 1) * NT] for i in range(4)]
        h1T = cut(U, 0, KT * NT, k=KT)
        RW = cut(U, 2112, 4 * SEQR, k=4)
        HT = cut(U, 3276, NCH * 24, c=NCH)
        CV = cut(U, 4044, 3 * SEQC, k=3)
        HI = U[0:24, 4908:4908 + CDIM]
        BCb = [U[:, 7980:7980 + 2048].rearrange("p (j n) -> p j n", n=P),
               U[:, 2112:2112 + 2048].rearrange("p (j n) -> p j n", n=P)]
        TT = sb("TT", [P, 4, 11, 8])
        ident = sb("ident", [P, P])
        utri = sb("utri", [P, P])
        ones = sb("ones", [P, P])
        PR1 = XBr[:, 5120:5248]
        PR2 = XBr[0:56, 5248:5376]
        zeros = XBr[0:2, 7000:8024]
        bcs = U[:, 10028:10156]
        bcT = U[:, 10156:10284]
        acsT = dtt[2][:, 0:2 * CH].rearrange("p (c l) -> p c l", c=2)
        cw = sb("cw", [P, P])
        pv = sb("pv", [P, 56])
        m1 = sb("m1", [P, 2, KT, 9])
        scT = sb("scT", [P, KT, 32])
        WDT = sb("WDT", [P, KT, 32])
        DDc = WDT[:, :, :].rearrange("p k h -> p (k h)").rearrange("p (c q s) -> p c q s", c=XC, q=2)
        dd = sb("dd", [HEADS, 2, NS])
        dtok = sb("dtok", [P, 4, 32])
        acst = sb("acst", [P, 2, 32])
        dcy = sb("dcy", [P, 2, 32])
        dec1 = sb("dec1", [P, 32])
        Dbc = sb("Dbc", [P, 32])
        Dcol = sb("Dcol", [P, XC])
        st = sb("st", [P, 16])
        hsc = sb("hsc", [HEADS, 4])
        npi = sb("npi", [1, 1], I32)
        xdtS = sb("xdtS", [P, XC, NS])
        yS = sb("yS", [P, XC, NS])

        BF = BIG[:, :, :].rearrange("p a b -> p (a b)")
        bcA = [BF[:, o:o + 4096].rearrange("p (h l) -> p h l", h=HEADS) for o in (0, 8192)]
        prevT = BF[:, 4096:6144]
        LT = [bcA[0][:, HPG * i:HPG * i + HPG, :] for i in range(GROUPS)]
        Btok = BF[:, 7168:8192]
        xdt = BF[:, 12288:14336]
        xdec = BF[:, 14336:16384]
        SR = [v.rearrange("p (c n) -> p c n", n=P) for v in
              (U[:, 4908:5932], U[:, 5932:6956], U[:, 6956:7980], BF[:, 4096:5120], BF[:, 5120:6144])]
        TLs = U[0:88, 4160:4672].rearrange("p (u f) -> p u f", u=4)
        CTs = [U[:, 9248 + 512 * i:9760 + 512 * i].rearrange("p (r l) -> p r l", r=4) for i in range(2)]
        CBm = [BF[:, 6144 + 128 * i:6272 + 128 * i] for i in range(2)]
        sq = [U[:, 8192 + 528 * i:8720 + 528 * i].rearrange("p (r l) -> p r l", r=2) for i in range(2)]
        rs = [U[:, 9248 + 264 * i:9512 + 264 * i] for i in range(2)]
        MB = U[:, 0:8192].rearrange("p (q u f) -> p q u f", q=2, u=4)
        wo1 = XBr[:, 0:8192].rearrange("p (k f) -> p k f", k=8)
        h2 = cut(XBr, 0, 3072, t=3)
        acc = cut(XBr, 3072, 3072, t=3)
        BR = XBr[:, 6144:8192]
        h2T = SZr[:, 0:2112].rearrange("p (k t) -> p k t", k=KT)
        BD = SZr[0:NE, 2112:3136]
        combT = SZr[0:NE, 3136:3136 + NT]
        n2b = SZr[:, 3136:4160]
        hg, gg, uu, sg, aa = [SZr[:, 512 * i:512 * i + 512] for i in range(5)]
        osb = SZr[:, 2560:3584]
        hgT = SZr[:, 3584:4096].rearrange("p (c s) -> p c s", c=4)
        actT = U[:, 0:512].rearrange("p (c s) -> p c s", c=4)
        bsel = [U[:, 512:576], U[:, 576:640]]
        G = [U[:, 2048 + 192 * i:2240 + 192 * i].rearrange("p (t j) -> p t j", t=3) for i in range(2)]
        o = 8192

        def small(n):
            nonlocal o
            o += n
            return U[:, o - n:o]
        Gw = small(384).rearrange("p (t d j) -> p t d j", t=3, d=2)
        SwT = small(3 * P)
        eye = SZr[:, 4096:4096 + NE + 1]
        posx = small(3 * (MAXPASS * NE + 1)).rearrange("p (i t) -> p i t", t=3)
        comb = small(96).rearrange("p (e t) -> p e t", t=3)
        mask = small(96).rearrange("p (t e) -> p t e", t=3)
        RWt = small(KT * NE).rearrange("p (k e) -> p k e", k=KT)
        lg = small(NE)
        rb = small(NE)
        oh = small(4 * NE).rearrange("p (k e) -> p k e", k=4)
        pw = small(4 * NE).rearrange("p (k e) -> p k e", k=4)
        m8 = small(8)
        ixf = small(8)
        ex = small(8)
        assert o <= 10496
        ix = sb("ix", [P, 8], U32)
        iota = sb("iota", [P, 64])
        thr = sb("thr", [1, 4])
        cnt = sb("cnt", [1, 8])

        PSB = [ctx.enter_context(nc.psum_tensor(f"PS{i}", [P, 512], F32)) for i in range(6)]
        PGU = ctx.enter_context(nc.psum_tensor("PGU", [P, 2, 512], F32))
        PS = [PGU[:, 0, :], PGU[:, 1, :]] + [b[:, :] for b in PSB]

        names = """ld_x ld_c ld_par ld_hist ld_wdt ld_ab ld_hs ld_D ld_rt ld_n2 ld_bd ld_br ld_fn
        consts_pool consts_dve silu_c cT_ps scT_ok par_ps par_ok hist_ps hist_ok ada_ps ms_ok xn_ok xnT_ps h1_act
        h1_dve m1_ps m1_ok dt_ps chunk_ps chunk_evac conv_done silu_done dtTok_ps dtok_ok acs_ps acs_ok
        bcs_ok bcs_ps bcT_ok dt_t dt_e dt_u dt_l dt_ok dec_ok dd_ok s_dd s_ddl s_acs s_bcd tl_ps tl_ok s_tl s_mod s_mb
        s_scaled item_done samp_ok
        xtok_ps xtok_ok btok_ok cb_ps lt_ok exp_ok mt_ok ce_ok cts_ok y_ps y_ok st_ps st_ok dcy_ok xdec_ok lastx
        hf_ps hf_ok s_hf sq_ok gn_ps gn_ok gn_rt ss_ok rt3_ok wo_ps xm_ok h2_ok h2T_ps h2T_ok lg_ps rt_m rt_e rt_p pos_ps np_ok cmb_ps cmb_ok
        ai_ps acc_ok moe_ready
        gu_used gath_ps sc_ps actT_ps hgT_ps swT_ps dn_used d_bs d_guf d_G d_g d_act d_add d_t d_gw a_actT
        a_sig a_hg a_hgT a_swT a_o y_done s_out s_y ch_dve ch_act ch_pool""".split()
        S = {n: sem(n) for n in names}
        ld_w = [sem(f"ld_w{i}") for i in range(3)]
        ld_wo = [sem(f"ld_wo{i}") for i in range(2)]
        ld_bc = [sem(f"ld_bc{i}") for i in range(2)]
        ld_s = [sem(f"ld_s{i}") for i in range(NSLOT)]
        st_s = [sem(f"st_s{i}") for i in range(NSLOT)]
        ld_bcb = [sem(f"ld_bcb{i}") for i in range(2)]
        gu_ld = [sem(f"gu_ld{i}") for i in range(4)]
        dn_ld = [sem(f"dn_ld{i}") for i in range(2)]

        gu_w = io["moe_w_gate_up"]
        dn_w = io["moe_w_down"]
        state_rows = io["state_ssm"].rearrange("s h p n -> s (h p) n")
        state_out = io["new_ssm_sample"].rearrange("s h p n -> s (h p) n")

        def gu_src(e, j):
            return gu_w[0, e, 256 * j:256 * j + 256, :] if isinstance(e, int) else \
                gu_w[0, bass.ds(e, 1), 256 * j:256 * j + 256, :].rearrange("o r f -> (o r) f")

        def dn_src(e, j):
            return dn_w[0, e, 512 * j:512 * j + 512, :] if isinstance(e, int) else \
                dn_w[0, bass.ds(e, 1), 512 * j:512 * j + 512, :].rearrange("o r f -> (o r) f")

        def used(eng, u):
            if UNITS[u][0] == ADA:
                eng.wait_ge(S["ada_ps"], UNIT_A.index(u) + 1)
            else:
                eng.wait_ge(S["chunk_ps"], max(n for n, c in enumerate(CHUNKS) if c[0] == u) + 1)

        block = ctx.enter_context(nc.Block())

        @block.sync
        def _(sp):
            def wait(name, v):
                sp.wait_ge(S[name], v)

            def small_loads():
                sp.dma_start(PR1, io["ssd_conv_w"].rearrange("k (c f) -> (k c) f", f=P)).then_inc(S["ld_par"], 16)
                sp.dma_start(PR2[0:32, :], io["ssd_conv_b"].rearrange("(c f) -> c f", f=P)).then_inc(S["ld_par"], 16)
                sp.dma_start(PR2[32:40, :], io["norm1_w"][0].rearrange("(c f) -> c f", f=P)).then_inc(S["ld_par"], 16)
                sp.dma_start(PR2[40:56, :], io["ssd_norm_w"].rearrange("(c f) -> c f", f=P)).then_inc(S["ld_par"], 16)
                sp.dma_start(HI, io["state_ssm_conv"].rearrange("s k f -> (s k) f")).then_inc(S["ld_hist"], 16)
                sp.dma_start(WDT[:], io["ssd_w_in"][:, INNER + CDIM:].rearrange("(k p) h -> p k h", p=P))\
                   .then_inc(S["ld_wdt"], 16)
                with nc.allow_non_contiguous_dma(reason="one value per head"):
                    sp.dma_start(hsc[:, 0:1], io["ssd_dt_bias"].rearrange("(h o) -> h o", o=1)).then_inc(S["ld_hs"], 16)
                    sp.dma_start(hsc[:, 1:2], io["ssd_A_log"].rearrange("(h o) -> h o", o=1)).then_inc(S["ld_hs"], 16)
                sp.dma_start(Dbc[:], io["ssd_D"].rearrange("(o h) -> o h", o=1).to_broadcast([P, HEADS]))\
                   .then_inc(S["ld_D"], 16)

            sp.dma_start(XBr[0:1, 3072:4096], io["c_prompt"]).then_inc(S["ld_c"], 16)
            sp.dma_start(XBr[1:9, 3072:4096], io["c_sample"]).then_inc(S["ld_c"], 16)
            sp.dma_start(XT[:, 0:2, :], io["x_prompt"][0].rearrange("(t p) f -> p t f", p=P)).then_inc(S["ld_x"], 16)
            sp.dma_start(XT[0:NS, 2, :], io["x_sample"][:, 0, :]).then_inc(S["ld_x"], 16)
            wait("consts_dve", 1)
            for q in range(4):
                src = bass.AP(tensor=io["ada_b"].tensor, offset=io["ada_b"].offset + 256 * q,
                              ap=[[0, 9], [D, 6], [1, 256]])
                sp.dma_start(AB[32 * q:32 * q + 9, :, :], src).then_inc(S["ld_ab"], 16)

            def load_bcb(s):
                if s == 0:
                    wait("s_bcd", 16)
                if s == 1:
                    wait("silu_done", NCONV)
                if s >= 2:
                    wait("item_done", 2 * (s - 1))
                src = bass.AP(tensor=bc_d.tensor, offset=s * 2048, ap=[[0, P], [1, 2048]])
                sp.dma_start(BCb[s % 2].rearrange("p j n -> p (j n)"), src).then_inc(ld_bcb[s % 2], 16)

            def load_state(j):
                s, half = divmod(j, 2)
                if j >= NSLOT:
                    sp.wait_ge(st_s[j % NSLOT], 16 * (j // NSLOT))
                sp.dma_start(SR[j % NSLOT], state_rows[s, D * half:D * half + D, :].rearrange("(c p) n -> p c n", p=P))\
                  .then_inc(ld_s[j % NSLOT], 16)

            for u, (kind, col) in enumerate(UNITS):
                if u == 1:
                    small_loads()
                if u == 8:
                    wait("hist_ps", 1)
                    for j in range(3):
                        load_state(j)
                if u >= 3:
                    used(sp, u - 3)
                if kind == ADA:
                    src = io["ada_w"][0, :, col * D:(col + 1) * D]
                else:
                    src = io["ssd_w_in"][:, col:col + D]
                sp.dma_start(W[u % 3], src.rearrange("(k p) f -> p k f", p=P)).then_inc(ld_w[u % 3], 16)
            load_bcb(0)
            for j in range(3, 16):
                if j == 5:
                    load_bcb(1)
                if j == 3:
                    used(sp, 9)
                if j >= 6 and j % 2 == 0:
                    load_bcb(j // 2 - 1)
                load_state(j)
            load_bcb(7)
            wait("tl_ok", 1)
            cp = io["new_ssm_conv_prompt"][0]
            cs = io["new_ssm_conv_sample"]
            for t in range(3):
                sp.dma_start(cp[t, :].rearrange("(u c f) -> c u f", u=4, c=8),
                             TLs[8 * t:8 * t + 8, :, :]).then_inc(S["s_tl"], 16)
            for s in range(NS):
                sp.dma_start(cs[s, 2, :].rearrange("(u c f) -> c u f", u=4, c=8),
                             TLs[24 + 8 * s:32 + 8 * s, :, :]).then_inc(S["s_tl"], 16)
            used(sp, len(UNITS) - 1)
            wait("s_mod", 64)
            wait("item_done", 16)
            wait("s_tl", 11 * 16)
            for r in range(3):
                sp.wait_ge(st_s[r], 16 * len(range(r, 16, NSLOT)))
            src = bass.AP(tensor=mod_d.tensor, offset=0, ap=[[0, P], [1, 4 * D]])
            sp.dma_start(MB[:, 0, :, :].rearrange("p u f -> p (u f)"), src).then_inc(S["s_mb"], 16)
            sp.dma_start(MB[0:NS, 1, :, :], mod_d[1:9, :, :]).then_inc(S["s_mb"], 16)
            sp.dma_start(W[2], io["ssd_w_out"][0:D, :].rearrange("(k p) f -> p k f", p=P)).then_inc(ld_wo[0], 16)
            wait("y_ok", 16)
            wait("hf_ok", 4)
            wait("s_hf", 16)
            sp.dma_start(wo1, io["ssd_w_out"][D:2 * D, :].rearrange("(k p) f -> p k f", p=P)).then_inc(ld_wo[1], 16)
            for j in range(4):
                sp.dma_start(BIG[:, 4 * j:4 * j + 4, :].rearrange("p (k h) f -> p k (h f)", k=2),
                             gu_src(0, j).rearrange("(k p) f -> p k f", p=P)).then_inc(gu_ld[j], 16)
            wait("wo_ps", 1)
            for j in range(2):
                sp.dma_start(BIG[:, 16 + 4 * j:20 + 4 * j, :],
                             dn_src(0, j).rearrange("(k p) f -> p k f", p=P)).then_inc(dn_ld[j], 16)
            wait("np_ok", 1)
            npass = sp.value_load(npi[0:1, 0:1], min_val=1, max_val=MAXPASS)

            def load_expert(e, it):
                for j in range(4):
                    sp.wait_ge(S["gu_used"], it * 4 + (j - 3))
                    sp.dma_start(BIG[:, 4 * j:4 * j + 4, :].rearrange("p (k h) f -> p k (h f)", k=2),
                                 gu_src(e, j).rearrange("(k p) f -> p k f", p=P)).then_inc(gu_ld[j], 16)
                for j in range(2):
                    sp.wait_ge(S["dn_used"], it * 2 + (j - 1))
                    sp.dma_start(BIG[:, 16 + 4 * j:20 + 4 * j, :],
                                 dn_src(e, j).rearrange("(k p) f -> p k f", p=P)).then_inc(dn_ld[j], 16)

            with sp.Fori(0, npass) as ps:
                with sp.Fori(1, NE) as e:
                    load_expert(e, ps * NE + e)
                with sp.If(ps + 1 < npass):
                    load_expert(0, ps * NE + NE)
            wait("y_done", 3)
            yo = io["y_prompt"][0].rearrange("(t p) f -> p t f", p=P)
            sp.dma_start(yo, XT[:, 0:2, :]).then_inc(S["s_y"], 16)
            sp.dma_start(io["y_sample"][:, 0, :], XT[0:NS, 2, :]).then_inc(S["s_y"], 16)
            wait("s_y", 32)

        @block.gpsimd
        def _(pool):
            g = nc.gpsimd

            def wait(name, v):
                pool.wait_ge(S[name], v)

            g.memset(zeros, 0.0).then_inc(S["ch_pool"], 1)
            g.memset(ident[:], 0.0)
            g.memset(utri[:], 1.0)
            g.memset(ones[:], 1.0)
            g.memset(TT[:], 0.0)
            g.iota(iota[:], [[1, 64]], base=0, channel_multiplier=0,
                   allow_small_or_imprecise_dtypes=True)
            g.iota(thr[:], [[CAP, 4]], base=CAP, channel_multiplier=0,
                   allow_small_or_imprecise_dtypes=True).then_inc(S["ch_pool"], 1)
            wait("ch_pool", 2)
            g.affine_select(out=ident[:], in_=ident[:], pattern=[[-1, P]], compare_op=ALU.not_equal, fill=1.0,
                            base=0, channel_multiplier=1)
            g.affine_select(out=utri[:], in_=utri[:], pattern=[[1, P]], compare_op=ALU.is_ge, fill=0.0,
                            base=0, channel_multiplier=-1).then_inc(S["consts_pool"], 1)
            g.dma_start(io["new_sconv_prompt"][0], zeros).then_inc(S["s_out"], 16)
            g.dma_start(io["new_sconv_sample"].rearrange("s k f -> (s k) f"),
                        io["state_sconv"].rearrange("s k f -> (s k) f")).then_inc(S["s_out"], 16)
            g.dma_start(io["new_ssm_conv_sample"][:, 0:2, :], io["state_ssm_conv"][:, 1:3, :]).then_inc(S["s_out"], 16)
            wait("dd_ok", 1)
            g.dma_start(dd_d, dd[:]).then_inc(S["s_dd"], 16)
            wait("s_dd", 16)
            for half in range(2):
                src = bass.AP(tensor=dd_d.tensor, offset=half * 16, ap=[[0, 64], [32, 16], [1, 16]])
                g.dma_start(WDT[64 * half:64 * half + 64, :, :].rearrange("p k (a b) -> p (k a) b", a=2), src)\
                 .then_inc(S["s_ddl"], 16)
            wait("acs_ok", 1)
            g.dma_start(acs_d, acsT).then_inc(S["s_acs"], 16)
            wait("bcT_ok", 1)
            g.dma_start(bc_d, bcT).then_inc(S["s_bcd"], 16)
            wait("s_acs", 16)

            def store_state(j):
                s, half = divmod(j, 2)
                wait("item_done", j + 1)
                g.dma_start(state_out[s, D * half:D * half + D, :].rearrange("(c p) n -> p c n", p=P),
                            SR[j % NSLOT]).then_inc(st_s[j % NSLOT], 16)

            def last_sum(c):
                pool.wait_ge(ld_bc[c], 16)
                g.tensor_tensor(dcy[:, c, :], bcA[c][:, :, CH - 1], acst[:, c, :], ALU.subtract)\
                 .then_inc(S["lastx"], 1)

            def differences(q):
                c, gr = divmod(q, GROUPS)
                if q == 0:
                    wait("lastx", 1)
                if c == 1:
                    wait("y_ps", gr + 1)
                for r in range(HPG):
                    h = gr * HPG + r
                    i = g.tensor_scalar(LT[gr][:, r, :], bcA[c][:, h, :], acst[:, c, h:h + 1], 0.0,
                                        ALU.subtract, ALU.min)
                i.then_inc(S["lt_ok"], 1)

            def decayed(c):
                wait("dcy_ok", c + 1)
                if c == 1:
                    wait("st_ps", GROUPS)
                for b in range(4):
                    wait("xtok_ok", 4 * c + b + 1)
                    g.tensor_tensor(xdec[:, 512 * b:512 * b + 512].rearrange("p (h d) -> p h d", d=HD),
                                    xdt[:, 512 * b:512 * b + 512].rearrange("p (h d) -> p h d", d=HD),
                                    dcy[:, c, 8 * b:8 * b + 8].unsqueeze(2).to_broadcast([P, 8, HD]), ALU.mult)\
                     .then_inc(S["xdec_ok"], 1)

            wait("ms_ok", 6)
            for q in range(4):
                g.dma_start(mod_d[:, :, 256 * q:256 * q + 256], MS[32 * q:32 * q + 9, 2:6, :])\
                 .then_inc(S["s_mod"], 16)

            def load_acs(c):
                used(pool, 9 + c)
                src = bass.AP(tensor=acs_d.tensor, offset=c * CH, ap=[[0, P], [2 * CH, HEADS], [1, CH]])
                g.dma_start(bcA[c], src).then_inc(ld_bc[c], 16)

            load_acs(0)
            for j in range(16):
                store_state(j)
                if j == 3:
                    last_sum(0)
                if 3 <= j < 3 + GROUPS:
                    differences(j - 3)
                if j == 14:
                    load_acs(1)
            last_sum(1)
            decayed(0)
            for q in range(GROUPS, 16):
                differences(q)
                if q == GROUPS + 3:
                    decayed(1)
            for r in range(NSLOT):
                pool.wait_ge(st_s[r], 16 * len(range(r, 16, NSLOT)))
            wait("gn_ok", GROUPS)
            g.dma_start(RWt[:, :, :], io["router_w"][0].rearrange("(k p) e -> p k e", p=P)).then_inc(S["ld_rt"], 16)
            g.dma_start(rb, io["router_b"][0:1, :].to_broadcast([P, NE])).then_inc(S["ld_rt"], 16)
            wait("wo_ps", 2)
            g.dma_start(n2b, io["norm2_w"][0:1, :].to_broadcast([P, D])).then_inc(S["ld_n2"], 16)
            g.dma_start(BD, io["moe_b_down"][0]).then_inc(S["ld_bd"], 16)
            g.memset(BR, 0.0).then_inc(S["ch_pool"], 1)
            wait("ch_pool", 3)
            g.dma_start(BR[0:NE, :], io["moe_b_gate_up"][0]).then_inc(S["ld_br"], 16)
            wait("h2_ok", 3)
            g.dma_start(MB[:, 0, 1, :], io["final_norm_w"].rearrange("(o f) -> o f", o=1).to_broadcast([P, D]))\
             .then_inc(S["ld_fn"], 16)
            wait("s_out", 48)

        @block.scalar
        def _(act):
            a = nc.scalar

            def wait(name, v):
                act.wait_ge(S[name], v)

            def link(ins, k=[0]):
                k[0] += 1
                ins.then_inc(S["ch_act"], 1)
                act.wait_ge(S["ch_act"], k[0])

            wait("ld_c", 32)
            a.activation(CR, CR, ACT.Silu).then_inc(S["silu_c"], 1)

            def root(at, n):
                wait("ss_ok", n)
                a.activation(st[:, at:at + 3], st[:, at:at + 3], ACT.Sqrt, bias=st[:, 15:16], scale=1.0 / D)\
                 .then_inc(S["rt3_ok"], 1)

            root(0, 1)
            wait("par_ps", 1)
            a.copy(cw[:], PS[7][:, 0:128])
            a.copy(pv[:], PS[7][:, 128:184]).then_inc(S["par_ok"], 1)
            wait("hist_ps", 1)
            a.copy(HT[:, 0:16, :].rearrange("p c k -> p (c k)"), PS[6][:, 0:384])
            a.copy(HT[:, 16:32, :].rearrange("p c k -> p (c k)"), PS[7][:, 0:384]).then_inc(S["hist_ok"], 1)
            wait("xnT_ps", 1)
            wait("m1_ok", 1)
            for k in range(KT):
                i = a.activation(h1T[:, k, 0:NP], PS[k // 2][:, 256 * (k % 2):256 * (k % 2) + 256], ACT.Identity,
                                 bias=m1[:, 0, k, 0:1], scale=m1[:, 1, k, 0:1])
            i.then_inc(S["h1_act"], 1)
            wait("ld_hs", 32)
            a.activation(hsc[:, 2:3], hsc[:, 1:2], ACT.Exp)
            wait("dt_t", 1)
            a.activation(dtt[1], dtt[1], ACT.Exp).then_inc(S["dt_e"], 1)
            wait("dt_u", 1)
            a.activation(dtt[3], dtt[2], ACT.Ln).then_inc(S["dt_l"], 1)
            wait("dt_ok", 1)
            a.activation(dd[:, 1, :], dtt[1][:, NP:NT], ACT.Exp).then_inc(S["dec_ok"], 1)

            def conv_silu(n):
                c = CHUNKS[n][3]
                wait("conv_done", n + 1)
                a.activation(XB[:, c, 0:NP], CV[:, n % 3, 0:NP], ACT.Silu, bias=pv[:, c:c + 1])
                a.activation(XB[:, c, NP:NT], CV[:, n % 3, 259:SEQC:4], ACT.Silu, bias=pv[:, c:c + 1])\
                 .then_inc(S["silu_done"], 1)

            def scale_states(j):
                s, half = divmod(j, 2)
                act.wait_ge(ld_s[j % NSLOT], 16 * (j // NSLOT + 1))
                if j == 0:
                    wait("s_ddl", 32)
                for c in range(8):
                    i = a.mul(SR[j % NSLOT][:, c, :], SR[j % NSLOT][:, c, :], DDc[:, 8 * half + c, 1, s:s + 1])
                i.then_inc(S["s_scaled"], 1)

            for n, (u, j, kind, c) in enumerate(CHUNKS):
                wait("chunk_ps", n + 1)
                ps = PS[n % 4][:, 0:NT]
                if kind == "z":
                    if n == NCONV:
                        wait("s_acs", 16)
                        wait("dtTok_ps", 1)
                    if n == NCONV + 4:
                        wait("s_mod", 64)
                    a.activation(SZ[:, c, :], ps, ACT.Silu).then_inc(S["chunk_evac"], 1)
                    if n > NCONV:
                        scale_states(n - NCONV - 1)
                else:
                    if n == 0:
                        wait("consts_dve", 1)
                        wait("s_out", 48)
                    if n >= 4:
                        wait("conv_done", n - 3)
                    a.copy(RW[:, n % 4, 3:3 + NP], ps[:, 0:NP])
                    a.copy(RW[:, n % 4, 262:SEQR:4], ps[:, NP:NT]).then_inc(S["chunk_evac"], 1)
                    if n >= 1:
                        conv_silu(n - 1)
                    if n == NCONV - 1:
                        conv_silu(n)
            scale_states(15)

            def exp_differences(q):
                wait("lt_ok", q + 1)
                a.activation(LT[q % GROUPS], LT[q % GROUPS], ACT.Exp).then_inc(S["exp_ok"], 1)

            def exp_sums(gr):
                if gr >= 2:
                    wait("y_ps", GROUPS + gr - 1)
                a.activation(CTs[gr % 2], bcA[1][:, HPG * gr:HPG * gr + HPG, :], ACT.Exp).then_inc(S["ce_ok"], 1)

            def copy_b(c):
                wait("xtok_ps", 6 * c + 6)
                if c == 1:
                    wait("st_ps", GROUPS)
                a.copy(Btok[:, 0:512], PS[0])
                a.copy(Btok[:, 512:1024], PS[1]).then_inc(S["btok_ok"], 1)

            for c in range(2):
                wait("lastx", c + 1)
                a.activation(dcy[:, c, :], dcy[:, c, :], ACT.Exp).then_inc(S["dcy_ok"], 1)
                if c == 1:
                    link(a.activation(dec1[:], bcA[1][:, :, CH - 1], ACT.Exp))
                for gr in range(GROUPS):
                    if c == 1:
                        exp_sums(gr)
                    exp_differences(c * GROUPS + gr)
                    if gr == 1:
                        copy_b(c)
            for b in range(4):
                wait("hf_ps", b + 1)
                a.copy(xdt[:, 512 * b:512 * b + 512], PS[b % 2]).then_inc(S["hf_ok"], 1)
            act.wait_ge(S["hf_ok"], 4)
            act.dma_start(io["new_ssm_prompt"][0].rearrange("h p n -> (h p) n").rearrange("(c q) n -> q c n", q=P),
                          xdt.rearrange("p (c n) -> p c n", n=P)).then_inc(S["s_hf"], 16)
            def gn_root(gr):
                wait("gn_ps", gr + 1)
                if gr >= 2:
                    wait("gn_ok", gr - 1)
                a.activation(rs[gr % 2], PS[2 + gr % 2][:, 0:NT], ACT.Sqrt, bias=st[:, 15:16], scale=1.0 / 256)\
                 .then_inc(S["gn_rt"], 1)

            for gr in range(GROUPS):
                if gr == 0:
                    wait("y_ok", 16)
                    wait("samp_ok", 1)
                a.activation(sq[gr % 2], SZ[:, 2 * gr:2 * gr + 2, :], ACT.Square).then_inc(S["sq_ok"], 1)
                if gr >= 1:
                    gn_root(gr - 1)
            gn_root(GROUPS - 1)
            root(4, 2)
            for t in range(3):
                wait("h2T_ps", t + 1)
                R = ROWS[t]
                for b in range(2):
                    i = a.copy(h2T[:, 4 * b:4 * b + 4, 128 * t:128 * t + R],
                               PS[2 * (t % 2) + b][:, 0:512].rearrange("p (k r) -> p k r", k=4)[:, :, 0:R])
                i.then_inc(S["h2T_ok"], 1)
            for t in range(3):
                R = ROWS[t]
                wait("rt_m", t + 1)
                a.activation(ex[0:R, 0:4], m8[0:R, 0:4], ACT.Exp, bias=m8[0:R, 7:8]).then_inc(S["rt_e"], 1)
            wait("moe_ready", 1)
            wait("np_ok", 1)
            npass = act.value_load(npi[0:1, 0:1], min_val=1, max_val=MAXPASS)

            def expert_out(x):
                for nh in range(2):
                    i = a.copy(osb[64 * x:64 * x + 64, 512 * nh:512 * nh + 512], PS[5][64 * nh:64 * nh + 64, :])
                i.then_inc(S["a_o"], 1)

            wait("gath_ps", 1)
            a.copy(hg, PS[2]).then_inc(S["a_hg"], 1)
            wait("hgT_ps", 1)
            a.copy(hgT.rearrange("p c s -> p (c s)"), PS[3]).then_inc(S["a_hgT"], 1)
            with act.Fori(0, npass * (NE // 2)) as it:
                for x in range(2):
                    f = it * 2 + x
                    act.wait_ge(S["d_g"], f + 1)
                    a.activation(sg, gg, ACT.Sigmoid, scale=ALPHA).then_inc(S["a_sig"], 1)
                    act.wait_ge(S["gath_ps"], f + 2)
                    a.copy(hg, PS[2]).then_inc(S["a_hg"], 1)
                    if x == 1:
                        act.wait_ge(S["sc_ps"], it * 3 + 3)
                        expert_out(0)
                    act.wait_ge(S["actT_ps"], f + 1)
                    a.copy(actT.rearrange("p c s -> p (c s)"), PS[4]).then_inc(S["a_actT"], 1)
                    act.wait_ge(S["hgT_ps"], f + 2)
                    a.copy(hgT.rearrange("p c s -> p (c s)"), PS[3]).then_inc(S["a_hgT"], 1)
                    if x == 0:
                        act.wait_ge(S["dn_used"], it * 4 + 2)
                act.wait_ge(S["swT_ps"], it + 1)
                a.copy(SwT, PS[2][:, 0:3 * P]).then_inc(S["a_swT"], 1)
                act.wait_ge(S["dn_used"], it * 4 + 4)
                expert_out(1)
            root(8, 3)

        @block.tensor
        def _(pe):
            t_ = nc.tensor

            def wait(name, v):
                pe.wait_ge(S[name], v)

            def mm(out, lhsT, rhs, start=True, stop=True):
                return t_.matmul(out, lhsT, rhs, start=start, stop=stop)

            wait("consts_pool", 1)
            wait("silu_c", 1)
            for k in range(KT):
                i = t_.transpose(PS[6][:, 9 * k:9 * k + 9], CR[:, P * k:P * k + P], ident[0:9, 0:9])
            i.then_inc(S["cT_ps"], 1)
            wait("ld_par", 64)
            t_.transpose(PS[7][:, 0:128], PR1, ident[:])
            t_.transpose(PS[7][:, 128:184], PR2, ident[0:56, 0:56]).then_inc(S["par_ps"], 1)
            wait("ld_hist", 16)
            wait("scT_ok", 1)
            wait("par_ok", 1)
            for c in range(NCH):
                i = t_.transpose(PS[6 + c // 16][:, 24 * (c % 16):24 * (c % 16) + 24], HI[:, P * c:P * c + P],
                                 ident[0:24, 0:24])
            i.then_inc(S["hist_ps"], 1)

            def loaded(u):
                pe.wait_ge(ld_w[u % 3], 16 * (u // 3 + 1))

            def ada(u):
                a = UNIT_A.index(u)
                loaded(u)
                if a >= 2:
                    wait("ms_ok", a - 1)
                if a == 1:
                    wait("hist_ok", 1)
                for k in range(KT):
                    for q in range(4):
                        i = t_.matmul(PS[5 + 2 * (a % 2)][32 * q:32 * q + 32, 0:256], scT[:, k, :],
                                      W[u % 3][:, k, 256 * q:256 * q + 256], start=(k == 0), stop=(k == KT - 1),
                                      tile_position=(0, 32 * q))
                i.then_inc(S["ada_ps"], 1)

            wait("xn_ok", 3)
            for k in range(KT):
                for t in range(2):
                    t_.transpose(PS[k // 2][:, 256 * (k % 2) + 128 * t:256 * (k % 2) + 128 * t + 128],
                                 xn[:, t, P * k:P * k + P], ident[:])
            for k in range(KT):
                i = t_.transpose(PS[4][:, 8 * k:8 * k + 8], xn[0:NS, 2, P * k:P * k + P], ident[0:NS, 0:NS])
            i.then_inc(S["xnT_ps"], 1)
            ada(0)
            ada(1)
            wait("ms_ok", 2)
            wait("hist_ok", 1)
            for u in range(2):
                for hf in range(2):
                    i = t_.transpose(PS[6][:, 128 * (2 * u + hf):128 * (2 * u + hf) + 128],
                                     MS[:, u, 128 * hf:128 * hf + 128], ident[:])
            i.then_inc(S["m1_ps"], 1)
            wait("h1_act", 1)
            wait("h1_dve", 1)
            wait("ld_wdt", 16)
            for k in range(KT):
                i = mm(PS[7][0:32, 0:NT], WDT[:, k, :], h1T[:, k, :], k == 0, k == KT - 1)
            i.then_inc(S["dt_ps"], 1)
            n = 0
            for u, (kind, col) in enumerate(UNITS):
                if u < 2:
                    continue
                if u == 11:
                    wait("bcT_ok", 1)
                    wait("conv_done", NCONV)
                    for q in range(4):
                        i = t_.transpose(PS[4][0:88, P * q:P * q + P],
                                         TT[:, q, :, :].rearrange("p t c -> p (t c)"), ident[:])
                    i.then_inc(S["tl_ps"], 1)
                if kind == ADA:
                    ada(u)
                else:
                    loaded(u)
                    for _ in range(8):
                        j = CHUNKS[n][1]
                        if n >= 4:
                            wait("chunk_evac", n - 3)
                        for k in range(KT):
                            i = mm(PS[n % 4][:, 0:NT], W[u % 3][:, k, P * j:P * j + P], h1T[:, k, :],
                                   k == 0, k == KT - 1)
                        i.then_inc(S["chunk_ps"], 1)
                        n += 1
                if u == 2:
                    wait("dt_ok", 1)
                    for q in range(4):
                        i = t_.transpose(PS[4][:, 32 * q:32 * q + 32], dtt[q // 2][:, CH * (q % 2):CH * (q % 2) + CH],
                                         ident[0:32, 0:32])
                    i.then_inc(S["dtTok_ps"], 1)
                if u == 4:
                    wait("dtok_ok", 1)
                    for c in range(2):
                        mm(PS[6][:, 32 * c:32 * c + 32], utri[:], dtok[:, 2 + c, :])
                    for c in range(2):
                        i = mm(PS[6][0:32, 128 + 128 * c:256 + 128 * c], dtok[:, 2 + c, :], utri[:])
                    i.then_inc(S["acs_ps"], 1)
                if u == 6:
                    wait("bcs_ok", 1)
                    t_.transpose(PS[4][:, 0:128], bcs, ident[:]).then_inc(S["bcs_ps"], 1)

            def cb(q):
                c, gr = divmod(q, GROUPS)
                if q >= 2:
                    wait("mt_ok", q - 1)
                i = mm(PS[2 + q % 2][:, 0:CH], XB[:, XC + gr, CH * c:CH * c + CH],
                       XB[:, XC + GC + gr, CH * c:CH * c + CH])
                i.then_inc(S["cb_ps"], 1)

            for c in range(2):
                for b in range(6):
                    first = XC if b >= 4 else 0
                    if c == 0 and b < 2:
                        wait("chunk_evac", 48)
                    if c == 1 and b < 2:
                        wait("btok_ok", 1)
                    if 2 <= b:
                        wait("xtok_ok", 4 * c + b - 1)
                    for m in range(4):
                        i = t_.transpose(PS[b % 2][:, P * m:P * m + P],
                                         XB[:, first + 4 * (b - 4 if b >= 4 else b) + m, CH * c:CH * c + CH], ident[:])
                    i.then_inc(S["xtok_ps"], 1)
                if c == 0:
                    cb(0)
                for gr in range(GROUPS):
                    q = c * GROUPS + gr
                    if q + 1 < 16:
                        cb(q + 1)
                    if c == 1:
                        wait("st_ok", gr + 1)
                    wait("mt_ok", q + 1)
                    if c == 1:
                        wait("cts_ok", gr + 1)
                    if q >= 2:
                        wait("y_ok", q - 1)
                    if q == 0:
                        wait("tl_ok", 1)
                    for pair in range(2):
                        for r in (2 * pair, 2 * pair + 1):
                            h = HPG * gr + r
                            out = PS[4 + q % 2][64 * (r % 2):64 * (r % 2) + 64, CH * pair:CH * pair + CH]
                            i = mm(out, xdt[:, HD * h:HD * h + HD], LT[gr][:, r, :], True, c == 0)
                            if c == 1:
                                i = mm(out, prevT[:, HD * h:HD * h + HD], CTs[gr % 2][:, r, :], False, True)
                    i.then_inc(S["y_ps"], 1)
                    if gr == 0:
                        wait("btok_ok", c + 1)
                    if gr % 2 == 0:
                        wait("xdec_ok", 4 * c + gr // 2 + 1)
                    if q == 0:
                        wait("samp_ok", 1)
                    if q >= 2:
                        wait("st_ok", q - 1)
                    mm(PS[6 + q % 2][:, 0:256], Btok[:, P * gr:P * gr + P], xdec[:, 256 * gr:256 * gr + 256])\
                        .then_inc(S["st_ps"], 1)
            wait("st_ok", 16)
            for b in range(4):
                if b >= 2:
                    wait("hf_ok", b - 1)
                for m in range(4):
                    i = t_.transpose(PS[b % 2][:, P * m:P * m + P], prevT[:, 512 * b + P * m:512 * b + P * m + P],
                                     ident[:])
                i.then_inc(S["hf_ps"], 1)
            for gr in range(GROUPS):
                wait("sq_ok", gr + 1)
                if gr >= 2:
                    wait("gn_ok", gr - 1)
                for m in range(2):
                    i = mm(PS[2 + gr % 2][:, 0:NT], ones[:], sq[gr % 2][:, m, :], m == 0, m == 1)
                i.then_inc(S["gn_ps"], 1)
            wait("hf_ok", 4)
            wait("gn_ok", GROUPS)
            for half in range(2):
                pe.wait_ge(ld_wo[half], 16)
                w = W[2] if half == 0 else wo1
                for k8 in range(8):
                    k = 8 * half + k8
                    for t in range(2):
                        for nh in range(2):
                            mm(PS[2 * t + nh], SZ[:, k, CH * t:CH * t + CH], w[:, k8, 512 * nh:512 * nh + 512],
                               k == 0, k == XC - 1)
                for k8 in range(8):
                    k = 8 * half + k8
                    for q in range(4):
                        i = t_.matmul(PS[4][32 * q:32 * q + NS, 0:256], SZ[:, k, NP:NT], w[:, k8, 256 * q:256 * q + 256],
                                      start=(k == 0), stop=(k == XC - 1), tile_position=(0, 32 * q))
                i.then_inc(S["wo_ps"], 1)
            for t in range(3):
                R = ROWS[t]
                wait("h2_ok", t + 1)
                if t == 0:
                    wait("xm_ok", 3)
                if t == 2:
                    wait("h2T_ok", 1)
                for k in range(KT):
                    i = t_.transpose(PS[2 * (t % 2) + k // 4][:, P * (k % 4):P * (k % 4) + R],
                                     h2[0:R, t, P * k:P * k + P], ident[0:R, 0:R])
                i.then_inc(S["h2T_ps"], 1)
            wait("ld_rt", 32)
            for t in range(3):
                R = ROWS[t]
                wait("h2T_ok", t + 1)
                for k in range(KT):
                    i = mm(PS[4][0:R, 32 * t:32 * t + 32], h2T[:, k, CH * t:CH * t + R], RWt[:, k, :],
                           k == 0, k == KT - 1)
                i.then_inc(S["lg_ps"], 1)
            wait("rt_p", 3)
            for t in range(3):
                R = ROWS[t]
                for t2 in range(t):
                    mm(PS[5][0:R, 32 * t:32 * t + 32], ones[:, 0:R], mask[:, t2, :], t2 == 0, False)
                mm(PS[5][0:R, 32 * t:32 * t + 32], utri[0:R, 0:R], mask[0:R, t, :], t == 0, True)
            for t in range(3):
                R = ROWS[t]
                i = mm(PS[5][0:1, 96:128], ones[0:R, 0:1], mask[0:R, t, :], t == 0, t == 2)
            i.then_inc(S["pos_ps"], 1)
            for t in range(3):
                R = ROWS[t]
                i = t_.transpose(PS[6][0:NE, CH * t:CH * t + R], comb[0:R, :, t], ident[0:R, 0:R])
            i.then_inc(S["cmb_ps"], 1)
            wait("cmb_ok", 1)
            wait("ld_bd", 16)
            for t in range(3):
                R = ROWS[t]
                for nh in range(2):
                    i = mm(PS[2 * (t % 2) + nh][0:R, :], combT[:, CH * t:CH * t + R], BD[:, 512 * nh:512 * nh + 512])
                i.then_inc(S["ai_ps"], 1)
                if t == 1:
                    wait("acc_ok", 1)
            wait("moe_ready", 1)
            wait("np_ok", 1)
            npass = pe.value_load(npi[0:1, 0:1], min_val=1, max_val=MAXPASS)

            def gather(x):
                for t in range(3):
                    for hf in range(2):
                        i = mm(PS[2][64 * hf:64 * hf + 64, :], G[x][:, t, :], h2[:, t, 512 * hf:512 * hf + 512],
                               t == 0, t == 2)
                i.then_inc(S["gath_ps"], 1)

            def turn_rows():
                for c in range(4):
                    i = t_.transpose(PS[3][:, P * c:P * c + P], hg[:, P * c:P * c + P], ident[:])
                i.then_inc(S["hgT_ps"], 1)

            def scatter(it, t):
                pe.wait_ge(S["d_add"], it * 3 + (t + 1))
                for nh in range(2):
                    i = mm(PS[6 + nh], SwT[:, P * t:P * t + P], osb[:, 512 * nh:512 * nh + 512])
                i.then_inc(S["sc_ps"], 1)

            wait("d_G", 1)
            gather(0)
            wait("a_hg", 1)
            turn_rows()
            with pe.Fori(0, npass * (NE // 2)) as it:
                for x in range(2):
                    f = it * 2 + x
                    pe.wait_ge(S["d_bs"], f + 1)
                    pe.wait_ge(S["a_hgT"], f + 1)
                    pe.wait_ge(S["d_guf"], f + 1)
                    for n2 in range(2):
                        for hf in range(2):
                            mm(PGU[64 * hf:64 * hf + 64, n2, :], bsel[x],
                               BR[:, 1024 * hf + 512 * n2:1024 * hf + 512 * n2 + 512], True, False)
                    for j in range(4):
                        pe.wait_ge(gu_ld[j], f * 16 + 16)
                        for k in (2 * j, 2 * j + 1):
                            for n2 in range(2):
                                for hf in range(2):
                                    i = mm(PGU[64 * hf:64 * hf + 64, n2, :],
                                           hgT[:, k % 4, 64 * (k // 4):64 * (k // 4) + 64],
                                           BIG[:, 2 * k + hf, 512 * n2:512 * n2 + 512], False, k == KT - 1)
                        i.then_inc(S["gu_used"], 1)
                    pe.wait_ge(S["d_G"], f + 2)
                    pe.wait_ge(S["a_swT"], it + 1)
                    gather(1 - x)
                    if x == 0:
                        pe.wait_ge(S["a_o"], it * 2 + 1)
                        scatter(it, 0)
                    else:
                        scatter(it, 2)
                    pe.wait_ge(S["d_act"], f + 1)
                    for c in range(4):
                        i = t_.transpose(PS[4][:, P * c:P * c + P], aa[:, P * c:P * c + P], ident[:])
                    i.then_inc(S["actT_ps"], 1)
                    pe.wait_ge(S["a_hg"], f + 2)
                    turn_rows()
                    if x == 1:
                        pe.wait_ge(S["d_gw"], it * 2 + 2)
                        for t in range(3):
                            i = t_.transpose(PS[2][:, P * t:P * t + P], Gw[:, t, :, :].rearrange("p d j -> p (d j)"),
                                             ident[:])
                        i.then_inc(S["swT_ps"], 1)
                    pe.wait_ge(S["a_actT"], f + 1)
                    pe.wait_ge(S["a_o"], f + 1)
                    for j in range(2):
                        pe.wait_ge(dn_ld[j], f * 16 + 16)
                        for k in range(4 * j, 4 * j + 4):
                            for nh in range(2):
                                i = mm(PS[5][64 * nh:64 * nh + 64, :],
                                       actT[:, k % 4, 64 * (k // 4):64 * (k // 4) + 64],
                                       BIG[:, 16 + k, 512 * nh:512 * nh + 512], k == 0, k == KT - 1)
                        i.then_inc(S["dn_used"], 1)
                    if x == 0:
                        scatter(it, 1)
            pe.wait_ge(S["a_o"], npass * NE + 1)
            pe.wait_ge(S["a_swT"], npass * (NE // 2) + 1)
            for t in range(3):
                scatter(npass * (NE // 2), t)

        @block.vector
        def _(dve):
            v = nc.vector

            def wait(name, val):
                dve.wait_ge(S[name], val)

            k_ = [0]

            def link(ins):
                k_[0] += 1
                ins.then_inc(S["ch_dve"], 1)
                dve.wait_ge(S["ch_dve"], k_[0])

            v.memset(AB, 0.0)
            v.memset(scT[:], 0.0)
            v.memset(RW[:, :, 0:3], 0.0).then_inc(S["consts_dve"], 1)
            wait("ld_x", 32)

            def rstd(x, at, jk, n):
                for t in range(3):
                    R = ROWS[t]
                    i = v.tensor_tensor_reduce(jk[0:R, :], x[0:R, t, :], x[0:R, t, :], 1.0, 0.0, ALU.mult, ALU.add,
                                               st[0:R, at + t:at + t + 1])
                    if t < 2:
                        link(i)
                i.then_inc(S["ss_ok"], 1)
                wait("rt3_ok", n)
                link(v.reciprocal(st[:, at:at + 3], st[:, at:at + 3]))

            link(v.memset(st[:], 1.0))
            link(v.memset(st[:, 15:16], EPS))
            rstd(XT, 0, junk, 1)
            for t in range(3):
                R = ROWS[t]
                v.tensor_scalar(xn[0:R, t, :], XT[0:R, t, :], st[0:R, t:t + 1], None, ALU.mult).then_inc(S["xn_ok"], 1)
            wait("cT_ps", 1)
            v.tensor_copy(scT[:, :, 0:9], PS[6][:, 0:72].rearrange("p (k r) -> p k r", k=KT)).then_inc(S["scT_ok"], 1)

            def mod_rows(a):
                if a == 0:
                    wait("ld_ab", 64)
                wait("ada_ps", a + 1)
                v.tensor_tensor(MS[:, a, :], PS[5 + 2 * (a % 2)][:, 0:256], AB[:, a, :], ALU.add)\
                 .then_inc(S["ms_ok"], 1)

            mod_rows(0)
            mod_rows(1)
            wait("m1_ps", 1)
            wait("par_ok", 1)
            src = PS[6].rearrange("p (u hf q r) -> p u hf q r", u=2, hf=2, q=4)
            for u in range(2):
                for hf in range(2):
                    i = v.tensor_copy(m1[:, u, hf::2, :], src[:, u, hf, :, 0:9])
            link(i)
            link(v.tensor_scalar(m1[:, 1, :, :], m1[:, 1, :, :], 1.0, None, ALU.add))
            v.tensor_tensor(m1[:, 1, :, :], m1[:, 1, :, :], pv[:, 32:40].unsqueeze(2).to_broadcast([P, KT, 9]),
                            ALU.mult).then_inc(S["m1_ok"], 1)
            dve.wait_ge(S["m1_ok"], 1)
            wait("xnT_ps", 1)
            hs = h1T[:, :, NP:NT]
            link(v.tensor_tensor(hs, PS[4][:, 0:64].rearrange("p (k s) -> p k s", k=KT), m1[:, 1, :, 1:9], ALU.mult))
            v.tensor_tensor(hs, hs, m1[:, 0, :, 1:9], ALU.add).then_inc(S["h1_dve"], 1)
            wait("dt_ps", 1)
            wait("ld_hs", 32)
            link(v.tensor_scalar(dtt[0], PS[7][0:32, 0:NT], hsc[:, 0:1], None, ALU.add))
            v.scalar_tensor_tensor(dtt[1], dtt[0], -1.0, dtt[0], ALU.mult, ALU.min).then_inc(S["dt_t"], 1)
            wait("dt_e", 1)
            v.tensor_scalar(dtt[2], dtt[1], 1.0, None, ALU.add).then_inc(S["dt_u"], 1)
            wait("dt_l", 1)
            link(v.tensor_scalar(dtt[2], dtt[2], -1.0, None, ALU.add))
            tz = xn[0:32, 0, 0:NT]
            wait("xnT_ps", 1)
            link(v.tensor_scalar(tz, dtt[2], 0.0, None, ALU.is_equal))
            link(v.tensor_tensor(dtt[2], dtt[2], tz, ALU.add))
            link(v.reciprocal(dtt[2], dtt[2]))
            link(v.tensor_tensor(dtt[2], dtt[1], dtt[2], ALU.mult))
            link(v.tensor_tensor(dtt[3], dtt[3], dtt[2], ALU.mult))
            link(v.tensor_tensor(dtt[1], dtt[1], tz, ALU.mult))
            link(v.tensor_tensor(dtt[3], dtt[3], dtt[1], ALU.add))
            link(v.tensor_scalar(hsc[:, 3:4], hsc[:, 2:3], -1.0, None, ALU.mult))
            link(v.scalar_tensor_tensor(dtt[0], dtt[0], 0.0, dtt[3], ALU.max, ALU.add))
            v.tensor_scalar(dtt[1], dtt[0], hsc[:, 3:4], None, ALU.mult).then_inc(S["dt_ok"], 1)
            wait("dec_ok", 1)
            v.tensor_copy(dd[:, 0, :], dtt[0][:, NP:NT]).then_inc(S["dd_ok"], 1)
            wait("ld_D", 16)
            v.tensor_copy(Dcol[0:64, :], Dbc[0:64, 0::2])
            link(v.tensor_copy(Dcol[64:128, :], Dbc[64:128, 1::2]))
            wait("hist_ok", 1)

            for n in range(NCONV):
                u, j, _, c = CHUNKS[n]
                if n in (8, 16, 24):
                    mod_rows(1 + n // 8)
                raw = RW[:, n % 4, :]
                wait("chunk_evac", n + 1)
                link(v.tensor_copy(raw[:, 259:SEQR].rearrange("p (s k) -> p s k", k=4)[:, :, 0:3],
                                   HT[:, c, :].rearrange("p (s k) -> p s k", k=3)))
                if n >= 3:
                    wait("silu_done", n - 2)
                link(v.tensor_scalar(CV[:, n % 3, :], raw[:, 0:SEQC], cw[:, c:c + 1], None, ALU.mult))
                for k in range(1, CONV):
                    i = v.scalar_tensor_tensor(CV[:, n % 3, :], raw[:, k:k + SEQC], cw[:, NCH * k + c:NCH * k + c + 1],
                                               CV[:, n % 3, :], ALU.mult, ALU.add)
                    if k < CONV - 1:
                        link(i)
                    if k == 1:
                        v.tensor_copy(TT[:, c // 8, 0:3, c % 8], raw[:, NP:NP + 3])
                        v.tensor_copy(TT[:, c // 8, 3:11, c % 8], raw[:, 262:SEQR:4])
                i.then_inc(S["conv_done"], 1)
                if n == 9:
                    wait("dtTok_ps", 1)
                    v.tensor_copy(dtok[:].rearrange("p a b -> p (a b)"), PS[4][:, 0:128]).then_inc(S["dtok_ok"], 1)
                if n == 17:
                    wait("acs_ps", 1)
                    v.tensor_copy(acst[:].rearrange("p a b -> p (a b)"), PS[6][:, 0:64])
                    v.tensor_copy(acsT, PS[6][0:32, 128:384].rearrange("p (c l) -> p c l", c=2))\
                     .then_inc(S["acs_ok"], 1)
                    wait("silu_done", 16)
                    dve.wait_ge(S["acs_ok"], 1)
                    v.tensor_copy(bcs.rearrange("p (s j) -> p s j", j=16),
                                  XB[:, XC:NCH, NP:NT].rearrange("p j s -> p s j")).then_inc(S["bcs_ok"], 1)
                if n == 25:
                    wait("bcs_ps", 1)
                    v.tensor_copy(bcT, PS[4][:, 0:128]).then_inc(S["bcT_ok"], 1)
            mod_rows(5)
            wait("silu_done", NCONV)
            wait("s_ddl", 32)
            link(v.tensor_tensor(xdtS[:], XB[:, 0:XC, NP:NT], DDc[:, :, 0, :], ALU.mult))
            wait("m1_ok", 1)
            junkp = [PS[6], PS[7]]
            for j in range(16):
                s, half = divmod(j, 2)
                if half == 0:
                    dve.wait_ge(ld_bcb[s % 2], 16 * (s // 2 + 1))
                wait("s_scaled", j + 1)
                for c in range(8):
                    cc = 8 * half + c
                    i = v.scalar_tensor_tensor(SR[j % NSLOT][:, c, :], BCb[s % 2][:, cc // 2, :], xdtS[:, cc, s:s + 1],
                                               SR[j % NSLOT][:, c, :], ALU.mult, ALU.add)
                link(i)
                for c in range(8):
                    cc = 8 * half + c
                    i = v.tensor_tensor_reduce(junkp[c // 4][:, P * (c % 4):P * (c % 4) + P], SR[j % NSLOT][:, c, :],
                                               BCb[s % 2][:, 8 + cc // 2, :], 1.0, 0.0, ALU.mult, ALU.add,
                                               yS[:, cc, s:s + 1])
                i.then_inc(S["item_done"], 1)
                dve.wait_ge(S["item_done"], j + 1)
                if j == 10:
                    wait("tl_ps", 1)
                    v.tensor_copy(TLs.rearrange("p u f -> p (u f)"), PS[4][0:88, :]).then_inc(S["tl_ok"], 1)
            link(v.tensor_tensor(xdtS[:], XB[:, 0:XC, NP:NT], Dcol[:].unsqueeze(2).to_broadcast([P, XC, NS]), ALU.mult))
            link(v.tensor_tensor(yS[:], yS[:], xdtS[:], ALU.add))
            wait("chunk_evac", 48)
            v.tensor_tensor(SZ[:, :, NP:NT], yS[:], SZ[:, :, NP:NT], ALU.mult).then_inc(S["samp_ok"], 1)

            def y_rows(q):
                c, gr = divmod(q, GROUPS)
                wait("y_ps", q + 1)
                for m in range(2):
                    i = v.scalar_tensor_tensor(PS[4 + q % 2][:, CH * m:CH * m + CH], XB[:, 2 * gr + m, CH * c:CH * c + CH],
                                               Dcol[:, 2 * gr + m:2 * gr + m + 1], PS[4 + q % 2][:, CH * m:CH * m + CH],
                                               ALU.mult, ALU.add)
                link(i)
                z = SZ[:, 2 * gr:2 * gr + 2, CH * c:CH * c + CH]
                v.tensor_tensor(z, PS[4 + q % 2][:, 0:256].rearrange("p (m l) -> p m l", m=2), z, ALU.mult)\
                 .then_inc(S["y_ok"], 1)

            def state_rows_out(q):
                c, gr = divmod(q, GROUPS)
                wait("st_ps", q + 1)
                pr = prevT[:, 256 * gr:256 * gr + 256]
                if c == 0:
                    v.tensor_copy(pr, PS[6 + q % 2][:, 0:256]).then_inc(S["st_ok"], 1)
                else:
                    p3 = pr.rearrange("p (h d) -> p h d", d=HD)
                    link(v.tensor_tensor(p3, p3, dec1[:, HPG * gr:HPG * gr + HPG].unsqueeze(2)
                                         .to_broadcast([P, HPG, HD]), ALU.mult))
                    v.tensor_tensor(pr, pr, PS[6 + q % 2][:, 0:256], ALU.add).then_inc(S["st_ok"], 1)

            for r in (3, 4):
                dve.wait_ge(st_s[r], 16 * len(range(r, 16, NSLOT)))
            for c in range(2):
                if c == 1:
                    wait("y_ps", GROUPS)
                for b in range(4):
                    wait("xtok_ps", 6 * c + b + 1)
                    v.tensor_tensor(xdt[:, 512 * b:512 * b + 512].rearrange("p (h d) -> p h d", d=HD),
                                    PS[b % 2].rearrange("p (h d) -> p h d", d=HD),
                                    dtok[:, c, 8 * b:8 * b + 8].unsqueeze(2).to_broadcast([P, 8, HD]), ALU.mult)\
                     .then_inc(S["xtok_ok"], 1)
                for gr in range(GROUPS):
                    q = c * GROUPS + gr
                    wait("cb_ps", q + 1)
                    link(v.tensor_tensor(CBm[q % 2], PS[2 + q % 2][:, 0:CH], utri[:], ALU.mult))
                    wait("exp_ok", q + 1)
                    v.tensor_tensor(LT[gr], LT[gr], CBm[q % 2].unsqueeze(1).to_broadcast([P, HPG, CH]),
                                    ALU.mult).then_inc(S["mt_ok"], 1)
                    if c == 1:
                        wait("ce_ok", gr + 1)
                        v.tensor_tensor(CTs[gr % 2], CTs[gr % 2],
                                        XB[:, XC + GC + gr, CH:2 * CH].unsqueeze(1).to_broadcast([P, HPG, CH]),
                                        ALU.mult).then_inc(S["cts_ok"], 1)
                    if q >= 1:
                        y_rows(q - 1)
                        state_rows_out(q - 1)
            y_rows(15)
            state_rows_out(15)
            dve.wait_ge(S["y_ok"], 16)
            for gr in range(GROUPS):
                wait("gn_rt", gr + 1)
                r = rs[gr % 2]
                link(v.reciprocal(r, r))
                for m in range(2):
                    i = v.scalar_tensor_tensor(SZ[:, 2 * gr + m, :], SZ[:, 2 * gr + m, :],
                                               pv[:, 40 + 2 * gr + m:41 + 2 * gr + m], r, ALU.mult, ALU.mult)
                i.then_inc(S["gn_ok"], 1)
            wait("s_mb", 32)
            wait("wo_ps", 2)
            for t in range(2):
                for nh in range(2):
                    i = v.tensor_tensor(PS[2 * t + nh], PS[2 * t + nh], MB[:, 0, 0, 512 * nh:512 * nh + 512], ALU.mult)
            for q in range(4):
                i = v.tensor_copy(acc[0:NS, 2, 256 * q:256 * q + 256], PS[4][32 * q:32 * q + NS, 0:256])
            link(i)
            for t in range(2):
                for nh in range(2):
                    xx = XT[:, t, 512 * nh:512 * nh + 512]
                    i = v.tensor_tensor(xx, xx, PS[2 * t + nh], ALU.add)
            link(v.tensor_tensor(acc[0:NS, 2, :], acc[0:NS, 2, :], MB[0:NS, 1, 0, :], ALU.mult))
            i = v.tensor_tensor(XT[0:NS, 2, :], XT[0:NS, 2, :], acc[0:NS, 2, :], ALU.add)
            i.then_inc(S["xm_ok"], 3)
            dve.wait_ge(S["xm_ok"], 3)
            wait("ld_n2", 16)
            link(v.scalar_tensor_tensor(MB[:, 0, 2, :], MB[:, 0, 2, :], 1.0, n2b, ALU.add, ALU.mult))
            link(v.scalar_tensor_tensor(MB[0:NS, 1, 2, :], MB[0:NS, 1, 2, :], 1.0, n2b[0:NS, :], ALU.add, ALU.mult))
            link(v.memset(h2[:, 2, :], 0.0))
            rstd(XT, 4, acc[:, 0, :], 2)
            for t in range(3):
                R = ROWS[t]
                q = t // 2
                link(v.scalar_tensor_tensor(h2[0:R, t, :], XT[0:R, t, :], st[0:R, 4 + t:5 + t], MB[0:R, q, 2, :],
                                            ALU.mult, ALU.mult))
                v.tensor_tensor(h2[0:R, t, :], h2[0:R, t, :], MB[0:R, q, 1, :], ALU.add).then_inc(S["h2_ok"], 1)
            wait("ld_rt", 32)
            wait("wo_ps", 2)
            v.memset(posx, -1.0)
            v.memset(comb, 0.0)
            v.memset(SwT, 0.0)
            v.memset(Gw, 0.0)
            link(v.memset(mask, 0.0))
            for t in range(3):
                R = ROWS[t]
                wait("lg_ps", 3)
                link(v.tensor_tensor(lg[0:R, :], PS[4][0:R, 32 * t:32 * t + 32], rb[0:R, :], ALU.add))
                link(v.max(m8[0:R, :], lg[0:R, :]))
                link(v.max_index(ix[0:R, :], m8[0:R, :], lg[0:R, :]))
                link(v.tensor_copy(ixf[0:R, :], ix[0:R, :]))
                v.tensor_scalar(m8[0:R, 7:8], m8[0:R, 0:1], -1.0, None, ALU.mult).then_inc(S["rt_m"], 1)
                wait("rt_e", t + 1)
                link(v.tensor_reduce(ex[0:R, 4:5], ex[0:R, 0:4], AX.X, ALU.add))
                link(v.reciprocal(ex[0:R, 4:5], ex[0:R, 4:5]))
                link(v.tensor_scalar(ex[0:R, 0:4], ex[0:R, 0:4], ex[0:R, 4:5], None, ALU.mult))
                for k in range(TOPK):
                    v.tensor_scalar(oh[0:R, k, :], iota[0:R, 0:NE], ixf[0:R, k:k + 1], None, ALU.is_equal)
                    i = v.tensor_scalar(pw[0:R, k, :], iota[0:R, 0:NE], ixf[0:R, k:k + 1], ex[0:R, k:k + 1],
                                        ALU.is_equal, ALU.mult)
                link(i)
                v.tensor_reduce(mask[0:R, t, :], oh[0:R, :, :].rearrange("p k e -> p e k"), AX.X, ALU.add)
                v.tensor_reduce(comb[0:R, :, t], pw[0:R, :, :].rearrange("p k e -> p e k"), AX.X, ALU.add)\
                 .then_inc(S["rt_p"], 1)
                dve.wait_ge(S["rt_p"], t + 1)
            wait("pos_ps", 1)
            link(v.tensor_reduce(cnt[:, 0:1], PS[5][0:1, 96:128], AX.X, ALU.max))
            link(v.tensor_scalar(cnt[:, 1:5], thr[:], cnt[:, 0:1], None, ALU.is_lt))
            link(v.tensor_reduce(cnt[:, 5:6], cnt[:, 1:5], AX.X, ALU.add))
            v.tensor_scalar(npi[:], cnt[:, 5:6], 1.0, None, ALU.add).then_inc(S["np_ok"], 1)
            for t in range(3):
                R = ROWS[t]
                i = v.tensor_tensor(mask[0:R, t, :], mask[0:R, t, :], PS[5][0:R, 32 * t:32 * t + 32], ALU.mult)
            link(i)
            for t in range(3):
                R = ROWS[t]
                for p_ in range(MAXPASS):
                    i = v.tensor_scalar(posx[0:R, NE * p_:NE * p_ + NE, t], mask[0:R, t, :], -1.0 - CAP * p_, None,
                                        ALU.add)
            link(i)
            wait("cmb_ps", 1)
            v.tensor_copy(combT, PS[6][0:NE, 0:NT]).then_inc(S["cmb_ok"], 1)
            for t in range(3):
                R = ROWS[t]
                wait("ai_ps", t + 1)
                for nh in range(2):
                    i = v.tensor_copy(acc[0:R, t, 512 * nh:512 * nh + 512], PS[2 * (t % 2) + nh][0:R, :])
                i.then_inc(S["acc_ok"], 1)
            dve.wait_ge(S["acc_ok"], 3)
            wait("ld_br", 16)
            link(v.memset(osb, 0.0))

            def gather_matrix(x, i):
                return v.tensor_tensor(G[x], iota[:].unsqueeze(1).to_broadcast([P, 3, CAP]),
                                       posx[:, bass.ds(i, 1), :].rearrange("p o t -> p (o t)").unsqueeze(2)
                                       .to_broadcast([P, 3, CAP]), ALU.is_equal)

            def bias_select(x, e):
                return v.tensor_copy(bsel[x], eye[:, bass.ds(e, 1)].to_broadcast([P, 64]))

            v.tensor_copy(eye[:, 0:NE], ident[:, 0:NE])
            link(v.tensor_copy(eye[:, NE:NE + 1], ident[:, 0:1]))
            gather_matrix(0, 0).then_inc(S["d_G"], 1)
            bias_select(0, 0).then_inc(S["d_bs"], 1)
            v.tensor_copy(cnt[:, 6:7], cnt[:, 5:6]).then_inc(S["moe_ready"], 1)
            for nm in ("d_guf", "d_add", "a_o", "a_swT"):
                dve.sem_inc(S[nm], 1)
            wait("np_ok", 1)
            wait("moe_ready", 1)
            npass = dve.value_load(npi[0:1, 0:1], min_val=1, max_val=MAXPASS)
            flat = PGU[:, :, :].rearrange("p a b -> p (a b)")

            def adds(it, t):
                dve.wait_ge(S["sc_ps"], it * 3 + (t + 1))
                R = ROWS[t]
                for nh in range(2):
                    y = acc[0:R, t, 512 * nh:512 * nh + 512]
                    i = v.tensor_tensor(y, y, PS[6 + nh][0:R, :], ALU.add)
                i.then_inc(S["d_add"], 1)

            with dve.Fori(0, npass) as ps:
                with dve.Fori(0, NE // 2) as pair:
                    it = ps * (NE // 2) + pair
                    for x in range(2):
                        f = it * 2 + x
                        gather_matrix(1 - x, f + 1).then_inc(S["d_G"], 1)
                        bias_select(1 - x, pair * 2 + (x + 1)).then_inc(S["d_bs"], 1)
                        dve.wait_ge(S["gu_used"], f * 4 + 4)
                        v.tensor_scalar(gg, flat[:, 0::2], LIMIT, None, ALU.min).then_inc(S["d_g"], 1)
                        v.tensor_scalar(uu, flat[:, 1::2], -LIMIT, LIMIT, ALU.max, ALU.min)\
                         .then_inc(S["d_guf"], 1)
                        dve.wait_ge(S["d_guf"], f + 2)
                        v.scalar_tensor_tensor(uu, uu, 1.0, gg, ALU.add, ALU.mult).then_inc(S["d_t"], 1)
                        dve.wait_ge(S["d_t"], f + 1)
                        dve.wait_ge(S["a_sig"], f + 1)
                        v.tensor_tensor(aa, uu, sg, ALU.mult).then_inc(S["d_act"], 1)
                        adds(it, 2 * x)
                        v.tensor_tensor(Gw[:, :, x, :], G[x], comb[:, bass.ds(pair * 2 + x, 1), :]
                                        .rearrange("p o t -> p (o t)").unsqueeze(2).to_broadcast([P, 3, CAP]),
                                        ALU.mult).then_inc(S["d_gw"], 1)
                        dve.wait_ge(S["d_gw"], f + 1)
                        if x == 0:
                            adds(it, 1)
            for t in range(3):
                adds(npass * (NE // 2), t)
            dve.wait_ge(S["d_add"], npass * (3 * NE // 2) + 4)
            wait("ld_fn", 16)
            for t in range(3):
                R = ROWS[t]
                link(v.tensor_tensor(acc[0:R, t, :], acc[0:R, t, :], MB[0:R, t // 2, 3, :], ALU.mult))
                link(v.tensor_tensor(acc[0:R, t, :], acc[0:R, t, :], XT[0:R, t, :], ALU.add))
            rstd(acc, 8, h2[:, 0, :], 3)
            for t in range(3):
                R = ROWS[t]
                v.scalar_tensor_tensor(XT[0:R, t, :], acc[0:R, t, :], st[0:R, 8 + t:9 + t], MB[0:R, 0, 1, :],
                                       ALU.mult, ALU.mult).then_inc(S["y_done"], 1)



_UNUSED = ("sc_w_in", "sc_conv_w", "sc_w_out")
_OUTS = [("y_prompt", (1, NP, D)), ("y_sample", (NS, 1, D)), ("new_ssm_prompt", (1, HEADS, HD, STATE)),
         ("new_ssm_conv_prompt", (1, CONV - 1, CDIM)), ("new_sconv_prompt", (1, 2, D)),
         ("new_ssm_sample", (NS, HEADS, HD, STATE)), ("new_ssm_conv_sample", (NS, CONV - 1, CDIM)),
         ("new_sconv_sample", (NS, 2, D))]


def kernel(**inputs):
    import numpy as _np
    import concourse.bacc as _bacc
    from concourse import mybir as _mybir
    from concourse.bass_utils import run_bass_kernel_spmd as _run

    nc = _bacc.Bacc("TRN2", target_bir_lowering=False, num_devices=1)
    arrays, io = {}, {}
    for name, x in inputs.items():
        if name in _UNUSED:
            continue
        x = _np.ascontiguousarray(x)
        arrays[f"in_{name}"] = x
        io[name] = nc.dram_tensor(f"in_{name}", x.shape, _mybir.dt.from_np(x.dtype), kind="ExternalInput").ap()
    for name, shape in _OUTS:
        io[name] = nc.dram_tensor(f"out_{name}", shape, _mybir.dt.float32, kind="ExternalOutput").ap()
    build(nc, io)
    r = _run(nc, [arrays], core_ids=[0])
    return tuple(r.results[0][f"out_{name}"] for name, _ in _OUTS)
```

```python
from contextlib import ExitStack

import concourse.bass as bass
from concourse import mybir

F32 = mybir.dt.float32
I32 = mybir.dt.int32
U32 = mybir.dt.uint32
ALU = mybir.AluOpType
ACT = mybir.ActivationFunctionType
AX = mybir.AxisListType

P = 128
D = 1024
KT = D // P
NP = 256
NS = 8
NT = NP + NS
ROWS = (128, 128, NS)
INNER = 2 * D
HEADS, HD = 32, 64
GROUPS, HPG, STATE = 8, 4, 128
CONV = 4
XC = INNER // P
GC = GROUPS
NCH = XC + 2 * GC
CDIM = NCH * P
CH = 128
NSLOT = 5
NE = 32
TOPK = 4
CAP = 64
MAXPASS = -(-NT // CAP)
LIMIT = 7.0
ALPHA = 1.702
EPS = 1e-5
SEQR = 3 + NP + 4 * NS
SEQC = SEQR - 3

ADA, WIN = "ada", "win"
UNITS = [(ADA, 0), (ADA, 1), (WIN, 4096), (ADA, 2), (WIN, 5120), (ADA, 3), (WIN, 2048), (ADA, 4), (WIN, 3072),
         (ADA, 5), (WIN, 1024), (WIN, 0)]
CHUNKS = []
for _u, (_kind, _col) in enumerate(UNITS):
    if _kind == WIN:
        for _j in ((4, 5, 6, 7, 0, 1, 2, 3) if _col == D else range(8)):
            _c = _col // P + _j
            CHUNKS.append((_u, _j, "z", _c) if _c < XC else (_u, _j, "c", _c - XC))
NCONV = NCH
UNIT_A = [u for u, (k, _) in enumerate(UNITS) if k == ADA]


def build(nc, io):
    with ExitStack() as ctx:
        def sb(name, shape, dt=F32):
            return ctx.enter_context(nc.sbuf_tensor(name, shape, dt))

        def sem(name):
            return ctx.enter_context(nc.semaphore(name))

        mod_d = nc.dram_tensor("mod_d", (9, 4, D), F32, kind="Internal").ap()
        dd_d = nc.dram_tensor("dd_d", (HEADS, 2, NS), F32, kind="Internal").ap()
        acs_d = nc.dram_tensor("acs_d", (HEADS, 2, CH), F32, kind="Internal").ap()
        bc_d = nc.dram_tensor("bc_d", (P, P), F32, kind="Internal").ap()

        BIG = sb("BIG", [P, 24, D])
        XBr = sb("XBr", [P, NCH * NT])
        XT = sb("XT", [P, 3, D])
        SZr = sb("SZr", [P, XC * NT])
        U = sb("U", [P, 10496])

        def cut(base, a, n, **kw):
            v = base[:, a:a + n]
            if kw:
                (k, m), = kw.items()
                v = v.rearrange(f"p ({k} x) -> p {k} x", **{k: m})
            return v

        W = [BIG[:, 8 * i:8 * i + 8, :] for i in range(3)]
        XB = XBr[:, :].rearrange("p (c t) -> p c t", t=NT)
        SZ = SZr[:, :].rearrange("p (c t) -> p c t", t=NT)
        xn = cut(XBr, 0, 3072, t=3)
        CR = XBr[0:9, 3072:4096]
        junk = cut(XBr, 4096, 1024)
        AB = cut(SZr, 0, 1536, u=6)
        MS = cut(SZr, 1536, 1536, u=6)
        dtt = [SZr[0:HEADS, 3072 + i * NT:3072 + (i + 1) * NT] for i in range(4)]
        h1T = cut(U, 0, KT * NT, k=KT)
        RW = cut(U, 2112, 4 * SEQR, k=4)
        HT = cut(U, 3276, NCH * 24, c=NCH)
        CV = cut(U, 4044, 3 * SEQC, k=3)
        HI = U[0:24, 4908:4908 + CDIM]
        BCb = [U[:, 7980:7980 + 2048].rearrange("p (j n) -> p j n", n=P),
               U[:, 2112:2112 + 2048].rearrange("p (j n) -> p j n", n=P)]
        TT = sb("TT", [P, 4, 11, 8])
        ident = sb("ident", [P, P])
        utri = sb("utri", [P, P])
        ones = sb("ones", [P, P])
        PR1 = XBr[:, 5120:5248]
        PR2 = XBr[0:56, 5248:5376]
        zeros = XBr[0:2, 7000:8024]
        bcs = U[:, 10028:10156]
        bcT = U[:, 10156:10284]
        acsT = dtt[2][:, 0:2 * CH].rearrange("p (c l) -> p c l", c=2)
        cw = sb("cw", [P, P])
        pv = sb("pv", [P, 56])
        m1 = sb("m1", [P, 2, KT, 9])
        scT = sb("scT", [P, KT, 32])
        WDT = sb("WDT", [P, KT, 32])
        DDc = WDT[:, :, :].rearrange("p k h -> p (k h)").rearrange("p (c q s) -> p c q s", c=XC, q=2)
        dd = sb("dd", [HEADS, 2, NS])
        dtok = sb("dtok", [P, 4, 32])
        acst = sb("acst", [P, 2, 32])
        dcy = sb("dcy", [P, 2, 32])
        dec1 = sb("dec1", [P, 32])
        Dbc = sb("Dbc", [P, 32])
        Dcol = sb("Dcol", [P, XC])
        st = sb("st", [P, 16])
        hsc = sb("hsc", [HEADS, 4])
        npi = sb("npi", [1, 1], I32)
        xdtS = sb("xdtS", [P, XC, NS])
        yS = sb("yS", [P, XC, NS])

        BF = BIG[:, :, :].rearrange("p a b -> p (a b)")
        bcA = [BF[:, o:o + 4096].rearrange("p (h l) -> p h l", h=HEADS) for o in (0, 8192)]
        prevT = BF[:, 4096:6144]
        LT = [bcA[0][:, HPG * i:HPG * i + HPG, :] for i in range(GROUPS)]
        Btok = [BF[:, 7168:8192], U[:, 4908:5932]]
        xdt = [BF[:, 12288:14336], U[:, 0:2048]]
        xdec = [BF[:, 14336:16384], U[:, 2112:4160]]
        diagD = [U[:, o:o + 1024].rearrange("p (c l) -> p c l", c=8) for o in (5932, 6956)]
        SR = [v.rearrange("p (c n) -> p c n", n=P) for v in
              (U[:, 4908:5932], U[:, 5932:6956], U[:, 6956:7980], BF[:, 4096:5120], BF[:, 5120:6144])]
        TLs = U[0:88, 4160:4672].rearrange("p (u f) -> p u f", u=4)
        CTs = [U[:, 9248 + 512 * i:9760 + 512 * i].rearrange("p (r l) -> p r l", r=4) for i in range(2)]
        CBm = [BF[:, 6144 + 128 * i:6272 + 128 * i] for i in range(2)]
        sq = [U[:, 8192 + 528 * i:8720 + 528 * i].rearrange("p (r l) -> p r l", r=2) for i in range(2)]
        gnr = BF[0:GROUPS, 14336:14336 + NT]
        gsel = BF[0:GROUPS, 14848:15872].rearrange("p (g l) -> p g l", g=GROUPS)
        onecol = sb("onecol", [P, 2 * GROUPS - 1])
        MB = U[:, 0:8192].rearrange("p (q u f) -> p q u f", q=2, u=4)
        n2b = U[:, 3072:4096]
        scr = U[:, 7168:8192]
        h2 = cut(XBr, 0, 3072, t=3)
        acc = cut(XBr, 3072, 3072, t=3)
        BR = XBr[:, 6144:8192]
        h2T = XBr[:, 3072:5184].rearrange("p (k t) -> p k t", k=KT)
        BD = U[:, 4096:5120]
        hg, gg, uu, sg, aa = [SZr[:, 512 * i:512 * i + 512] for i in range(5)]
        osb = SZr[:, 2560:3584]
        hgT = SZr[:, 3584:4096].rearrange("p (c s) -> p c s", c=4)
        actT = U[:, 0:512].rearrange("p (c s) -> p c s", c=4)
        bsel = [U[:, 512:576], U[:, 576:640]]
        G = [U[:, 2048 + 192 * i:2240 + 192 * i].rearrange("p (t j) -> p t j", t=3) for i in range(2)]
        o = 8192

        def small(n):
            nonlocal o
            o += n
            return U[:, o - n:o]
        Gw = small(384).rearrange("p (t d j) -> p t d j", t=3, d=2)
        SwT = small(3 * P)
        eye = SZr[:, 4096:4096 + NE + 1]
        posx = small(3 * (MAXPASS * NE + 1)).rearrange("p (i t) -> p i t", t=3)
        comb = small(96).rearrange("p (e t) -> p e t", t=3)
        mask = small(96).rearrange("p (t e) -> p t e", t=3)
        RWt = small(KT * NE).rearrange("p (k e) -> p k e", k=KT)
        lg = small(NE)
        rb = small(NE)
        oh = small(4 * NE).rearrange("p (k e) -> p k e", k=4)
        pw = small(4 * NE).rearrange("p (k e) -> p k e", k=4)
        m8 = small(8)
        ixf = small(8)
        ex = small(8)
        assert o <= 10496
        ix = sb("ix", [P, 8], U32)
        iota = sb("iota", [P, 64])
        thr = sb("thr", [1, 4])
        cnt = sb("cnt", [1, 8])

        PSB = [ctx.enter_context(nc.psum_tensor(f"PS{i}", [P, 512], F32)) for i in range(6)]
        PGU = ctx.enter_context(nc.psum_tensor("PGU", [P, 2, 512], F32))
        PS = [PGU[:, 0, :], PGU[:, 1, :]] + [b[:, :] for b in PSB]

        names = """ld_x ld_c ld_par ld_hist ld_wdt ld_ab ld_hs ld_D ld_rt ld_n2 ld_bd ld_br ld_fn
        consts_pool consts_dve silu_c cT_ps scT_ok par_ps par_ok hist_ps hist_ok ada_ps ms_ok xn_ok xnT_ps h1_act
        h1_dve m1_ps m1_ok dt_ps chunk_ps chunk_evac conv_done silu_done dtTok_ps dtok_ok acs_ps acs_ok
        bcs_ok bcs_ps bcT_ok dt_t dt_e dt_u dt_l dt_ok dec_ok dd_ok s_dd s_ddl s_acs s_bcd tl_ps tl_ok s_tl s_mod s_mb
        s_scaled item_done samp_ok
        xtok_ps xtok_ok st_act diag_ok cb_ps lt_ok exp_ok mt_ok ce_ok cts_ok y_ps y_ok st_ps st_ok dcy_ok xdec_ok lastx
        hf_ps hf_ok s_hf sq_ok gn_ps gn_rt gn_rc gn_bc gn_ok pool_set ss_ok rt3_ok
        wo_ps h2_ok h2T_ps h2T_ok lg_ps rt_m rt_e rt_p rt_k pos_ps np_ok moe_ready ld_half ld_cols
        gu_used gath_ps sc_ps actT_ps hgT_ps swT_ps dn_used d_bs d_guf d_G d_g d_act d_add d_t d_gw a_actT
        a_sig a_hg a_hgT a_swT a_o y_done s_out s_y ch_dve ch_act ch_pool""".split()
        S = {n: sem(n) for n in names}
        ld_w = [sem(f"ld_w{i}") for i in range(3)]
        ld_wo = [sem(f"ld_wo{i}") for i in range(2)]
        ld_bc = [sem(f"ld_bc{i}") for i in range(2)]
        ld_s = [sem(f"ld_s{i}") for i in range(NSLOT)]
        st_s = [sem(f"st_s{i}") for i in range(NSLOT)]
        ld_bcb = [sem(f"ld_bcb{i}") for i in range(2)]
        gu_ld = [sem(f"gu_ld{i}") for i in range(4)]
        dn_ld = [sem(f"dn_ld{i}") for i in range(2)]

        gu_w = io["moe_w_gate_up"]
        dn_w = io["moe_w_down"]
        state_rows = io["state_ssm"].rearrange("s h p n -> s (h p) n")
        state_out = io["new_ssm_sample"].rearrange("s h p n -> s (h p) n")

        def gu_src(e, j):
            return gu_w[0, e, 256 * j:256 * j + 256, :] if isinstance(e, int) else \
                gu_w[0, bass.ds(e, 1), 256 * j:256 * j + 256, :].rearrange("o r f -> (o r) f")

        def dn_src(e, j):
            return dn_w[0, e, 512 * j:512 * j + 512, :] if isinstance(e, int) else \
                dn_w[0, bass.ds(e, 1), 512 * j:512 * j + 512, :].rearrange("o r f -> (o r) f")

        def used(eng, u):
            if UNITS[u][0] == ADA:
                eng.wait_ge(S["ada_ps"], UNIT_A.index(u) + 1)
            else:
                eng.wait_ge(S["chunk_ps"], max(n for n, c in enumerate(CHUNKS) if c[0] == u) + 1)

        def last_bank(t, nh):
            return PS[((6, 7), (0, 1), (3, 4))[t][nh]]

        block = ctx.enter_context(nc.Block())

        @block.sync
        def _(sp):
            def wait(name, v):
                sp.wait_ge(S[name], v)

            def small_loads():
                with nc.allow_non_contiguous_dma(reason="one value per head"):
                    sp.dma_start(hsc[:, 0:1], io["ssd_dt_bias"].rearrange("(h o) -> h o", o=1)).then_inc(S["ld_hs"], 16)
                    sp.dma_start(hsc[:, 1:2], io["ssd_A_log"].rearrange("(h o) -> h o", o=1)).then_inc(S["ld_hs"], 16)
                sp.dma_start(Dbc[:], io["ssd_D"].rearrange("(o h) -> o h", o=1).to_broadcast([P, HEADS]))\
                   .then_inc(S["ld_D"], 16)

            sp.dma_start(XBr[0:1, 3072:4096], io["c_prompt"]).then_inc(S["ld_c"], 16)
            sp.dma_start(XBr[1:9, 3072:4096], io["c_sample"]).then_inc(S["ld_c"], 16)
            sp.dma_start(XT[:, 0:2, :], io["x_prompt"][0].rearrange("(t p) f -> p t f", p=P)).then_inc(S["ld_x"], 16)
            sp.dma_start(XT[0:NS, 2, :], io["x_sample"][:, 0, :]).then_inc(S["ld_x"], 16)

            def load_bcb(s):
                if s == 0:
                    wait("s_bcd", 16)
                if s == 1:
                    wait("silu_done", NCONV)
                if s >= 2:
                    wait("item_done", 2 * (s - 1))
                src = bass.AP(tensor=bc_d.tensor, offset=s * 2048, ap=[[0, P], [1, 2048]])
                sp.dma_start(BCb[s % 2].rearrange("p j n -> p (j n)"), src).then_inc(ld_bcb[s % 2], 16)

            def load_state(j):
                s, half = divmod(j, 2)
                if j >= NSLOT:
                    sp.wait_ge(st_s[j % NSLOT], 16 * (j // NSLOT))
                sp.dma_start(SR[j % NSLOT], state_rows[s, D * half:D * half + D, :].rearrange("(c p) n -> p c n", p=P))\
                  .then_inc(ld_s[j % NSLOT], 16)

            for u, (kind, col) in enumerate(UNITS):
                if u == 1:
                    wait("consts_dve", 1)
                    for q in range(4):
                        src = bass.AP(tensor=io["ada_b"].tensor, offset=io["ada_b"].offset + 256 * q,
                                      ap=[[0, 9], [D, 6], [1, 256]])
                        sp.dma_start(AB[32 * q:32 * q + 9, :, :], src).then_inc(S["ld_ab"], 16)
                if u == 1:
                    sp.dma_start(WDT[:], io["ssd_w_in"][:, INNER + CDIM:].rearrange("(k p) h -> p k h", p=P))\
                      .then_inc(S["ld_wdt"], 16)
                if u == 8:
                    wait("hist_ps", 1)
                    for j in range(3):
                        load_state(j)
                if u >= 3:
                    used(sp, u - 3)
                if kind == ADA:
                    src = io["ada_w"][0, :, col * D:(col + 1) * D]
                else:
                    src = io["ssd_w_in"][:, col:col + D]
                if u == 2:
                    sp.dma_start(W[2][:, :, 0:D // 2], src[:, 0:D // 2].rearrange("(k p) f -> p k f", p=P))\
                      .then_inc(S["ld_cols"], 16)
                    sp.dma_start(W[2][:, :, D // 2:D], src[:, D // 2:D].rearrange("(k p) f -> p k f", p=P))\
                      .then_inc(ld_w[2], 16)
                    small_loads()
                    continue
                first = 0
                if u == 1:
                    first = KT // 2
                    sp.dma_start(W[1][:, 0:first, :], src[0:P * first, :].rearrange("(k p) f -> p k f", p=P))\
                      .then_inc(S["ld_half"], 16)
                sp.dma_start(W[u % 3][:, first:KT, :], src[P * first:D, :].rearrange("(k p) f -> p k f", p=P))\
                  .then_inc(ld_w[u % 3], 16)
            load_bcb(0)
            for j in range(3, 16):
                if j == 5:
                    load_bcb(1)
                if j == 3:
                    used(sp, 9)
                if j >= 6 and j % 2 == 0:
                    load_bcb(j // 2 - 1)
                load_state(j)
            load_bcb(7)
            wait("tl_ok", 1)
            cp = io["new_ssm_conv_prompt"][0]
            cs = io["new_ssm_conv_sample"]
            for t in range(3):
                sp.dma_start(cp[t, :].rearrange("(u c f) -> c u f", u=4, c=8),
                             TLs[8 * t:8 * t + 8, :, :]).then_inc(S["s_tl"], 16)
            for s in range(NS):
                sp.dma_start(cs[s, 2, :].rearrange("(u c f) -> c u f", u=4, c=8),
                             TLs[24 + 8 * s:32 + 8 * s, :, :]).then_inc(S["s_tl"], 16)
            used(sp, len(UNITS) - 1)
            sp.wait_ge(ld_bc[1], 16)
            sp.dma_start(W[2], io["ssd_w_out"][0:D, :].rearrange("(k p) f -> p k f", p=P)).then_inc(ld_wo[0], 16)
            wait("y_ok", 16)
            wait("hf_ps", 4)
            sp.dma_start(W[0], io["ssd_w_out"][D:2 * D, :].rearrange("(k p) f -> p k f", p=P)).then_inc(ld_wo[1], 16)

            wait("s_mod", 64)
            wait("s_tl", 11 * 16)
            for r in range(3):
                sp.wait_ge(st_s[r], 16 * len(range(r, 16, NSLOT)))
            src = bass.AP(tensor=mod_d.tensor, offset=0, ap=[[0, P], [1, 3 * D]])
            sp.dma_start(MB[:, 0, 0:3, :].rearrange("p u f -> p (u f)"), src).then_inc(S["s_mb"], 16)
            sp.dma_start(MB[0:NS, 1, 0:3, :], mod_d[1:9, 0:3, :]).then_inc(S["s_mb"], 16)
            sp.dma_start(n2b, io["norm2_w"][0:1, :].to_broadcast([P, D])).then_inc(S["ld_n2"], 16)

            def load_gu(e, j):
                sp.dma_start(BIG[:, 4 * j:4 * j + 4, :].rearrange("p (k h) f -> p k (h f)", k=2),
                             gu_src(e, j).rearrange("(k p) f -> p k f", p=P)).then_inc(gu_ld[j], 16)

            def load_dn(e, j):
                sp.dma_start(BIG[:, 16 + 4 * j:20 + 4 * j, :],
                             dn_src(e, j).rearrange("(k p) f -> p k f", p=P)).then_inc(dn_ld[j], 16)

            wait("s_hf", 16)
            for j in (2, 3):
                if j == 3:
                    wait("gn_bc", GROUPS)
                load_gu(0, j)
            wait("wo_ps", 1)
            for j in range(2):
                load_dn(0, j)
            wait("wo_ps", 5)
            for j in (0, 1):
                load_gu(0, j)
            wait("np_ok", 1)
            npass = sp.value_load(npi[0:1, 0:1], min_val=1, max_val=MAXPASS)

            def load_expert(e, it):
                for j in range(4):
                    sp.wait_ge(S["gu_used"], it * 4 + (j - 3))
                    load_gu(e, j)
                for j in range(2):
                    sp.wait_ge(S["dn_used"], it * 2 + (j - 1))
                    load_dn(e, j)

            with sp.Fori(0, npass) as ps:
                with sp.Fori(1, NE) as e:
                    load_expert(e, ps * NE + e)
                with sp.If(ps + 1 < npass):
                    load_expert(0, ps * NE + NE)
            for t in range(3):
                wait("y_done", t + 1)
                out = io["y_prompt"][0, P * t:P * t + P, :] if t < 2 else io["y_sample"][:, 0, :]
                sp.dma_start(out, XT[0:ROWS[t], t, :]).then_inc(S["s_y"], 16)
            wait("s_y", 48)

        @block.gpsimd
        def _(pool):
            g = nc.gpsimd

            def wait(name, v):
                pool.wait_ge(S[name], v)

            g.memset(zeros, 0.0).then_inc(S["ch_pool"], 1)
            g.memset(ident[:], 0.0)
            g.memset(utri[:], 1.0)
            g.memset(ones[:], 1.0)
            g.memset(TT[:], 0.0)
            g.memset(onecol[:], 0.0)
            g.iota(iota[:], [[1, 64]], base=0, channel_multiplier=0,
                   allow_small_or_imprecise_dtypes=True)
            g.iota(thr[:], [[CAP, 4]], base=CAP, channel_multiplier=0,
                   allow_small_or_imprecise_dtypes=True).then_inc(S["ch_pool"], 1)
            wait("ch_pool", 2)
            g.affine_select(out=ident[:], in_=ident[:], pattern=[[-1, P]], compare_op=ALU.not_equal, fill=1.0,
                            base=0, channel_multiplier=1)
            g.affine_select(out=utri[:], in_=utri[:], pattern=[[1, P]], compare_op=ALU.is_ge, fill=0.0,
                            base=0, channel_multiplier=-1).then_inc(S["consts_pool"], 1)
            g.memset(onecol[:, GROUPS - 1:GROUPS], 1.0)
            g.dma_start(io["new_sconv_prompt"][0], zeros).then_inc(S["s_out"], 16)
            g.dma_start(io["new_sconv_sample"].rearrange("s k f -> (s k) f"),
                        io["state_sconv"].rearrange("s k f -> (s k) f")).then_inc(S["s_out"], 16)
            g.dma_start(io["new_ssm_conv_sample"][:, 0:2, :], io["state_ssm_conv"][:, 1:3, :]).then_inc(S["s_out"], 16)
            wait("dd_ok", 1)
            g.dma_start(dd_d, dd[:]).then_inc(S["s_dd"], 16)
            wait("s_dd", 16)
            for half in range(2):
                src = bass.AP(tensor=dd_d.tensor, offset=half * 16, ap=[[0, 64], [32, 16], [1, 16]])
                g.dma_start(WDT[64 * half:64 * half + 64, :, :].rearrange("p k (a b) -> p (k a) b", a=2), src)\
                 .then_inc(S["s_ddl"], 16)
            wait("acs_ok", 1)
            g.dma_start(acs_d, acsT).then_inc(S["s_acs"], 16)
            wait("bcT_ok", 1)
            g.dma_start(bc_d, bcT).then_inc(S["s_bcd"], 16)
            wait("s_acs", 16)

            def store_state(j):
                s, half = divmod(j, 2)
                wait("item_done", j + 1)
                g.dma_start(state_out[s, D * half:D * half + D, :].rearrange("(c p) n -> p c n", p=P),
                            SR[j % NSLOT]).then_inc(st_s[j % NSLOT], 16)

            def last_sum(c):
                pool.wait_ge(ld_bc[c], 16)
                g.tensor_tensor(dcy[:, c, :], bcA[c][:, :, CH - 1], acst[:, c, :], ALU.subtract)\
                 .then_inc(S["lastx"], 1)

            def differences(q):
                c, gr = divmod(q, GROUPS)
                if q == 0:
                    wait("lastx", 1)
                if c == 1:
                    wait("y_ps", gr + 1)
                if c == 1:
                    heads = slice(HPG * gr, HPG * gr + HPG)
                    g.tensor_tensor(LT[gr], bcA[1][:, heads, :],
                                    acst[:, 1, heads].unsqueeze(2).to_broadcast([P, HPG, CH]),
                                    ALU.subtract).then_inc(S["lt_ok"], 1)
                    return
                for r in range(HPG):
                    h = gr * HPG + r
                    i = g.tensor_scalar(LT[gr][:, r, :], bcA[0][:, h, :], acst[:, 0, h:h + 1], 0.0,
                                        ALU.subtract, ALU.min)
                i.then_inc(S["lt_ok"], 1)

            def decayed(c):
                wait("dcy_ok", c + 1)
                for b in range(4):
                    wait("xtok_ok", 6 * c + b + 1)
                    g.tensor_tensor(xdec[c][:, 512 * b:512 * b + 512].rearrange("p (h d) -> p h d", d=HD),
                                    xdt[c][:, 512 * b:512 * b + 512].rearrange("p (h d) -> p h d", d=HD),
                                    dcy[:, c, 8 * b:8 * b + 8].unsqueeze(2).to_broadcast([P, 8, HD]), ALU.mult)\
                     .then_inc(S["xdec_ok"], 1)

            def diagonals(i):
                pool.wait_ge(st_s[1 + i], 16 * len(range(1 + i, 16, NSLOT)))
                g.tensor_tensor(diagD[i], ident[:].unsqueeze(1).to_broadcast([P, 8, P]),
                                Dcol[:, 8 * i:8 * i + 8].unsqueeze(2).to_broadcast([P, 8, P]), ALU.mult)\
                 .then_inc(S["diag_ok"], 1)

            wait("ms_ok", 6)
            for q in range(4):
                g.dma_start(mod_d[:, :, 256 * q:256 * q + 256], MS[32 * q:32 * q + 9, 2:6, :])\
                 .then_inc(S["s_mod"], 16)

            def load_acs(c):
                used(pool, 9 + c)
                src = bass.AP(tensor=acs_d.tensor, offset=c * CH, ap=[[0, P], [2 * CH, HEADS], [1, CH]])
                g.dma_start(bcA[c], src).then_inc(ld_bc[c], 16)

            load_acs(0)
            for j in range(16):
                if j == 15:
                    decayed(0)
                store_state(j)
                if j == 3:
                    last_sum(0)
                if 3 <= j < 3 + GROUPS:
                    differences(j - 3)
                if j == 13:
                    diagonals(0)
                if j == 14:
                    load_acs(1)
            diagonals(1)
            last_sum(1)
            for q in range(GROUPS, 16):
                differences(q)
                if q == GROUPS + 1:
                    decayed(1)
            for r in range(NSLOT):
                pool.wait_ge(st_s[r], 16 * len(range(r, 16, NSLOT)))
            wait("y_ok", 16)
            g.memset(h2[:, 2, :], 0.0)
            g.memset(BR, 0.0).then_inc(S["ch_pool"], 1)
            wait("ch_pool", 3)
            g.dma_start(BR[0:NE, :], io["moe_b_gate_up"][0]).then_inc(S["ld_br"], 16)
            wait("gn_ps", GROUPS)
            g.dma_start(RWt[:, :, :], io["router_w"][0].rearrange("(k p) e -> p k e", p=P)).then_inc(S["ld_rt"], 16)
            g.dma_start(rb, io["router_b"][0:1, :].to_broadcast([P, NE])).then_inc(S["ld_rt"], 16)
            g.memset(posx, -1.0)
            g.memset(comb, 0.0)
            g.memset(SwT, 0.0)
            g.memset(Gw, 0.0)
            g.memset(mask, 0.0).then_inc(S["pool_set"], 1)
            wait("wo_ps", 5)
            g.tensor_copy(eye[:, 0:NE], ident[:, 0:NE])
            g.tensor_copy(eye[:, NE:NE + 1], ident[:, 0:1])
            g.memset(osb, 0.0).then_inc(S["pool_set"], 1)
            wait("h2_ok", 4)
            g.memset(BD, 0.0).then_inc(S["ch_pool"], 1)
            g.dma_start(MB[:, 0, 1, :], io["final_norm_w"].rearrange("(o f) -> o f", o=1).to_broadcast([P, D]))\
             .then_inc(S["ld_fn"], 16)
            wait("ch_pool", 4)
            g.dma_start(BD[0:NE, :], io["moe_b_down"][0]).then_inc(S["ld_bd"], 16)
            src = bass.AP(tensor=mod_d.tensor, offset=3 * D, ap=[[0, P], [1, D]])
            g.dma_start(MB[:, 0, 3, :], src).then_inc(S["ld_fn"], 16)
            g.dma_start(MB[0:NS, 1, 3, :], mod_d[1:9, 3, :]).then_inc(S["ld_fn"], 16)
            wait("lg_ps", 3)
            g.memset(acc, 0.0).then_inc(S["pool_set"], 1)
            wait("s_out", 48)

        @block.scalar
        def _(act):
            a = nc.scalar

            def wait(name, v):
                act.wait_ge(S[name], v)

            def link(ins, k=[0]):
                k[0] += 1
                ins.then_inc(S["ch_act"], 1)
                act.wait_ge(S["ch_act"], k[0])

            act.dma_start(PR1, io["ssd_conv_w"].rearrange("k (c f) -> (k c) f", f=P)).then_inc(S["ld_par"], 16)
            act.dma_start(PR2[0:32, :], io["ssd_conv_b"].rearrange("(c f) -> c f", f=P)).then_inc(S["ld_par"], 16)
            act.dma_start(PR2[32:40, :], io["norm1_w"][0].rearrange("(c f) -> c f", f=P)).then_inc(S["ld_par"], 16)
            act.dma_start(PR2[40:56, :], io["ssd_norm_w"].rearrange("(c f) -> c f", f=P)).then_inc(S["ld_par"], 16)
            act.dma_start(HI, io["state_ssm_conv"].rearrange("s k f -> (s k) f")).then_inc(S["ld_hist"], 16)
            wait("ld_c", 32)
            a.activation(CR, CR, ACT.Silu).then_inc(S["silu_c"], 1)

            def root(at, n, width=3):
                wait("ss_ok", n)
                a.activation(st[:, at:at + width], st[:, at:at + width], ACT.Sqrt, bias=st[:, 15:16], scale=1.0 / D)\
                 .then_inc(S["rt3_ok"], 1)

            root(0, 1)
            wait("par_ps", 1)
            a.copy(cw[:], PS[7][:, 0:128])
            a.copy(pv[:], PS[7][:, 128:184]).then_inc(S["par_ok"], 1)
            wait("hist_ps", 1)
            a.copy(HT[:, 0:16, :].rearrange("p c k -> p (c k)"), PS[6][:, 0:384])
            a.copy(HT[:, 16:32, :].rearrange("p c k -> p (c k)"), PS[7][:, 0:384]).then_inc(S["hist_ok"], 1)
            wait("xnT_ps", 1)
            wait("m1_ok", 1)
            for k in range(4):
                a.activation(h1T[:, k, 0:NP], PS[k // 2][:, 256 * (k % 2):256 * (k % 2) + 256], ACT.Identity,
                             bias=m1[:, 0, k, 0:1], scale=m1[:, 1, k, 0:1]).then_inc(S["h1_act"], 1)
            wait("ld_hs", 32)
            a.activation(hsc[:, 2:3], hsc[:, 1:2], ACT.Exp)
            wait("dt_t", 1)
            a.activation(dtt[1], dtt[1], ACT.Exp).then_inc(S["dt_e"], 1)
            wait("dt_u", 1)
            a.activation(dtt[3], dtt[2], ACT.Ln).then_inc(S["dt_l"], 1)
            wait("dt_ok", 1)
            a.activation(dd[:, 1, :], dtt[1][:, NP:NT], ACT.Exp).then_inc(S["dec_ok"], 1)

            def conv_silu(n):
                c = CHUNKS[n][3]
                wait("conv_done", n + 1)
                a.activation(XB[:, c, 0:NP], CV[:, n % 3, 0:NP], ACT.Silu, bias=pv[:, c:c + 1])
                a.activation(XB[:, c, NP:NT], CV[:, n % 3, 259:SEQC:4], ACT.Silu, bias=pv[:, c:c + 1])\
                 .then_inc(S["silu_done"], 1)

            def scale_states(j):
                s, half = divmod(j, 2)
                act.wait_ge(ld_s[j % NSLOT], 16 * (j // NSLOT + 1))
                if j == 0:
                    wait("s_ddl", 32)
                for c in range(8):
                    i = a.mul(SR[j % NSLOT][:, c, :], SR[j % NSLOT][:, c, :], DDc[:, 8 * half + c, 1, s:s + 1])
                i.then_inc(S["s_scaled"], 1)

            def token_rows(m):
                c, b = divmod(m, 6)
                wait("xtok_ps", m + 1)
                if b >= 4:
                    if m == 10:
                        act.wait_ge(st_s[0], 16 * len(range(0, 16, NSLOT)))
                    i = a.copy(Btok[c][:, 512 * (b - 4):512 * (b - 4) + 512], PS[m % 2])
                else:
                    for h in range(8 * b, 8 * b + 8):
                        i = a.mul(xdt[c][:, HD * h:HD * h + HD], PS[m % 2][:, HD * (h % 8):HD * (h % 8) + HD],
                                  dtok[:, c, h:h + 1])
                i.then_inc(S["xtok_ok"], 1)

            def exp_differences(q):
                wait("lt_ok", q + 1)
                lt = LT[q % GROUPS]
                if q >= GROUPS:
                    link(a.activation(lt, lt, ACT.Relu, scale=-1.0))
                a.activation(lt, lt, ACT.Exp, scale=-1.0 if q >= GROUPS else 1.0).then_inc(S["exp_ok"], 1)

            def exp_decay(c):
                wait("lastx", c + 1)
                a.activation(dcy[:, c, :], dcy[:, c, :], ACT.Exp).then_inc(S["dcy_ok"], 1)

            for n, (u, j, kind, c) in enumerate(CHUNKS):
                wait("chunk_ps", n + 1)
                ps = PS[n % 4][:, 0:NT]
                if kind == "z":
                    if n == NCONV:
                        wait("s_acs", 16)
                        wait("dtTok_ps", 1)
                    if n == NCONV + 4:
                        wait("s_mod", 64)
                    a.activation(SZ[:, c, :], ps, ACT.Silu).then_inc(S["chunk_evac"], 1)
                    if n == NCONV + 15:
                        exp_decay(0)
                        exp_differences(0)
                        exp_differences(1)
                    if n > NCONV:
                        scale_states(n - NCONV - 1)
                    if n == NCONV + 15:
                        token_rows(0)
                        token_rows(1)
                else:
                    if n == 0:
                        wait("consts_dve", 1)
                        wait("s_out", 48)
                    if n >= 4:
                        wait("conv_done", n - 3)
                    a.copy(RW[:, n % 4, 3:3 + NP], ps[:, 0:NP])
                    a.copy(RW[:, n % 4, 262:SEQR:4], ps[:, NP:NT]).then_inc(S["chunk_evac"], 1)
                    if n >= 1:
                        conv_silu(n - 1)
                    if n == NCONV - 1:
                        conv_silu(n)
            scale_states(15)
            for m in range(2, 6):
                token_rows(m)

            def exp_sums(gr):
                if gr >= 2:
                    wait("y_ps", GROUPS + gr - 1)
                a.activation(CTs[gr % 2], bcA[1][:, HPG * gr:HPG * gr + HPG, :], ACT.Exp).then_inc(S["ce_ok"], 1)

            def state_copy(gr):
                wait("st_ps", gr + 1)
                if gr == 0:
                    for r in (3, 4):
                        act.wait_ge(st_s[r], 16 * len(range(r, 16, NSLOT)))
                a.copy(prevT[:, 256 * gr:256 * gr + 256], PS[6 + gr % 2][:, 0:256]).then_inc(S["st_act"], 1)

            def square(gr):
                if gr == 0:
                    wait("samp_ok", 1)
                wait("y_ok", GROUPS + gr + 1)
                if gr >= 2:
                    wait("gn_ps", gr - 1)
                a.activation(sq[gr % 2], SZ[:, 2 * gr:2 * gr + 2, :], ACT.Square).then_inc(S["sq_ok"], 1)

            for gr in range(2, GROUPS):
                exp_differences(gr)
            token_rows(6)
            token_rows(7)
            for gr in range(GROUPS):
                if gr == 5:
                    exp_decay(1)
                    link(a.activation(dec1[:], bcA[1][:, :, CH - 1], ACT.Exp))
                    exp_sums(0)
                    exp_differences(GROUPS)
                state_copy(gr)
                if gr < 4:
                    token_rows(8 + gr)
            for gr in range(1, GROUPS):
                exp_sums(gr)
                exp_differences(GROUPS + gr)
                if gr >= 2:
                    square(gr - 2)
            for gr in (GROUPS - 2, GROUPS - 1):
                square(gr)
            wait("gn_ps", GROUPS)
            a.activation(gnr, PS[0][0:GROUPS, 0:NT], ACT.Sqrt, bias=st[0:GROUPS, 15:16], scale=1.0 / 256)\
             .then_inc(S["gn_rt"], 1)
            for b in range(4):
                wait("hf_ps", b + 1)
                a.copy(xdt[0][:, 512 * b:512 * b + 512], PS[2 + b % 2]).then_inc(S["hf_ok"], 1)
            act.wait_ge(S["hf_ok"], 4)
            act.dma_start(io["new_ssm_prompt"][0].rearrange("h p n -> (h p) n").rearrange("(c q) n -> q c n", q=P),
                          xdt[0].rearrange("p (c n) -> p c n", n=P)).then_inc(S["s_hf"], 16)
            def h2_columns(i, t):
                wait("h2T_ps", i + 1)
                R = ROWS[t]
                if t == 2:
                    ins = a.copy(h2T[:, :, NP:NT], PS[5][:, 0:64].rearrange("p (k r) -> p k r", k=KT))
                else:
                    for b in range(2):
                        ins = a.copy(h2T[:, 4 * b:4 * b + 4, 128 * t:128 * t + R],
                                     PS[(6, 0)[t] + b].rearrange("p (k r) -> p k r", k=4))
                ins.then_inc(S["h2T_ok"], 1)

            def exp_logits(i, t):
                R = ROWS[t]
                wait("rt_m", i + 1)
                a.activation(ex[0:R, 0:4], m8[0:R, 0:4], ACT.Exp, bias=m8[0:R, 7:8]).then_inc(S["rt_e"], 1)

            root(6, 2, 1)
            h2_columns(0, 2)
            root(4, 3, 1)
            exp_logits(0, 2)
            a.activation(st[:, 13:14], st[:, 15:16], ACT.Sqrt)
            h2_columns(1, 0)
            root(5, 4, 1)
            a.activation(st[:, 14:15], st[:, 15:16], ACT.Exp)
            h2_columns(2, 1)
            exp_logits(1, 0)
            exp_logits(2, 1)
            def expert_out(x):
                for nh in range(2):
                    i = a.copy(osb[64 * x:64 * x + 64, 512 * nh:512 * nh + 512], PS[5][64 * nh:64 * nh + 64, :])
                i.then_inc(S["a_o"], 1)

            wait("gath_ps", 1)
            a.copy(hg, PS[2]).then_inc(S["a_hg"], 1)
            wait("hgT_ps", 1)
            a.copy(hgT.rearrange("p c s -> p (c s)"), PS[3]).then_inc(S["a_hgT"], 1)
            wait("moe_ready", 1)
            wait("np_ok", 1)
            npass = act.value_load(npi[0:1, 0:1], min_val=1, max_val=MAXPASS)
            with act.Fori(0, npass * (NE // 2)) as it:
                for x in range(2):
                    f = it * 2 + x
                    if x == 1:
                        act.wait_ge(S["sc_ps"], it * 3 + 3)
                        expert_out(0)
                    act.wait_ge(S["d_g"], f + 1)
                    a.activation(sg, gg, ACT.Sigmoid, scale=ALPHA).then_inc(S["a_sig"], 1)
                    act.wait_ge(S["gath_ps"], f + 2)
                    a.copy(hg, PS[2]).then_inc(S["a_hg"], 1)
                    act.wait_ge(S["actT_ps"], f + 1)
                    a.copy(actT.rearrange("p c s -> p (c s)"), PS[4]).then_inc(S["a_actT"], 1)
                    act.wait_ge(S["hgT_ps"], f + 2)
                    a.copy(hgT.rearrange("p c s -> p (c s)"), PS[3]).then_inc(S["a_hgT"], 1)
                    if x == 0:
                        act.wait_ge(S["dn_used"], it * 4 + 2)
                act.wait_ge(S["swT_ps"], it + 1)
                a.copy(SwT, PS[2][:, 0:3 * P]).then_inc(S["a_swT"], 1)
                act.wait_ge(S["dn_used"], it * 4 + 4)
                expert_out(1)
            for t in range(3):
                root(8 + t, 5 + t, 1)

        @block.tensor
        def _(pe):
            t_ = nc.tensor

            def wait(name, v):
                pe.wait_ge(S[name], v)

            def mm(out, lhsT, rhs, start=True, stop=True):
                return t_.matmul(out, lhsT, rhs, start=start, stop=stop)

            wait("consts_pool", 1)
            wait("silu_c", 1)
            for k in range(KT):
                i = t_.transpose(PS[6][:, 9 * k:9 * k + 9], CR[:, P * k:P * k + P], ident[0:9, 0:9])
            i.then_inc(S["cT_ps"], 1)
            wait("ld_par", 64)
            t_.transpose(PS[7][:, 0:128], PR1, ident[:])
            t_.transpose(PS[7][:, 128:184], PR2, ident[0:56, 0:56]).then_inc(S["par_ps"], 1)
            wait("ld_hist", 16)
            wait("scT_ok", 1)
            wait("par_ok", 1)
            for c in range(NCH):
                i = t_.transpose(PS[6 + c // 16][:, 24 * (c % 16):24 * (c % 16) + 24], HI[:, P * c:P * c + P],
                                 ident[0:24, 0:24])
            i.then_inc(S["hist_ps"], 1)

            def loaded(u):
                pe.wait_ge(ld_w[u % 3], 16 * (u // 3 + 1))

            def ada(u):
                a = UNIT_A.index(u)
                if u == 1:
                    wait("ld_half", 16)
                else:
                    loaded(u)
                if a >= 2:
                    wait("ms_ok", a - 1)
                if a == 1:
                    wait("hist_ok", 1)
                for k in range(KT):
                    if u == 1 and k == KT // 2:
                        loaded(u)
                    for q in range(4):
                        i = t_.matmul(PS[5 + 2 * (a % 2)][32 * q:32 * q + 32, 0:256], scT[:, k, :],
                                      W[u % 3][:, k, 256 * q:256 * q + 256], start=(k == 0), stop=(k == KT - 1),
                                      tile_position=(0, 32 * q))
                i.then_inc(S["ada_ps"], 1)

            wait("xn_ok", 3)
            for k in range(KT):
                for t in range(2):
                    t_.transpose(PS[k // 2][:, 256 * (k % 2) + 128 * t:256 * (k % 2) + 128 * t + 128],
                                 xn[:, t, P * k:P * k + P], ident[:])
            for k in range(KT):
                i = t_.transpose(PS[4][:, 8 * k:8 * k + 8], xn[0:NS, 2, P * k:P * k + P], ident[0:NS, 0:NS])
            i.then_inc(S["xnT_ps"], 1)
            ada(0)
            ada(1)
            wait("ms_ok", 2)
            wait("hist_ok", 1)
            for u in range(2):
                for hf in range(2):
                    i = t_.transpose(PS[6][:, 128 * (2 * u + hf):128 * (2 * u + hf) + 128],
                                     MS[:, u, 128 * hf:128 * hf + 128], ident[:])
            i.then_inc(S["m1_ps"], 1)
            wait("ld_wdt", 16)
            for k in range(KT):
                wait("h1_act", min(k + 1, 4))
                wait("h1_dve", max(k - 2, 1))
                i = mm(PS[7][0:32, 0:NT], WDT[:, k, :], h1T[:, k, :], k == 0, k == KT - 1)
            i.then_inc(S["dt_ps"], 1)
            n = 0
            for u, (kind, col) in enumerate(UNITS):
                if u < 2:
                    continue
                if u == 11:
                    wait("bcT_ok", 1)
                    wait("conv_done", NCONV)
                    for q in range(4):
                        i = t_.transpose(PS[4][0:88, P * q:P * q + P],
                                         TT[:, q, :, :].rearrange("p t c -> p (t c)"), ident[:])
                    i.then_inc(S["tl_ps"], 1)
                if kind == ADA:
                    ada(u)
                else:
                    if u == 2:
                        wait("ld_cols", 16)
                    else:
                        loaded(u)
                    for _ in range(8):
                        j = CHUNKS[n][1]
                        if u == 2 and j == 4:
                            loaded(u)
                        if n >= 4:
                            wait("chunk_evac", n - 3)
                        for k in range(KT):
                            i = mm(PS[n % 4][:, 0:NT], W[u % 3][:, k, P * j:P * j + P], h1T[:, k, :],
                                   k == 0, k == KT - 1)
                        i.then_inc(S["chunk_ps"], 1)
                        n += 1
                if u == 2:
                    wait("dt_ok", 1)
                    for q in range(4):
                        i = t_.transpose(PS[4][:, 32 * q:32 * q + 32], dtt[q // 2][:, CH * (q % 2):CH * (q % 2) + CH],
                                         ident[0:32, 0:32])
                    i.then_inc(S["dtTok_ps"], 1)
                if u == 4:
                    wait("dtok_ok", 1)
                    for c in range(2):
                        mm(PS[6][:, 32 * c:32 * c + 32], utri[:], dtok[:, 2 + c, :])
                    for c in range(2):
                        i = mm(PS[6][0:32, 128 + 128 * c:256 + 128 * c], dtok[:, 2 + c, :], utri[:])
                    i.then_inc(S["acs_ps"], 1)
                if u == 6:
                    wait("bcs_ok", 1)
                    t_.transpose(PS[4][:, 0:128], bcs, ident[:]).then_inc(S["bcs_ps"], 1)

            def cb(q):
                c, gr = divmod(q, GROUPS)
                if q >= 2:
                    wait("mt_ok", q - 1)
                i = mm(PS[2 + q % 2][:, 0:CH], XB[:, XC + gr, CH * c:CH * c + CH],
                       XB[:, XC + GC + gr, CH * c:CH * c + CH])
                i.then_inc(S["cb_ps"], 1)

            def square_sums(gr):
                wait("sq_ok", gr + 1)
                for m in range(2):
                    i = mm(PS[0][0:GROUPS, 0:NT], onecol[:, GROUPS - 1 - gr:2 * GROUPS - 1 - gr], sq[gr % 2][:, m, :],
                           gr == 0 and m == 0, gr == GROUPS - 1 and m == 1)
                i.then_inc(S["gn_ps"], 1)

            def turn_tokens(m):
                c, b = divmod(m, 6)
                if m == 0:
                    wait("chunk_evac", 48)
                if m >= 2:
                    wait("xtok_ok", m - 1)
                first = XC if b >= 4 else 0
                for r in range(4):
                    i = t_.transpose(PS[m % 2][:, P * r:P * r + P],
                                     XB[:, first + 4 * (b % 4) + r, CH * c:CH * c + CH], ident[:])
                i.then_inc(S["xtok_ps"], 1)

            for m in range(6):
                turn_tokens(m)
            for m in (6, 7):
                turn_tokens(m)
            cb(0)
            for c in range(2):
                for gr in range(GROUPS):
                    q = c * GROUPS + gr
                    if q + 1 < 16:
                        cb(q + 1)
                    if c == 1:
                        wait("st_act", gr + 1)
                    if q in (0, 4):
                        wait("diag_ok", q // 4 + 1)
                    if q == 0:
                        wait("tl_ok", 1)
                    if q >= 2:
                        wait("y_ok", q - 1)
                    for pair in range(2):
                        cc = 2 * gr + pair
                        mm(PS[4 + q % 2][:, CH * pair:CH * pair + CH], diagD[cc // 8][:, cc % 8, :],
                           XB[:, cc, CH * c:CH * c + CH], pair == 0, False)
                    wait("mt_ok", q + 1)
                    if c == 1:
                        wait("cts_ok", gr + 1)
                    if gr == 0:
                        wait("xtok_ok", 6 * c + 6)
                    for pair in range(2):
                        for r in (2 * pair, 2 * pair + 1):
                            h = HPG * gr + r
                            out = PS[4 + q % 2][64 * (r % 2):64 * (r % 2) + 64, CH * pair:CH * pair + CH]
                            i = mm(out, xdt[c][:, HD * h:HD * h + HD], LT[gr][:, r, :], False, c == 0 and pair == 1)
                            if c == 1:
                                i = mm(out, prevT[:, HD * h:HD * h + HD], CTs[gr % 2][:, r, :], False, pair == 1)
                    i.then_inc(S["y_ps"], 1)
                    if gr % 2 == 0:
                        wait("xdec_ok", 4 * c + gr // 2 + 1)
                    if q == 0:
                        wait("samp_ok", 1)
                    if q >= 10:
                        wait("st_ok", q - 9)
                    elif q >= 2:
                        wait("st_act", q - 1)
                    mm(PS[6 + q % 2][:, 0:256], Btok[c][:, P * gr:P * gr + P], xdec[c][:, 256 * gr:256 * gr + 256])\
                        .then_inc(S["st_ps"], 1)
                    if q < 4:
                        turn_tokens(8 + q)
                    if c == 1 and gr >= 2:
                        square_sums(gr - 2)
            for gr in (GROUPS - 2, GROUPS - 1):
                square_sums(gr)
            wait("st_ok", GROUPS)
            for b in range(4):
                if b >= 2:
                    wait("hf_ok", b - 1)
                for m in range(4):
                    i = t_.transpose(PS[2 + b % 2][:, P * m:P * m + P],
                                     prevT[:, 512 * b + P * m:512 * b + P * m + P], ident[:])
                i.then_inc(S["hf_ps"], 1)

            def group_scale(gr):
                if gr >= 3:
                    wait("gn_ok", gr - 2)
                mm(PS[5 + gr % 3][:, 0:NT], gsel[:, gr, :], gnr).then_inc(S["gn_bc"], 1)

            wait("gn_rc", 1)
            for gr in range(3):
                group_scale(gr)
            wait("hf_ok", 4)

            def project(k, t):
                w = W[2] if k < 8 else W[0]
                for nh in range(2):
                    ins = mm(PS[2 * t + nh], SZ[:, k, CH * t:CH * t + CH], w[:, k % 8, 512 * nh:512 * nh + 512],
                             k == 0, k == XC - 1)
                if k == XC - 1:
                    ins.then_inc(S["wo_ps"], 1)

            def project_samples(half):
                w = W[2] if half == 0 else W[0]
                for k8 in range(8):
                    k = 8 * half + k8
                    for q in range(4):
                        i = t_.matmul(PS[4][32 * q:32 * q + NS, 0:256], SZ[:, k, NP:NT], w[:, k8, 256 * q:256 * q + 256],
                                      start=(k == 0), stop=(k == XC - 1), tile_position=(0, 32 * q))
                i.then_inc(S["wo_ps"], 1)

            def h2_turn(i, t):
                R = ROWS[t]
                wait("h2_ok", i + 1)
                for k in range(KT):
                    if i == 2 and k == KT // 2:
                        wait("h2_ok", 4)
                    out = PS[5][:, 8 * k:8 * k + 8] if t == 2 else PS[(6, 0)[t] + k // 4][:, P * (k % 4):P * (k % 4) + R]
                    ins = t_.transpose(out, h2[0:R, t, P * k:P * k + P], ident[0:R, 0:R])
                ins.then_inc(S["h2T_ps"], 1)

            def logits(i, t):
                R = ROWS[t]
                wait("h2T_ok", i + 1)
                if i == 2:
                    wait("rt_m", 1)
                for k in range(KT):
                    ins = mm(PS[(5, 4, 4)[t]][0:R, 32 * t:32 * t + 32], h2T[:, k, CH * t:CH * t + R], RWt[:, k, :],
                             k == 0, k == KT - 1)
                ins.then_inc(S["lg_ps"], 1)

            pe.wait_ge(ld_wo[0], 16)
            for k in range(8):
                wait("gn_ok", k // 2 + 1)
                for t in range(2):
                    project(k, t)
                if k % 2 == 1 and k // 2 + 3 < GROUPS:
                    group_scale(k // 2 + 3)
            project_samples(0)
            pe.wait_ge(ld_wo[1], 16)
            group_scale(GROUPS - 1)
            wait("gn_ok", GROUPS)
            project_samples(1)
            for k in range(8, XC):
                project(k, 0)
            h2_turn(0, 2)
            for nh in range(2):
                for k in range(8, XC):
                    i = mm(PS[2 + nh], SZ[:, k, CH:2 * CH], W[0][:, k - 8, 512 * nh:512 * nh + 512], False, k == XC - 1)
                    if nh == 1 and k == 11:
                        wait("ld_rt", 32)
                        logits(0, 2)
                        h2_turn(1, 0)
                i.then_inc(S["wo_ps"], 1)
            logits(1, 0)
            h2_turn(2, 1)
            logits(2, 1)
            wait("rt_k", 3)
            for t in range(3):
                R = ROWS[t]
                for t2 in range(t):
                    mm(PS[6][0:R, 32 * t:32 * t + 32], ones[:, 0:R], mask[:, t2, :], t2 == 0, False)
                mm(PS[6][0:R, 32 * t:32 * t + 32], utri[0:R, 0:R], mask[0:R, t, :], t == 0, True)
            for t in range(3):
                R = ROWS[t]
                i = mm(PS[6][0:1, 96:128], ones[0:R, 0:1], mask[0:R, t, :], t == 0, t == 2)
            i.then_inc(S["pos_ps"], 1)
            def gather(x):
                for t in range(3):
                    for hf in range(2):
                        i = mm(PS[2][64 * hf:64 * hf + 64, :], G[x][:, t, :], h2[:, t, 512 * hf:512 * hf + 512],
                               t == 0, t == 2)
                i.then_inc(S["gath_ps"], 1)

            def turn_rows():
                for c in range(4):
                    i = t_.transpose(PS[3][:, P * c:P * c + P], hg[:, P * c:P * c + P], ident[:])
                i.then_inc(S["hgT_ps"], 1)

            def scatter(it, t):
                pe.wait_ge(S["d_add"], it * 3 + (t + 1))
                for nh in range(2):
                    i = mm(PS[6 + nh], SwT[:, P * t:P * t + P], osb[:, 512 * nh:512 * nh + 512])
                i.then_inc(S["sc_ps"], 1)

            wait("d_G", 1)
            gather(0)
            wait("a_hg", 1)
            turn_rows()
            wait("moe_ready", 1)
            wait("np_ok", 1)
            npass = pe.value_load(npi[0:1, 0:1], min_val=1, max_val=MAXPASS)
            wait("pool_set", 2)
            wait("ld_br", 16)
            wait("ld_bd", 16)
            with pe.Fori(0, npass * (NE // 2)) as it:
                for x in range(2):
                    f = it * 2 + x
                    pe.wait_ge(S["d_bs"], f + 1)
                    pe.wait_ge(S["a_hgT"], f + 1)
                    pe.wait_ge(S["d_guf"], f + 1)
                    for n2 in range(2):
                        for hf in range(2):
                            mm(PGU[64 * hf:64 * hf + 64, n2, :], bsel[x],
                               BR[:, 1024 * hf + 512 * n2:1024 * hf + 512 * n2 + 512], True, False)
                    for j in range(4):
                        pe.wait_ge(gu_ld[j], f * 16 + 16)
                        for k in (2 * j, 2 * j + 1):
                            for n2 in range(2):
                                for hf in range(2):
                                    i = mm(PGU[64 * hf:64 * hf + 64, n2, :],
                                           hgT[:, k % 4, 64 * (k // 4):64 * (k // 4) + 64],
                                           BIG[:, 2 * k + hf, 512 * n2:512 * n2 + 512], False, k == KT - 1)
                        i.then_inc(S["gu_used"], 1)
                        if x == 1 and j == 1:
                            scatter(it, 2)
                    pe.wait_ge(S["d_G"], f + 2)
                    pe.wait_ge(S["a_swT"], it + 1)
                    gather(1 - x)
                    if x == 0:
                        pe.wait_ge(S["a_o"], it * 2 + 1)
                        scatter(it, 0)
                    pe.wait_ge(S["d_act"], f + 1)
                    for c in range(4):
                        i = t_.transpose(PS[4][:, P * c:P * c + P], aa[:, P * c:P * c + P], ident[:])
                    i.then_inc(S["actT_ps"], 1)
                    pe.wait_ge(S["a_hg"], f + 2)
                    turn_rows()
                    if x == 1:
                        pe.wait_ge(S["d_gw"], it * 2 + 2)
                        for t in range(3):
                            i = t_.transpose(PS[2][:, P * t:P * t + P], Gw[:, t, :, :].rearrange("p d j -> p (d j)"),
                                             ident[:])
                        i.then_inc(S["swT_ps"], 1)
                    pe.wait_ge(S["a_actT"], f + 1)
                    pe.wait_ge(S["a_o"], f + 1)
                    for nh in range(2):
                        mm(PS[5][64 * nh:64 * nh + 64, :], bsel[x], BD[:, 512 * nh:512 * nh + 512], True, False)
                    for j in range(2):
                        pe.wait_ge(dn_ld[j], f * 16 + 16)
                        for k in range(4 * j, 4 * j + 4):
                            for nh in range(2):
                                i = mm(PS[5][64 * nh:64 * nh + 64, :],
                                       actT[:, k % 4, 64 * (k // 4):64 * (k // 4) + 64],
                                       BIG[:, 16 + k, 512 * nh:512 * nh + 512], False, k == KT - 1)
                        i.then_inc(S["dn_used"], 1)
                    if x == 0:
                        scatter(it, 1)
            pe.wait_ge(S["a_o"], npass * NE + 1)
            pe.wait_ge(S["a_swT"], npass * (NE // 2) + 1)
            pe.wait_ge(S["a_hgT"], npass * NE + 1)
            pe.wait_ge(S["d_add"], npass * (3 * NE // 2) + 1)
            for t in range(3):
                for nh in range(2):
                    i = mm(last_bank(t, nh), SwT[:, P * t:P * t + P], osb[:, 512 * nh:512 * nh + 512])
                i.then_inc(S["sc_ps"], 1)

        @block.vector
        def _(dve):
            v = nc.vector

            def wait(name, val):
                dve.wait_ge(S[name], val)

            k_ = [0]

            def link(ins):
                k_[0] += 1
                ins.then_inc(S["ch_dve"], 1)
                dve.wait_ge(S["ch_dve"], k_[0])

            v.memset(AB, 0.0)
            v.memset(scT[:], 0.0)
            v.memset(RW[:, :, 0:3], 0.0).then_inc(S["consts_dve"], 1)
            wait("ld_x", 32)

            def rstd(x, at, jk, n):
                for t in range(3):
                    R = ROWS[t]
                    i = v.tensor_tensor_reduce(jk[0:R, :], x[0:R, t, :], x[0:R, t, :], 1.0, 0.0, ALU.mult, ALU.add,
                                               st[0:R, at + t:at + t + 1])
                    if t < 2:
                        link(i)
                i.then_inc(S["ss_ok"], 1)
                wait("rt3_ok", n)
                link(v.reciprocal(st[:, at:at + 3], st[:, at:at + 3]))

            link(v.memset(st[:], 1.0))
            link(v.memset(st[:, 15:16], EPS))
            rstd(XT, 0, junk, 1)
            for t in range(3):
                R = ROWS[t]
                v.tensor_scalar(xn[0:R, t, :], XT[0:R, t, :], st[0:R, t:t + 1], None, ALU.mult).then_inc(S["xn_ok"], 1)
            wait("cT_ps", 1)
            v.tensor_copy(scT[:, :, 0:9], PS[6][:, 0:72].rearrange("p (k r) -> p k r", k=KT)).then_inc(S["scT_ok"], 1)

            def mod_rows(a):
                if a == 0:
                    wait("ld_ab", 64)
                wait("ada_ps", a + 1)
                v.tensor_tensor(MS[:, a, :], PS[5 + 2 * (a % 2)][:, 0:256], AB[:, a, :], ALU.add)\
                 .then_inc(S["ms_ok"], 1)

            mod_rows(0)
            mod_rows(1)
            wait("m1_ps", 1)
            wait("par_ok", 1)
            src = PS[6].rearrange("p (u hf q r) -> p u hf q r", u=2, hf=2, q=4)
            for u in range(2):
                for hf in range(2):
                    i = v.tensor_copy(m1[:, u, hf::2, :], src[:, u, hf, :, 0:9])
            link(i)
            link(v.tensor_scalar(m1[:, 1, :, :], m1[:, 1, :, :], 1.0, None, ALU.add))
            v.tensor_tensor(m1[:, 1, :, :], m1[:, 1, :, :], pv[:, 32:40].unsqueeze(2).to_broadcast([P, KT, 9]),
                            ALU.mult).then_inc(S["m1_ok"], 1)
            dve.wait_ge(S["m1_ok"], 1)
            wait("xnT_ps", 1)
            hs = h1T[:, :, NP:NT]
            link(v.tensor_tensor(hs, PS[4][:, 0:64].rearrange("p (k s) -> p k s", k=KT), m1[:, 1, :, 1:9], ALU.mult))
            v.tensor_tensor(hs, hs, m1[:, 0, :, 1:9], ALU.add).then_inc(S["h1_dve"], 1)
            for k in range(4, KT):
                v.tensor_scalar(h1T[:, k, 0:NP], PS[k // 2][:, 256 * (k % 2):256 * (k % 2) + 256],
                                m1[:, 1, k, 0:1], m1[:, 0, k, 0:1], ALU.mult, ALU.add).then_inc(S["h1_dve"], 1)
            wait("dt_ps", 1)
            wait("ld_hs", 32)
            link(v.tensor_scalar(dtt[0], PS[7][0:32, 0:NT], hsc[:, 0:1], None, ALU.add))
            v.scalar_tensor_tensor(dtt[1], dtt[0], -1.0, dtt[0], ALU.mult, ALU.min).then_inc(S["dt_t"], 1)
            wait("dt_e", 1)
            v.tensor_scalar(dtt[2], dtt[1], 1.0, None, ALU.add).then_inc(S["dt_u"], 1)
            wait("dt_l", 1)
            link(v.tensor_scalar(dtt[2], dtt[2], -1.0, None, ALU.add))
            tz = xn[0:32, 0, 0:NT]
            wait("xnT_ps", 1)
            link(v.tensor_scalar(tz, dtt[2], 0.0, None, ALU.is_equal))
            link(v.tensor_tensor(dtt[2], dtt[2], tz, ALU.add))
            link(v.reciprocal(dtt[2], dtt[2]))
            link(v.tensor_tensor(dtt[2], dtt[1], dtt[2], ALU.mult))
            link(v.tensor_tensor(dtt[3], dtt[3], dtt[2], ALU.mult))
            link(v.tensor_tensor(dtt[1], dtt[1], tz, ALU.mult))
            link(v.tensor_tensor(dtt[3], dtt[3], dtt[1], ALU.add))
            link(v.tensor_scalar(hsc[:, 3:4], hsc[:, 2:3], -1.0, None, ALU.mult))
            link(v.scalar_tensor_tensor(dtt[0], dtt[0], 0.0, dtt[3], ALU.max, ALU.add))
            v.tensor_scalar(dtt[1], dtt[0], hsc[:, 3:4], None, ALU.mult).then_inc(S["dt_ok"], 1)
            wait("dec_ok", 1)
            v.tensor_copy(dd[:, 0, :], dtt[0][:, NP:NT]).then_inc(S["dd_ok"], 1)
            wait("ld_D", 16)
            v.tensor_copy(Dcol[0:64, :], Dbc[0:64, 0::2])
            link(v.tensor_copy(Dcol[64:128, :], Dbc[64:128, 1::2]))
            wait("hist_ok", 1)

            for n in range(NCONV):
                u, j, _, c = CHUNKS[n]
                if n in (8, 16, 24):
                    mod_rows(1 + n // 8)
                raw = RW[:, n % 4, :]
                wait("chunk_evac", n + 1)
                link(v.tensor_copy(raw[:, 259:SEQR].rearrange("p (s k) -> p s k", k=4)[:, :, 0:3],
                                   HT[:, c, :].rearrange("p (s k) -> p s k", k=3)))
                if n >= 3:
                    wait("silu_done", n - 2)
                link(v.tensor_scalar(CV[:, n % 3, :], raw[:, 0:SEQC], cw[:, c:c + 1], None, ALU.mult))
                for k in range(1, CONV):
                    i = v.scalar_tensor_tensor(CV[:, n % 3, :], raw[:, k:k + SEQC], cw[:, NCH * k + c:NCH * k + c + 1],
                                               CV[:, n % 3, :], ALU.mult, ALU.add)
                    if k < CONV - 1:
                        link(i)
                    if k == 1:
                        v.tensor_copy(TT[:, c // 8, 0:3, c % 8], raw[:, NP:NP + 3])
                        v.tensor_copy(TT[:, c // 8, 3:11, c % 8], raw[:, 262:SEQR:4])
                i.then_inc(S["conv_done"], 1)
                if n == 9:
                    wait("dtTok_ps", 1)
                    v.tensor_copy(dtok[:].rearrange("p a b -> p (a b)"), PS[4][:, 0:128]).then_inc(S["dtok_ok"], 1)
                if n == 17:
                    wait("acs_ps", 1)
                    v.tensor_copy(acst[:].rearrange("p a b -> p (a b)"), PS[6][:, 0:64])
                    v.tensor_copy(acsT, PS[6][0:32, 128:384].rearrange("p (c l) -> p c l", c=2))\
                     .then_inc(S["acs_ok"], 1)
                    wait("silu_done", 16)
                    dve.wait_ge(S["acs_ok"], 1)
                    v.tensor_copy(bcs.rearrange("p (s j) -> p s j", j=16),
                                  XB[:, XC:NCH, NP:NT].rearrange("p j s -> p s j")).then_inc(S["bcs_ok"], 1)
                if n == 25:
                    wait("bcs_ps", 1)
                    v.tensor_copy(bcT, PS[4][:, 0:128]).then_inc(S["bcT_ok"], 1)
            mod_rows(5)
            wait("silu_done", NCONV)
            wait("s_ddl", 32)
            link(v.tensor_tensor(xdtS[:], XB[:, 0:XC, NP:NT], DDc[:, :, 0, :], ALU.mult))
            wait("m1_ok", 1)
            junkp = [PS[6], PS[7]]
            for j in range(16):
                s, half = divmod(j, 2)
                if half == 0:
                    dve.wait_ge(ld_bcb[s % 2], 16 * (s // 2 + 1))
                wait("s_scaled", j + 1)
                for c in range(8):
                    cc = 8 * half + c
                    i = v.scalar_tensor_tensor(SR[j % NSLOT][:, c, :], BCb[s % 2][:, cc // 2, :], xdtS[:, cc, s:s + 1],
                                               SR[j % NSLOT][:, c, :], ALU.mult, ALU.add)
                link(i)
                for c in range(8):
                    cc = 8 * half + c
                    i = v.tensor_tensor_reduce(junkp[c // 4][:, P * (c % 4):P * (c % 4) + P], SR[j % NSLOT][:, c, :],
                                               BCb[s % 2][:, 8 + cc // 2, :], 1.0, 0.0, ALU.mult, ALU.add,
                                               yS[:, cc, s:s + 1])
                i.then_inc(S["item_done"], 1)
                dve.wait_ge(S["item_done"], j + 1)
                if j == 10:
                    wait("tl_ps", 1)
                    v.tensor_copy(TLs.rearrange("p u f -> p (u f)"), PS[4][0:88, :]).then_inc(S["tl_ok"], 1)
            link(v.tensor_tensor(xdtS[:], XB[:, 0:XC, NP:NT], Dcol[:].unsqueeze(2).to_broadcast([P, XC, NS]), ALU.mult))
            link(v.tensor_tensor(yS[:], yS[:], xdtS[:], ALU.add))
            wait("chunk_evac", 48)
            v.tensor_tensor(SZ[:, :, NP:NT], yS[:], SZ[:, :, NP:NT], ALU.mult).then_inc(S["samp_ok"], 1)

            def y_rows(q):
                c, gr = divmod(q, GROUPS)
                wait("y_ps", q + 1)
                z = SZ[:, 2 * gr:2 * gr + 2, CH * c:CH * c + CH]
                v.tensor_tensor(z, PS[4 + q % 2][:, 0:256].rearrange("p (m l) -> p m l", m=2), z, ALU.mult)\
                 .then_inc(S["y_ok"], 1)

            def state_after(q):
                gr = q - GROUPS
                wait("st_ps", q + 1)
                pr = prevT[:, 256 * gr:256 * gr + 256]
                p3 = pr.rearrange("p (h d) -> p h d", d=HD)
                link(v.tensor_tensor(p3, p3, dec1[:, HPG * gr:HPG * gr + HPG].unsqueeze(2)
                                     .to_broadcast([P, HPG, HD]), ALU.mult))
                v.tensor_tensor(pr, pr, PS[6 + q % 2][:, 0:256], ALU.add).then_inc(S["st_ok"], 1)

            for c in range(2):
                for gr in range(GROUPS):
                    q = c * GROUPS + gr
                    wait("cb_ps", q + 1)
                    link(v.tensor_tensor(CBm[q % 2], PS[2 + q % 2][:, 0:CH], utri[:], ALU.mult))
                    wait("exp_ok", q + 1)
                    v.tensor_tensor(LT[gr], LT[gr], CBm[q % 2].unsqueeze(1).to_broadcast([P, HPG, CH]),
                                    ALU.mult).then_inc(S["mt_ok"], 1)
                    if c == 1:
                        wait("ce_ok", gr + 1)
                        v.tensor_tensor(CTs[gr % 2], CTs[gr % 2],
                                        XB[:, XC + GC + gr, CH:2 * CH].unsqueeze(1).to_broadcast([P, HPG, CH]),
                                        ALU.mult).then_inc(S["cts_ok"], 1)
                    if q >= 1:
                        y_rows(q - 1)
                    if q > GROUPS:
                        state_after(q - 1)
            y_rows(15)
            state_after(15)
            v.tensor_copy(gsel, ident[0:GROUPS, 0:GROUPS].unsqueeze(2).to_broadcast([GROUPS, GROUPS, P]))
            wait("gn_rt", 1)
            v.reciprocal(gnr, gnr).then_inc(S["gn_rc"], 1)
            dve.wait_ge(S["y_ok"], 16)
            for gr in range(GROUPS):
                wait("gn_bc", gr + 1)
                for m in range(2):
                    i = v.scalar_tensor_tensor(SZ[:, 2 * gr + m, :], SZ[:, 2 * gr + m, :],
                                               pv[:, 40 + 2 * gr + m:41 + 2 * gr + m], PS[5 + gr % 3][:, 0:NT],
                                               ALU.mult, ALU.mult)
                i.then_inc(S["gn_ok"], 1)
            wait("s_mb", 32)
            wait("ld_n2", 16)
            v.scalar_tensor_tensor(MB[:, 0, 2, :], MB[:, 0, 2, :], 1.0, n2b, ALU.add, ALU.mult)
            link(v.scalar_tensor_tensor(MB[0:NS, 1, 2, :], MB[0:NS, 1, 2, :], 1.0, n2b[0:NS, :], ALU.add, ALU.mult))

            def mix(i, t):
                R = ROWS[t]
                q = t // 2
                wait("wo_ps", i + 2)
                if t == 2:
                    for c in range(4):
                        ins = v.tensor_copy(scr[0:NS, 256 * c:256 * c + 256], PS[4][32 * c:32 * c + NS, 0:256])
                    link(ins)
                    link(v.tensor_tensor(scr[0:NS, :], scr[0:NS, :], MB[0:NS, 1, 0, :], ALU.mult))
                    link(v.tensor_tensor(XT[0:NS, 2, :], XT[0:NS, 2, :], scr[0:NS, :], ALU.add))
                else:
                    for nh in range(2):
                        ins = v.tensor_tensor(PS[2 * t + nh], PS[2 * t + nh], MB[:, 0, 0, 512 * nh:512 * nh + 512],
                                              ALU.mult)
                    link(ins)
                    for nh in range(2):
                        xx = XT[:, t, 512 * nh:512 * nh + 512]
                        ins = v.tensor_tensor(xx, xx, PS[2 * t + nh], ALU.add)
                    link(ins)
                v.tensor_tensor_reduce(scr[0:R, :], XT[0:R, t, :], XT[0:R, t, :], 1.0, 0.0, ALU.mult, ALU.add,
                                       st[0:R, 4 + t:5 + t]).then_inc(S["ss_ok"], 1)
                wait("rt3_ok", i + 2)
                link(v.reciprocal(st[0:R, 4 + t:5 + t], st[0:R, 4 + t:5 + t]))
                link(v.scalar_tensor_tensor(h2[0:R, t, :], XT[0:R, t, :], st[0:R, 4 + t:5 + t], MB[0:R, q, 2, :],
                                            ALU.mult, ALU.mult))
                v.tensor_tensor(h2[0:R, t, :], h2[0:R, t, :], MB[0:R, q, 1, :], ALU.add).then_inc(S["h2_ok"], 1)

            def route(i, t):
                R = ROWS[t]
                wait("lg_ps", i + 1)
                link(v.tensor_tensor(lg[0:R, :], PS[(5, 4, 4)[t]][0:R, 32 * t:32 * t + 32], rb[0:R, :], ALU.add))
                link(v.max(m8[0:R, :], lg[0:R, :]))
                link(v.max_index(ix[0:R, :], m8[0:R, :], lg[0:R, :]))
                v.tensor_scalar(m8[0:R, 7:8], m8[0:R, 0:1], -1.0, None, ALU.mult).then_inc(S["rt_m"], 1)
                link(v.tensor_copy(ixf[0:R, :], ix[0:R, :]))
                for k in range(TOPK):
                    ins = v.tensor_scalar(oh[0:R, k, :], iota[0:R, 0:NE], ixf[0:R, k:k + 1], None, ALU.is_equal)
                link(ins)
                v.tensor_reduce(mask[0:R, t, :], oh[0:R, :, :].rearrange("p k e -> p e k"), AX.X, ALU.add)\
                 .then_inc(S["rt_k"], 1)
                wait("rt_e", i + 1)
                link(v.tensor_reduce(ex[0:R, 4:5], ex[0:R, 0:4], AX.X, ALU.add))
                link(v.reciprocal(ex[0:R, 4:5], ex[0:R, 4:5]))
                link(v.tensor_scalar(ex[0:R, 0:4], ex[0:R, 0:4], ex[0:R, 4:5], None, ALU.mult))
                for k in range(TOPK):
                    ins = v.tensor_scalar(pw[0:R, k, :], iota[0:R, 0:NE], ixf[0:R, k:k + 1], ex[0:R, k:k + 1],
                                          ALU.is_equal, ALU.mult)
                link(ins)
                v.tensor_reduce(comb[0:R, :, t], pw[0:R, :, :].rearrange("p k e -> p e k"), AX.X, ALU.add)\
                 .then_inc(S["rt_p"], 1)
                dve.wait_ge(S["rt_p"], i + 1)

            wait("ld_rt", 32)
            wait("pool_set", 1)
            mix(0, 2)
            mix(1, 0)
            route(0, 2)
            for nh in range(2):
                wait("wo_ps", 4 + nh)
                xx = XT[:, 1, 512 * nh:512 * nh + 512]
                link(v.tensor_tensor(PS[2 + nh], PS[2 + nh], MB[:, 0, 0, 512 * nh:512 * nh + 512], ALU.mult))
                link(v.tensor_tensor(xx, xx, PS[2 + nh], ALU.add))
                link(v.tensor_tensor_reduce(scr[:, 0:512], xx, xx, 1.0, 0.0, ALU.mult, ALU.add,
                                            st[:, (12, 5)[nh]:(13, 6)[nh]]))
            v.tensor_tensor(st[:, 5:6], st[:, 5:6], st[:, 12:13], ALU.add).then_inc(S["ss_ok"], 1)
            wait("rt3_ok", 4)
            link(v.reciprocal(st[:, 5:6], st[:, 5:6]))
            for nh in range(2):
                cols = slice(512 * nh, 512 * nh + 512)
                link(v.scalar_tensor_tensor(h2[:, 1, cols], XT[:, 1, cols], st[:, 5:6], MB[:, 0, 2, cols],
                                            ALU.mult, ALU.mult))
                v.tensor_tensor(h2[:, 1, cols], h2[:, 1, cols], MB[:, 0, 1, cols], ALU.add).then_inc(S["h2_ok"], 1)
            route(1, 0)
            route(2, 1)
            wait("pos_ps", 1)
            for t in range(3):
                R = ROWS[t]
                i = v.tensor_tensor(mask[0:R, t, :], mask[0:R, t, :], PS[6][0:R, 32 * t:32 * t + 32], ALU.mult)
            link(i)

            def places(p_):
                for t in range(3):
                    R = ROWS[t]
                    ins = v.tensor_scalar(posx[0:R, NE * p_:NE * p_ + NE, t], mask[0:R, t, :], -1.0 - CAP * p_, None,
                                          ALU.add)
                link(ins)

            places(0)

            def gather_matrix(x, i):
                return v.tensor_tensor(G[x], iota[:].unsqueeze(1).to_broadcast([P, 3, CAP]),
                                       posx[:, bass.ds(i, 1), :].rearrange("p o t -> p (o t)").unsqueeze(2)
                                       .to_broadcast([P, 3, CAP]), ALU.is_equal)

            def bias_select(x, e):
                return v.tensor_copy(bsel[x], eye[:, bass.ds(e, 1)].to_broadcast([P, 64]))

            gather_matrix(0, 0).then_inc(S["d_G"], 1)
            for p_ in range(1, MAXPASS):
                places(p_)
            wait("pool_set", 2)
            bias_select(0, 0).then_inc(S["d_bs"], 1)
            link(v.tensor_reduce(cnt[:, 0:1], PS[6][0:1, 96:128], AX.X, ALU.max))
            link(v.tensor_scalar(cnt[:, 1:5], thr[:], cnt[:, 0:1], None, ALU.is_lt))
            link(v.tensor_reduce(cnt[:, 5:6], cnt[:, 1:5], AX.X, ALU.add))
            v.tensor_scalar(npi[:], cnt[:, 5:6], 1.0, None, ALU.add).then_inc(S["np_ok"], 1)
            v.tensor_copy(cnt[:, 6:7], cnt[:, 5:6]).then_inc(S["moe_ready"], 1)
            for nm in ("d_guf", "d_add", "a_o", "a_swT"):
                dve.sem_inc(S[nm], 1)
            wait("pool_set", 3)
            wait("np_ok", 1)
            wait("moe_ready", 1)
            npass = dve.value_load(npi[0:1, 0:1], min_val=1, max_val=MAXPASS)
            flat = PGU[:, :, :].rearrange("p a b -> p (a b)")

            def adds(it, t):
                dve.wait_ge(S["sc_ps"], it * 3 + (t + 1))
                R = ROWS[t]
                for nh in range(2):
                    y = acc[0:R, t, 512 * nh:512 * nh + 512]
                    i = v.tensor_tensor(y, y, PS[6 + nh][0:R, :], ALU.add)
                i.then_inc(S["d_add"], 1)

            with dve.Fori(0, npass) as ps:
                with dve.Fori(0, NE // 2) as pair:
                    it = ps * (NE // 2) + pair
                    for x in range(2):
                        f = it * 2 + x
                        gather_matrix(1 - x, f + 1).then_inc(S["d_G"], 1)
                        dve.wait_ge(S["gu_used"], f * 4 + 4)
                        v.tensor_scalar(gg, flat[:, 0::2], LIMIT, None, ALU.min).then_inc(S["d_g"], 1)
                        v.tensor_scalar(uu, flat[:, 1::2], -LIMIT, LIMIT, ALU.max, ALU.min)\
                         .then_inc(S["d_guf"], 1)
                        dve.wait_ge(S["d_guf"], f + 2)
                        v.scalar_tensor_tensor(uu, uu, 1.0, gg, ALU.add, ALU.mult).then_inc(S["d_t"], 1)
                        dve.wait_ge(S["d_t"], f + 1)
                        dve.wait_ge(S["a_sig"], f + 1)
                        v.tensor_tensor(aa, uu, sg, ALU.mult).then_inc(S["d_act"], 1)
                        bias_select(1 - x, pair * 2 + (x + 1)).then_inc(S["d_bs"], 1)
                        adds(it, 2 * x)
                        v.tensor_tensor(Gw[:, :, x, :], G[x], comb[:, bass.ds(pair * 2 + x, 1), :]
                                        .rearrange("p o t -> p (o t)").unsqueeze(2).to_broadcast([P, 3, CAP]),
                                        ALU.mult).then_inc(S["d_gw"], 1)
                        dve.wait_ge(S["d_gw"], f + 1)
                        if x == 0:
                            adds(it, 1)
            def y_rows_out(t):
                R = ROWS[t]
                wait("rt3_ok", 5 + t)
                link(v.reciprocal(st[0:R, 8 + t:9 + t], st[0:R, 8 + t:9 + t]))
                v.scalar_tensor_tensor(XT[0:R, t, :], acc[0:R, t, :], st[0:R, 8 + t:9 + t], MB[0:R, 0, 1, :],
                                       ALU.mult, ALU.mult).then_inc(S["y_done"], 1)

            wait("ld_fn", 48)
            dve.wait_ge(S["d_add"], npass * (3 * NE // 2) + 1)
            for t in range(3):
                R = ROWS[t]
                link(v.tensor_tensor(acc[0:R, t, :], acc[0:R, t, :], MB[0:R, t // 2, 3, :], ALU.mult))
                link(v.tensor_tensor(acc[0:R, t, :], acc[0:R, t, :], XT[0:R, t, :], ALU.add))
            for t in range(3):
                R = ROWS[t]
                dve.wait_ge(S["sc_ps"], npass * (3 * NE // 2) + (t + 1))
                for nh in range(2):
                    i = v.tensor_tensor(h2[0:R, t, 512 * nh:512 * nh + 512], last_bank(t, nh)[0:R, :],
                                        MB[0:R, t // 2, 3, 512 * nh:512 * nh + 512], ALU.mult)
                link(i)
                link(v.tensor_tensor(acc[0:R, t, :], acc[0:R, t, :], h2[0:R, t, :], ALU.add))
                v.tensor_tensor_reduce(h2[0:R, t, :], acc[0:R, t, :], acc[0:R, t, :], 1.0, 0.0, ALU.mult, ALU.add,
                                       st[0:R, 8 + t:9 + t]).then_inc(S["ss_ok"], 1)
                if t >= 1:
                    y_rows_out(t - 1)
            y_rows_out(2)


_UNUSED = ("sc_w_in", "sc_conv_w", "sc_w_out")
_OUTS = [("y_prompt", (1, NP, D)), ("y_sample", (NS, 1, D)), ("new_ssm_prompt", (1, HEADS, HD, STATE)),
         ("new_ssm_conv_prompt", (1, CONV - 1, CDIM)), ("new_sconv_prompt", (1, 2, D)),
         ("new_ssm_sample", (NS, HEADS, HD, STATE)), ("new_ssm_conv_sample", (NS, CONV - 1, CDIM)),
         ("new_sconv_sample", (NS, 2, D))]


def kernel(**inputs):
    import numpy as _np
    import concourse.bacc as _bacc
    from concourse import mybir as _mybir
    from concourse.bass_utils import run_bass_kernel_spmd as _run

    nc = _bacc.Bacc("TRN2", target_bir_lowering=False, num_devices=1)
    arrays, io = {}, {}
    for name, x in inputs.items():
        if name in _UNUSED:
            continue
        x = _np.ascontiguousarray(x)
        arrays[f"in_{name}"] = x
        io[name] = nc.dram_tensor(f"in_{name}", x.shape, _mybir.dt.from_np(x.dtype), kind="ExternalInput").ap()
    for name, shape in _OUTS:
        io[name] = nc.dram_tensor(f"out_{name}", shape, _mybir.dt.float32, kind="ExternalOutput").ap()
    build(nc, io)
    r = _run(nc, [arrays], core_ids=[0])
    return tuple(r.results[0][f"out_{name}"] for name, _ in _OUTS)
```
